# Optimizing a Trainium2 kernel written in Bass

```python
import math
import jax
import jax.numpy as jnp
from jax import lax
import numpy as np
import jax, jax.numpy as jnp

D_MODEL = 1024
BATCH = 1
SEQ = 256
DEPTH = 2

EPS = 1e-6
GM_WIDTH = 512
GM_GROUPS = 4
GM_GROUP_DIM = GM_WIDTH // GM_GROUPS
GM_CHUNK = 128
SSM_INNER = 1024
SSM_HEAD_DIM = 64
SSM_HEADS = SSM_INNER // SSM_HEAD_DIM
SSM_GROUPS = 2
SSM_STATE = 128
SSM_CONV = 4
SSM_CONV_DIM = SSM_INNER + 2 * SSM_GROUPS * SSM_STATE
SSM_CHUNK = 128
DA_HEADS = 4
DA_HEAD_DIM = 64
DA_V_DIM = 2 * DA_HEAD_DIM
DA_QK_WIDTH = DA_HEADS * 2 * DA_HEAD_DIM
DA_WIDTH = DA_HEADS * DA_V_DIM
ROPE_DIM = DA_HEAD_DIM // 4
ROPE_THETA = 500000.0
Q_BLOCK = 128
N_BRANCH = 3
IN_SIZES = (GM_WIDTH, GM_WIDTH, SSM_INNER, SSM_CONV_DIM, SSM_HEADS, DA_QK_WIDTH, DA_QK_WIDTH, DA_WIDTH, N_BRANCH * D_MODEL)
IN_DIM = sum(IN_SIZES)
FFN_DIM = 2816
FFN_CONV = 3


def rmsnorm(x, g):
    xf = x.astype(jnp.float32)
    y = xf * lax.rsqrt(jnp.mean(xf * xf, axis=-1, keepdims=True) + EPS)
    return (y * g.astype(jnp.float32)).astype(x.dtype)

def causal_dwconv(x, w, b):
    k = w.shape[1]
    rhs = jnp.transpose(w)[:, None, :].astype(x.dtype)
    y = lax.conv_general_dilated(x, rhs, window_strides=(1,), padding=[(k - 1, 0)],
                                 dimension_numbers=('NWC', 'WIO', 'NWC'),
                                 feature_group_count=x.shape[-1])
    return y + b.astype(x.dtype)

def split_cols(t, sizes):
    idx = [int(i) for i in np.cumsum(sizes)[:-1]]
    return jnp.split(t, idx, axis=-1)

def chunked_spatial_gating(u, v, v_gain, w_s, b_s):
    bsz, s, _ = v.shape
    n = s // GM_CHUNK
    vn = rmsnorm(v, v_gain).reshape(bsz, n, GM_CHUNK, GM_GROUPS, GM_GROUP_DIM)
    causal = jnp.tril(jnp.ones((GM_CHUNK, GM_CHUNK), dtype=bool))
    w = jnp.where(causal[None], w_s, jnp.zeros_like(w_s))
    mixed = jnp.einsum('gts,bnsgc->bntgc', w, vn) + jnp.transpose(b_s)[None, None, :, :, None]
    return u * mixed.reshape(bsz, s, GM_WIDTH)

def ssd_scan(xs, dt, a_log, bm, cm, d_skip):
    bsz, s = xs.shape[:2]
    nc, q = s // SSM_CHUNK, SSM_CHUNK
    hpg = SSM_HEADS // SSM_GROUPS
    f32 = jnp.float32
    x = xs.astype(f32).reshape(bsz, nc, q, SSM_GROUPS, hpg, SSM_HEAD_DIM)
    dtc = dt.astype(f32).reshape(bsz, nc, q, SSM_GROUPS, hpg)
    bc = bm.astype(f32).reshape(bsz, nc, q, SSM_GROUPS, SSM_STATE)
    cc = cm.astype(f32).reshape(bsz, nc, q, SSM_GROUPS, SSM_STATE)
    a = -jnp.exp(a_log.astype(f32)).reshape(SSM_GROUPS, hpg)
    a_cum = jnp.cumsum(dtc * a, axis=2)
    xdt = x * dtc[..., None]
    causal = jnp.tril(jnp.ones((q, q), dtype=bool))[:, :, None, None]
    seg = a_cum[:, :, :, None] - a_cum[:, :, None, :]
    decay = jnp.exp(jnp.where(causal, seg, -jnp.inf))
    cb = jnp.einsum('bctgn,bcsgn->bctsg', cc, bc)
    y_diag = jnp.einsum('bctsgh,bcsghp->bctghp', cb[..., None] * decay, xdt)
    decay_end = jnp.exp(a_cum[:, :, -1:] - a_cum)
    states = jnp.einsum('bcsgn,bcsgh,bcsghp->bcghpn', bc, decay_end, xdt)
    chunk_decay = jnp.exp(a_cum[:, :, -1])

    def step(h, inp):
        st, dec = inp
        return h * dec[..., None, None] + st, h

    h0 = jnp.zeros((bsz, SSM_GROUPS, hpg, SSM_HEAD_DIM, SSM_STATE), f32)
    _, prev = lax.scan(step, h0, (jnp.moveaxis(states, 1, 0), jnp.moveaxis(chunk_decay, 1, 0)))
    prev = jnp.moveaxis(prev, 0, 1)
    y_off = jnp.einsum('bctgn,bcghpn,bctgh->bctghp', cc, prev, jnp.exp(a_cum))
    y = y_diag + y_off + d_skip.astype(f32).reshape(SSM_GROUPS, hpg)[..., None] * x
    return y.reshape(bsz, s, SSM_INNER).astype(xs.dtype)

def mamba2_mixer(z, xbc, dt_raw, conv_w, conv_b, dt_bias, a_log, d_skip, norm_g):
    bsz, s = z.shape[:2]
    xbc = jax.nn.silu(causal_dwconv(xbc, conv_w, conv_b))
    xs, bm, cm = split_cols(xbc, (SSM_INNER, SSM_GROUPS * SSM_STATE, SSM_GROUPS * SSM_STATE))
    dt = jax.nn.softplus(dt_raw.astype(jnp.float32) + dt_bias.astype(jnp.float32))
    y = ssd_scan(xs.reshape(bsz, s, SSM_HEADS, SSM_HEAD_DIM), dt, a_log,
                 bm.reshape(bsz, s, SSM_GROUPS, SSM_STATE),
                 cm.reshape(bsz, s, SSM_GROUPS, SSM_STATE), d_skip)
    return rmsnorm(y * jax.nn.silu(z), norm_g)

def rope_tables(s):
    pos = jnp.arange(s, dtype=jnp.float32)
    inv_freq = 1.0 / (ROPE_THETA ** (jnp.arange(0, ROPE_DIM, 2, dtype=jnp.float32) / ROPE_DIM))
    ang = pos[:, None] * inv_freq[None, :]
    return jnp.cos(ang), jnp.sin(ang)

def partial_rope(t, cos, sin):
    half = ROPE_DIM // 2
    c = cos[None, :, None, None, :]
    sn = sin[None, :, None, None, :]
    t1 = t[..., :half]
    t2 = t[..., half:ROPE_DIM]
    return jnp.concatenate([t1 * c - t2 * sn, t2 * c + t1 * sn, t[..., ROPE_DIM:]], axis=-1)

def diff_attention(q, k, v, q_g, k_g, lam_vecs, subln_g, lam_init, cos, sin):
    bsz, s = q.shape[:2]
    f32 = jnp.float32
    qh = rmsnorm(q.reshape(bsz, s, DA_HEADS, 2, DA_HEAD_DIM), q_g).astype(f32)
    kh = rmsnorm(k.reshape(bsz, s, DA_HEADS, 2, DA_HEAD_DIM), k_g).astype(f32)
    qh = partial_rope(qh, cos, sin) * (DA_HEAD_DIM ** -0.5)
    kh = partial_rope(kh, cos, sin)
    vf = v.reshape(bsz, s, DA_HEADS, DA_V_DIM).astype(f32)
    lv = lam_vecs.astype(f32)
    lam = jnp.exp(jnp.sum(lv[0] * lv[1])) - jnp.exp(jnp.sum(lv[2] * lv[3])) + lam_init
    nb = s // Q_BLOCK
    q_blocks = jnp.moveaxis(qh.reshape(bsz, nb, Q_BLOCK, DA_HEADS, 2, DA_HEAD_DIM), 1, 0)
    k_pos = jnp.arange(s)

    def block(args):
        qb, bi = args
        scores = jnp.einsum('bqhmd,bkhmd->bhmqk', qb, kh)
        q_pos = bi * Q_BLOCK + jnp.arange(Q_BLOCK)
        mask = k_pos[None, :] <= q_pos[:, None]
        p = jax.nn.softmax(jnp.where(mask, scores, -jnp.inf), axis=-1)
        w = p[:, :, 0] - lam * p[:, :, 1]
        return jnp.einsum('bhqk,bkhd->bqhd', w, vf)

    out = lax.map(block, (q_blocks, jnp.arange(nb)))
    out = jnp.moveaxis(out, 0, 1).reshape(bsz, s, DA_HEADS, DA_V_DIM)
    out = rmsnorm(out, subln_g) * (1.0 - lam_init)
    return out.reshape(bsz, s, DA_WIDTH).astype(v.dtype)

def first_inputs(seed: int = 0) -> dict:
    key = jax.random.key(seed)
    ks = jax.random.split(key, 32)
    f32 = jnp.float32
    L = DEPTH

    def nrm(k, shape, scale):
        return jax.random.normal(k, shape, f32) * scale

    def gain(k, shape):
        return 1.0 + 0.05 * jax.random.normal(k, shape, f32)

    dt_init = jnp.exp(jax.random.uniform(ks[9], (L, SSM_HEADS), f32, math.log(1e-3), math.log(1e-1)))
    return {
        'x': nrm(ks[0], (BATCH, SEQ, D_MODEL), 1.0),
        'attn_norm_g': gain(ks[1], (L, D_MODEL)),
        'w_in': nrm(ks[2], (L, D_MODEL, IN_DIM), D_MODEL ** -0.5),
        'gm_v_norm_g': gain(ks[3], (L, GM_WIDTH)),
        'gm_w_s': nrm(ks[4], (L, GM_GROUPS, GM_CHUNK, GM_CHUNK), GM_CHUNK ** -0.5),
        'gm_b_s': 1.0 + 0.1 * jax.random.normal(ks[5], (L, GM_GROUPS, GM_CHUNK), f32),
        'ssm_conv_w': nrm(ks[6], (L, SSM_CONV_DIM, SSM_CONV), SSM_CONV ** -0.5),
        'ssm_conv_b': nrm(ks[7], (L, SSM_CONV_DIM), 0.02),
        'ssm_dt_bias': dt_init + jnp.log(-jnp.expm1(-dt_init)),
        'ssm_a_log': jnp.log(jax.random.uniform(ks[10], (L, SSM_HEADS), f32, 1.0, 16.0)),
        'ssm_d': gain(ks[11], (L, SSM_HEADS)),
        'ssm_norm_g': gain(ks[12], (L, SSM_INNER)),
        'da_q_norm_g': gain(ks[13], (L, DA_HEAD_DIM)),
        'da_k_norm_g': gain(ks[14], (L, DA_HEAD_DIM)),
        'da_lambda': nrm(ks[15], (L, 4, DA_HEAD_DIM), 0.1),
        'da_subln_g': gain(ks[16], (L, DA_V_DIM)),
        'w_branch_a': nrm(ks[17], (L, GM_WIDTH, D_MODEL), GM_WIDTH ** -0.5),
        'w_branch_b': nrm(ks[18], (L, SSM_INNER, D_MODEL), SSM_INNER ** -0.5),
        'w_branch_c': nrm(ks[19], (L, DA_WIDTH, D_MODEL), DA_WIDTH ** -0.5),
        'w_out': nrm(ks[20], (L, D_MODEL, D_MODEL), D_MODEL ** -0.5),
        'ffn_norm_g': gain(ks[21], (L, D_MODEL)),
        'ffn_w_up': nrm(ks[22], (L, D_MODEL, 2 * FFN_DIM), D_MODEL ** -0.5),
        'ffn_conv_w': nrm(ks[23], (L, 2 * FFN_DIM, FFN_CONV), FFN_CONV ** -0.5),
        'ffn_conv_b': nrm(ks[24], (L, 2 * FFN_DIM), 0.02),
        'ffn_w_down': nrm(ks[25], (L, FFN_DIM, D_MODEL), FFN_DIM ** -0.5),
    }

def first_block(x, attn_norm_g, w_in, gm_v_norm_g, gm_w_s, gm_b_s, ssm_conv_w, ssm_conv_b,
              ssm_dt_bias, ssm_a_log, ssm_d, ssm_norm_g, da_q_norm_g, da_k_norm_g, da_lambda,
              da_subln_g, w_branch_a, w_branch_b, w_branch_c, w_out, ffn_norm_g, ffn_w_up,
              ffn_conv_w, ffn_conv_b, ffn_w_down):
    bsz, s, _ = x.shape
    cos, sin = rope_tables(s)
    for layer in range(DEPTH):
        lam_init = 0.8 - 0.6 * math.exp(-0.3 * layer)
        h = rmsnorm(x, attn_norm_g[layer])
        proj = h @ w_in[layer]
        gm_u, gm_v, ssm_z, ssm_xbc, ssm_dt, da_q, da_k, da_v, gates = split_cols(proj, IN_SIZES)
        y_a = chunked_spatial_gating(jax.nn.gelu(gm_u), jax.nn.gelu(gm_v), gm_v_norm_g[layer],
                                     gm_w_s[layer], gm_b_s[layer])
        y_b = mamba2_mixer(ssm_z, ssm_xbc, ssm_dt, ssm_conv_w[layer], ssm_conv_b[layer],
                           ssm_dt_bias[layer], ssm_a_log[layer], ssm_d[layer], ssm_norm_g[layer])
        y_c = diff_attention(da_q, da_k, da_v, da_q_norm_g[layer], da_k_norm_g[layer],
                             da_lambda[layer], da_subln_g[layer], lam_init, cos, sin)
        g = jax.nn.sigmoid(gates).reshape(bsz, s, N_BRANCH, D_MODEL)
        merged = (g[:, :, 0] * (y_a @ w_branch_a[layer])
                  + g[:, :, 1] * (y_b @ w_branch_b[layer])
                  + g[:, :, 2] * (y_c @ w_branch_c[layer]))
        x = x + merged @ w_out[layer]
        h = rmsnorm(x, ffn_norm_g[layer])
        up = causal_dwconv(h @ ffn_w_up[layer], ffn_conv_w[layer], ffn_conv_b[layer])
        gate, val = jnp.split(up, 2, axis=-1)
        x = x + (jax.nn.silu(gate) * val) @ ffn_w_down[layer]
    return x


POOL_WINDOWS = (2, 4, 8, 16)
POOL_GROUPS = len(POOL_WINDOWS)
POOL_GROUP_DIM = D_MODEL // POOL_GROUPS
POOL_WIDTH = POOL_GROUPS * POOL_GROUP_DIM
ATTN_GROUPS = ((128, 1), (512, 4), (2048, 16))
HEADS_PER_GROUP = 4
N_HEADS = HEADS_PER_GROUP * len(ATTN_GROUPS)
HEAD_DIM = D_MODEL // 8
ATTN_WIDTH = N_HEADS * HEAD_DIM
ATTN_OUT = HEADS_PER_GROUP * HEAD_DIM
Q_BLOCK_2 = 64
NEG_INF = -1e30
N_BUCKETS = 32
MAX_DISTANCE = 1024
D_FF = ((8 * D_MODEL // 3 + 255) // 256) * 256
CONV_WIDTH = 3
SPLITS = [int(s) for s in np.cumsum([POOL_WIDTH, ATTN_WIDTH, ATTN_WIDTH, ATTN_WIDTH, D_MODEL])]
IN_WIDTH = POOL_WIDTH + 3 * ATTN_WIDTH + 2 * D_MODEL


def _rmsnorm(x, g):
    xf = x.astype(jnp.float32)
    y = xf * lax.rsqrt(jnp.mean(xf * xf, axis=-1, keepdims=True) + EPS)
    return (y * g.astype(jnp.float32)).astype(x.dtype)

def _t5_buckets(rel):
    n = -rel
    half = N_BUCKETS // 2
    ret = (n < 0).astype(np.int32) * half
    n = np.abs(n)
    max_exact = half // 2
    large = max_exact + (np.log(np.maximum(n, 1) / max_exact)
                         / np.log(MAX_DISTANCE / max_exact) * (half - max_exact)).astype(np.int32)
    large = np.minimum(large, half - 1)
    return (ret + np.where(n < max_exact, n, large)).astype(np.int32)

def _centred_mean(u, window):
    S = u.shape[1]
    c = jnp.pad(jnp.cumsum(u.astype(jnp.float32), axis=1), ((0, 0), (1, 0), (0, 0)))
    i = np.arange(S)
    lo = np.clip(i - window // 2, 0, S)
    hi = np.clip(i - window // 2 + window, 0, S)
    count = (hi - lo).astype(np.float32)
    return ((c[:, hi] - c[:, lo]) / count[None, :, None]).astype(u.dtype)

def _dilated_group(q, k, v, bias, window, dilation):
    B, S, H, Dh = q.shape
    half = window // (2 * dilation)
    offs = dilation * np.arange(-half, half + 1)
    pad = half * dilation
    k_pad = jnp.pad(k, ((0, 0), (pad, pad), (0, 0), (0, 0)))
    v_pad = jnp.pad(v, ((0, 0), (pad, pad), (0, 0), (0, 0)))
    t = np.arange(Q_BLOCK_2)
    scale = HEAD_DIM ** -0.5

    def block(q0):
        pos = q0 + t[:, None] + offs[None, :]
        valid = (pos >= 0) & (pos < S)
        idx = pos + pad
        kb = jnp.take(k_pad, idx, axis=1)
        vb = jnp.take(v_pad, idx, axis=1)
        qb = lax.dynamic_slice_in_dim(q, q0, Q_BLOCK_2, axis=1)
        logits = jnp.einsum('bqhd,bqkhd->bhqk', qb, kb,
                            preferred_element_type=jnp.float32) * scale
        logits = logits + bias.astype(jnp.float32)[None, :, None, :]
        logits = jnp.where(valid[None, None], logits, NEG_INF)
        lse = jax.nn.logsumexp(logits, axis=-1)
        p = jnp.exp(logits - lse[..., None]).astype(vb.dtype)
        o = jnp.einsum('bhqk,bqkhd->bqhd', p, vb)
        return o, lse

    starts = jnp.arange(S // Q_BLOCK_2, dtype=jnp.int32) * Q_BLOCK_2
    o, lse = lax.map(block, starts)
    o = o.transpose(1, 0, 2, 3, 4).reshape(B, S, H, Dh)
    lse = lse.transpose(1, 0, 3, 2).reshape(B, S, H)
    return o, lse

def _token_mixer(xn, w_in, w_pool, pool_scale, w_a, w_b, w_o, rel_bias):
    B, S, _ = xn.shape
    u, q, k, v, g_pool, g_attn = jnp.split(xn @ w_in, SPLITS, axis=-1)

    ug = u.reshape(B, S, POOL_GROUPS, POOL_GROUP_DIM)
    pooled = jnp.stack([_centred_mean(ug[:, :, gi], w) for gi, w in enumerate(POOL_WINDOWS)], axis=2) - ug
    pool_out = jnp.einsum('bsgc,gcd->bsgd', pooled, w_pool).reshape(B, S, POOL_WIDTH) * pool_scale

    q = q.reshape(B, S, N_HEADS, HEAD_DIM)
    k = k.reshape(B, S, N_HEADS, HEAD_DIM)
    v = v.reshape(B, S, N_HEADS, HEAD_DIM)
    outs, lses = [], []
    for gi, (window, dilation) in enumerate(ATTN_GROUPS):
        hs = slice(gi * HEADS_PER_GROUP, (gi + 1) * HEADS_PER_GROUP)
        half = window // (2 * dilation)
        buckets = _t5_buckets(dilation * np.arange(-half, half + 1))
        bias = rel_bias[buckets][:, hs].T
        o_g, lse_g = _dilated_group(q[:, :, hs], k[:, :, hs], v[:, :, hs], bias, window, dilation)
        outs.append(o_g)
        lses.append(lse_g)
    wts = jax.nn.softmax(jnp.stack(lses, axis=0), axis=0)
    attn = jnp.einsum('gbsh,gbshd->bshd', wts, jnp.stack(outs, axis=0).astype(jnp.float32))
    attn_out = attn.astype(xn.dtype).reshape(B, S, ATTN_OUT)

    merged = jax.nn.sigmoid(g_pool) * (pool_out @ w_a) + jax.nn.sigmoid(g_attn) * (attn_out @ w_b)
    return merged @ w_o

def _conv_ffn(xn, w_up, conv_w, conv_b, w_down):
    a, gval = jnp.split(xn @ w_up, 2, axis=-1)
    a = lax.conv_general_dilated(a, conv_w[:, None, :], window_strides=(1,),
                                 padding=((CONV_WIDTH // 2, CONV_WIDTH // 2),),
                                 dimension_numbers=('NWC', 'WIO', 'NWC'),
                                 feature_group_count=D_FF) + conv_b
    return (jax.nn.gelu(a) * gval) @ w_down

def second_inputs(seed: int = 0) -> dict:
    key = jax.random.key(seed)
    ks = jax.random.split(key, 16)
    f32 = jnp.float32

    def nrm(k, shape, scale):
        return jax.random.normal(k, shape, f32) * scale

    return {
        "x": nrm(ks[0], (BATCH, SEQ, D_MODEL), 1.0),
        "w_in": nrm(ks[1], (DEPTH, D_MODEL, IN_WIDTH), D_MODEL ** -0.5),
        "w_pool": nrm(ks[2], (DEPTH, POOL_GROUPS, POOL_GROUP_DIM, POOL_GROUP_DIM), POOL_GROUP_DIM ** -0.5),
        "pool_scale": 1.0 + nrm(ks[3], (DEPTH, POOL_WIDTH), 0.02),
        "w_a": nrm(ks[4], (DEPTH, POOL_WIDTH, D_MODEL), POOL_WIDTH ** -0.5),
        "w_b": nrm(ks[5], (DEPTH, ATTN_OUT, D_MODEL), ATTN_OUT ** -0.5),
        "w_o": nrm(ks[6], (DEPTH, D_MODEL, D_MODEL), D_MODEL ** -0.5),
        "norm1": 1.0 + nrm(ks[7], (DEPTH, D_MODEL), 0.02),
        "norm2": 1.0 + nrm(ks[8], (DEPTH, D_MODEL), 0.02),
        "w_up": nrm(ks[9], (DEPTH, D_MODEL, 2 * D_FF), D_MODEL ** -0.5),
        "conv_w": nrm(ks[10], (DEPTH, CONV_WIDTH, D_FF), CONV_WIDTH ** -0.5),
        "conv_b": nrm(ks[11], (DEPTH, D_FF), 0.01),
        "w_down": nrm(ks[12], (DEPTH, D_FF, D_MODEL), D_FF ** -0.5),
        "rel_bias": nrm(ks[13], (N_BUCKETS, N_HEADS), 0.2),
        "norm_f": 1.0 + nrm(ks[14], (D_MODEL,), 0.02),
    }

def second_block(x, w_in, w_pool, pool_scale, w_a, w_b, w_o, norm1, norm2,
              w_up, conv_w, conv_b, w_down, rel_bias, norm_f):
    h = x
    for layer in range(DEPTH):
        h = h + _token_mixer(_rmsnorm(h, norm1[layer]), w_in[layer], w_pool[layer], pool_scale[layer],
                             w_a[layer], w_b[layer], w_o[layer], rel_bias)
        h = h + _conv_ffn(_rmsnorm(h, norm2[layer]), w_up[layer], conv_w[layer], conv_b[layer], w_down[layer])
    return _rmsnorm(h, norm_f)


def setup_inputs(seed=0):
    out = dict(first_inputs(seed))
    for name, value in second_inputs(seed + 1).items():
        if name != "x":
            out[name + "_2"] = value
    return out


def reference(
    x, attn_norm_g, w_in, gm_v_norm_g, gm_w_s, gm_b_s, ssm_conv_w, ssm_conv_b, ssm_dt_bias,
    ssm_a_log, ssm_d, ssm_norm_g, da_q_norm_g, da_k_norm_g, da_lambda, da_subln_g, w_branch_a,
    w_branch_b, w_branch_c, w_out, ffn_norm_g, ffn_w_up, ffn_conv_w, ffn_conv_b, ffn_w_down,
    w_in_2, w_pool_2, pool_scale_2, w_a_2, w_b_2, w_o_2, norm1_2, norm2_2, w_up_2, conv_w_2,
    conv_b_2, w_down_2, rel_bias_2, norm_f_2,
):
    x = first_block(
        x, attn_norm_g, w_in, gm_v_norm_g, gm_w_s, gm_b_s, ssm_conv_w, ssm_conv_b, ssm_dt_bias,
        ssm_a_log, ssm_d, ssm_norm_g, da_q_norm_g, da_k_norm_g, da_lambda, da_subln_g,
        w_branch_a, w_branch_b, w_branch_c, w_out, ffn_norm_g, ffn_w_up, ffn_conv_w, ffn_conv_b,
        ffn_w_down,
    )
    return second_block(
        x, w_in_2, w_pool_2, pool_scale_2, w_a_2, w_b_2, w_o_2, norm1_2, norm2_2, w_up_2,
        conv_w_2, conv_b_2, w_down_2, rel_bias_2, norm_f_2,
    )


_drawn_inputs = setup_inputs


def setup_inputs(seed=0):
    import zlib

    import numpy as np

    out = dict(_drawn_inputs(seed))
    spreads = {}
    factors = {'gm_v_norm_g': 3.605,
     'ssm_conv_b': 2.913,
     'da_lambda': 5.538,
     'ffn_conv_b': 2.818,
     'pool_scale_2': 7.562,
     'norm1_2': 6.856,
     'norm2_2': 12.982,
     'conv_b_2': 37.264,
     'rel_bias_2': 4.943,
     'norm_f_2': 8.127}
    for name, (base, spread) in spreads.items():
        noise = np.random.default_rng([zlib.crc32(name.encode()), seed]).standard_normal(out[name].shape)
        drawn = base * np.exp(spread * noise) if base else spread * noise
        out[name] = jnp.asarray(drawn.astype(out[name].dtype))
    for name, factor in factors.items():
        out[name] = (out[name] * factor).astype(out[name].dtype)
    return out
```

```python
def plan_block(names, first_bank=0):
    groups = []
    bank = first_bank
    for name, count, kt, cols, tile, form, taker in names:
        for n in range(count):
            per_bank = 4 if name == "DN" else 1
            sub = n % per_bank
            groups.append(dict(name=f"{name}{n}", kind=name, n=n, kt=kt, cols=cols, form=form, taker=taker,
                               tile=tile(n), bank=bank % 3, opens=sub == 0, closes=sub == per_bank - 1, sub=sub))
            if sub == per_bank - 1:
                bank += 1
    return groups


def build_program(nc, t_in, out):
    import concourse.bass as bass
    from concourse import mybir
    from contextlib import ExitStack

    f32, f32r = mybir.dt.float32, mybir.dt.float32r
    ACT = mybir.ActivationFunctionType
    ALU = mybir.AluOpType
    AX = mybir.AxisListType

    P = 128
    S = 256
    TT = S // P
    D = 1024
    KD = D // P
    LAYERS = 2
    EPS = 1e-6
    RAW, SPL = 2, 3
    SLOT = 2048
    BANKS = 3
    FF = 2816
    FP = FF // 256
    FT = FF // P
    DNK = FT // 2
    H1 = 4
    NEG = -1e30

    A_H, A_YA, A_YB, A_YC, A_MG, A_H2, A_G = 0, 8, 12, 20, 0, 22, 0
    A_PD, A_PO, A_AT = 8, 16, 24

    const = lambda v: (lambda n: v)
    G1 = plan_block([
        ("XBC", 6, 8, 256, const(A_H), "A", "dve"),
        ("QK", 4, 8, 256, const(A_H), "B", "act"),
        ("V", 2, 8, 256, const(A_H), "B", "act"),
        ("GV", 2, 8, 256, const(A_H), "B", "act"),
        ("GU", 2, 8, 256, const(A_H), "A", "act"),
        ("Z", 4, 8, 256, const(A_H), "A", "act"),
        ("GA", 4, 8, 256, const(A_H), "A", "act"),
        ("BA", 4, 4, 256, const(A_YA), "A", "dve"),
        ("GB", 4, 8, 256, const(A_H), "A", "act"),
        ("BB", 4, 8, 256, const(A_YB), "A", "dve"),
        ("GC", 4, 8, 256, const(A_H), "A", "act"),
        ("BC", 4, 4, 256, const(A_YC), "A", "dve"),
        ("OUT", 4, 8, 256, const(A_MG), "A", "dve"),
        ("UP", 2 * FP, 8, 256, const(A_H2), "A", "dve"),
        ("DN", 16, DNK, 128, lambda n: A_G + DNK * (n % 2), "A", "dve"),
    ])
    G2 = plan_block([
        ("PU", 4, 8, 256, const(A_H), "B", "act"),
        ("Q", 6, 8, 256, const(A_H), "A", "act"),
        ("K", 6, 8, 256, const(A_H), "A", "act"),
        ("V", 6, 8, 256, const(A_H), "B", "act"),
        ("GP", 4, 8, 256, const(A_H), "A", "act"),
        ("WP", 4, 2, 256, lambda n: A_PD + 2 * n, "A", "dve"),
        ("WA", 4, 8, 256, const(A_PO), "A", "dve"),
        ("GT", 4, 8, 256, const(A_H), "A", "act"),
        ("WB", 4, 4, 256, const(A_AT), "A", "dve"),
        ("OUT", 4, 8, 256, const(A_MG), "A", "dve"),
        ("UP", 2 * FP, 8, 256, const(A_H2), "A", "dve"),
        ("DN", 16, DNK, 128, lambda n: A_G + DNK * (n % 2), "A", "dve"),
    ])
    assert len({g["name"] for g in G1}) == len(G1)

    C = t_in
    COLS1 = dict(norm1=(0, 8), cw=(8, 48), cb=(56, 12), sg=(68, 8), sd=(76, 8), norm2=(84, 8), fw=(92, 132), fb=(224, 44))
    COLS2 = dict(norm1=(0, 8), ps=(8, 8), norm2=(16, 8), fw=(24, 66), fb=(90, 22))
    ROWS1 = dict(gvg=(0, 512), gb=(512, 512), qg=(1024, 64), kg=(1088, 64), sub=(1152, 128), dtb=(1280, 16),
                 alog=(1296, 16), li=(1312, 2))
    NC1, NC2, NR1 = 268, 112, 1314

    ctx = ExitStack()
    with ctx:
        def sb(name, shape, dt=f32):
            return ctx.enter_context(nc.sbuf_tensor(name, shape, dt))

        def sem(name):
            return ctx.enter_context(nc.semaphore(name))

        raw = sb("w_raw", [P, RAW, SLOT])
        whi = sb("w_hi", [P, SPL, SLOT], f32r)
        wlo = sb("w_lo", [P, SPL, SLOT], f32r)
        ahi = sb("act_hi", [P, 30, S], f32r)
        alo = sb("act_lo", [P, 30, S], f32r)
        x = sb("x", [P, KD, S])
        g01 = sb("gates_01", [P, 2 * KD, S])
        ug = sb("spatial_uv", [P, KD, S])
        xbc = sb("xbc", [P, 12, S])
        qkv = sb("qkv", [P, 12 * S])
        tmp = sb("tmp", [P, 16 * S])
        cols1 = sb("cols1", [P, NC1])
        cols2 = cols1[:, 0:NC2]
        rows1 = sb("rows1", [P, NR1])
        colsf = sb("colsf", [P, KD])
        ident, tri = sb("ident", [P, P]), sb("tri", [P, P])
        amask = sb("amask", [P, S])
        ones = sb("ones", [P, P])
        rope = sb("rope", [P, TT, 2, 8])
        rstd = sb("rstd", [P, S])
        sm = sb("small", [P, 400])
        eps = sm[:, 399:400]

        PS = ctx.enter_context(nc.psum_tensor("chain_ps", [P, 5, 512], f32))
        PJ = ctx.enter_context(nc.psum_tensor("proj_ps", [P, BANKS, 512], f32))
        pA, pB, pC = PS[:, 0:2, :], PS[:, 2:4, :], PS[:, 4, :]

        quarter = lambda q, n=1: tmp[:, q * 1024:(q + n) * 1024]
        sq8 = quarter(0, 2).rearrange("p (k t) -> p k t", t=S)
        h32 = quarter(2, 2).rearrange("p (k t) -> p k t", t=S)
        xdt = quarter(0)
        dec = quarter(1).rearrange("p (h t) -> p h t", t=P)
        cdec = quarter(2).rearrange("p (h t) -> p h t", t=P)
        prev = quarter(3).rearrange("p (g q) -> p g q", g=2)
        qkT = quarter(0, 2).rearrange("p (j t) -> p j t", t=S)
        prob = quarter(2, 2)
        qk = qkv[:, 0:2048].rearrange("p (a c) -> p a c", a=TT)
        vv = qkv[:, 2048:3072].rearrange("p (a c) -> p a c", a=TT)
        o32 = qkv[:, 0:1024].rearrange("p (a c) -> p a c", a=TT)
        wT = qkv[:, 1024:2048].rearrange("p (j t) -> p j t", t=P)
        vg = ug[:, 0:4, :].rearrange("p k t -> p (k t)").rearrange("p (a c) -> p a c", a=TT)
        uu = ug[:, 4:8, :]
        G0, SZ = g01[:, 0:8, :], g01[:, 8:16, :]

        at = [0]

        def small(n):
            at[0] += n
            return sm[:, at[0] - n:at[0]]
        dtx, dta, dte, dtu, dtl, dtv, dtA = [small(32) for _ in range(7)]
        aexp, acum = small(16), small(16)
        dend = small(8)
        gms, gmr = small(2), small(2)
        qs, qr = small(32), small(32)
        mx, nb, ps_, pr = small(8), small(8), small(8), small(8)
        os_, orr = small(8), small(8)
        lms, lmv = small(2), small(1)
        bmx, bnm, bsm, brr = [small(2) for _ in range(4)]
        early = g01[:, 0:8, :].rearrange("p k t -> p (k t)")
        cbm = early[:, 0:256].rearrange("p (g t) -> p g t", g=2)
        bT = early[:, 256:512].rearrange("p (g n) -> p g n", g=2)
        wsT = early[:, 512:1024].rearrange("p (g t) -> p g t", g=4)
        wsn = early[:, 1024:1536].rearrange("p (g s) -> p g s", g=4)
        lmp = early[:, 1536:1664]
        dtw = early[:, 1664:1792].rearrange("p (k h) -> p k h", k=KD)
        lam_row = early[:, 1792:2048]

        w_loaded = [sem(f"w_loaded{n}") for n in range(RAW)]
        w_hi, w_lo_dve, w_lo_pool, group_done = sem("w_hi"), sem("w_lo_dve"), sem("w_lo_pool"), sem("group_done")
        taken = dict(act=sem("taken_act"), dve=sem("taken_dve"))
        loads_cleared = sem("loads_cleared")
        const_in, x_in, setup, start = sem("const_in"), sem("x_in"), sem("setup"), sem("start")
        out_in = sem("out_stored")
        STEPS = {}

        def step(name):
            if name not in STEPS:
                STEPS[name] = sem(name)
            return STEPS[name]

        def layer(b, i):
            return i + LAYERS if b == 2 else i

        NG = {1: len(G1), 2: len(G2)}
        BASE = {1: 0, 2: LAYERS * len(G1)}
        NTAKE = {b: {e: sum(1 for g in G if g["taker"] == e and g["closes"]) for e in ("act", "dve")}
                 for b, G in ((1, G1), (2, G2))}
        NLOAD = {b: [len(range(s, NG[b], RAW)) for s in range(RAW)] for b in (1, 2)}

        def count(b, i, k):
            return i * NG[b] + (BASE[b] + k + 1)

        def plain_count(b, i, k):
            return i * NG[b] + (BASE[b] + k)

        def taken_count(b, e, i, g):
            G = G1 if b == 1 else G2
            k = sum(1 for q in G[:g] if q["taker"] == e and q["closes"])
            base = LAYERS * NTAKE[1][e] if b == 2 else 0
            return i * NTAKE[b][e] + (base + k + 1)

        block = ctx.enter_context(nc.Block())

        def group_view(t, slot, g):
            return t[:, slot, 0:g["kt"] * g["cols"]].rearrange("p (k n) -> p k n", k=g["kt"])

        def weight_source(b, i, g):
            kind, n, c = g["kind"], g["n"], g["cols"]
            lay = bass.ds(i, 1)

            def of(name, k0, k1, c0):
                return C[name][lay, k0:k1, c0:c0 + c].rearrange("a (k p) n -> p (a k) n", p=P)
            if kind == "UP":
                return of("ffn_w_up" if b == 1 else "w_up_2", 0, D, (n % 2) * FF + (n // 2) * 256)
            if kind == "DN":
                return of("ffn_w_down" if b == 1 else "w_down_2", (n % 2) * DNK * P, (n % 2 + 1) * DNK * P, (n // 2) * P)
            if b == 1:
                first = dict(GU=0, GV=512, Z=1024, XBC=2048, QK=3600, V=4624, GA=5136, GB=6160, GC=7184)
                if kind in first:
                    return of("w_in", 0, D, first[kind] + 256 * n)
                name = dict(BA="w_branch_a", BB="w_branch_b", BC="w_branch_c", OUT="w_out")[kind]
                return of(name, 0, g["kt"] * P, 256 * n)
            first = dict(PU=0, Q=1024, K=2560, V=4096, GP=5632, GT=6656)
            if kind in first:
                return of("w_in_2", 0, D, first[kind] + 256 * n)
            if kind == "WP":
                return C["w_pool_2"][lay, n, :, :].rearrange("a (k p) n -> p (a k) n", p=P)
            name = dict(WA="w_a_2", WB="w_b_2", OUT="w_o_2")[kind]
            return of(name, 0, g["kt"] * P, 256 * n)

        def bias_loads(sp, i, u):
            sp.wait_ge(step("b2_bias_free"), i * 8 + (u + 1))
            sp.sem_inc(loads_cleared, 1)
            j, qt = u // 2, u % 2
            for g in range(3):
                row = C["bias_table"][4 * g + j, 255 - qt * P:255 - qt * P + P * 510]
                sp.dma_start(b2_bias[:, g, :], row.rearrange("(q f) -> q f", f=510)[:, 0:S]).then_inc(step("b2_bias_in"), 16)

        b2_bias = tmp[:, 0:768].rearrange("p (g k) -> p g k", g=3)
        b2_P = tmp[:, 768:1536]
        b2_PT = tmp[:, 1536:3072].rearrange("p (k q) -> p k q", q=S)

        POOL_K = {8: 4, 4: 2, 2: 1, DNK: 6}

        def low_part(eng, b, i, n, G, on_pool):
            if n >= len(G):
                return
            g = G[n]
            cut = g["kt"] - POOL_K[g["kt"]]
            ks = slice(cut, g["kt"]) if on_pool else slice(0, cut)
            eng.wait_ge(w_hi, plain_count(b, i, n + 1))
            eng.tensor_tensor(group_view(wlo, n % SPL, g)[:, ks, :], group_view(raw, n % RAW, g)[:, ks, :],
                              group_view(whi, n % SPL, g)[:, ks, :].bitcast(f32), ALU.subtract
                              ).then_inc(w_lo_pool if on_pool else w_lo_dve, 1)

        def high_part(act, b, i, n, G):
            if n >= len(G):
                return
            g = G[n]
            slot = n % RAW
            before = LAYERS * NLOAD[1][slot] if b == 2 else 0
            act.wait_ge(w_loaded[slot], i * (16 * NLOAD[b][slot]) + 16 * (before + n // RAW + 1))
            act.wait_ge(group_done, count(b, i, max(n - SPL + 1, 0)))
            act.activation(group_view(whi, n % SPL, g), group_view(raw, n % RAW, g), ACT.Copy).then_inc(w_hi, 1)

        def col(b, key, k):
            t, o = (cols1, COLS1) if b == 1 else (cols2, COLS2)
            return t[:, o[key][0] + k:o[key][0] + k + 1]

        def row(key):
            return rows1[:, ROWS1[key][0]:ROWS1[key][0] + ROWS1[key][1]]

        def bc(ap, dims, axis):
            return ap.unsqueeze(axis).to_broadcast(dims)

        def band(s):
            return xbc[:, 4 * s:4 * s + 4, :].rearrange("p k t -> p (k t)")

        def ypair(buf, val):
            q = 2 * buf + val
            return tmp[:, q * 512:(q + 1) * 512].rearrange("p (k t) -> p k t", t=S)

        BIAS_AT = {}
        SC_AT, TR_AT, PV_AT = {}, {}, {}
        hooks2 = (["V2", "V3", "V4", "V5"] + [f"GP{n}" for n in range(4)] + ["WP1", "WP3"]
                  + [f"WA{n}" for n in range(4)] + [f"GT{n}" for n in range(4)])
        for u in range(8):
            SC_AT[hooks2[2 * u]] = u
            TR_AT[hooks2[2 * u + 1]] = u
            at2 = [g["name"] for g in G2]
            BIAS_AT["K0" if u == 0 else at2[at2.index(hooks2[2 * u - 2]) + SPL]] = u
            if u % 2:
                PV_AT[hooks2[2 * u + 2]] = u // 2

        @block.sync
        def _(sp):
            for dst, name in ((ident, "c_ident"), (tri, "c_tri"), (amask, "c_amask")):
                sp.dma_start(dst[:, :], C[name]).then_inc(const_in, 16)
            sp.dma_start(rope[:, :, :, :].rearrange("p a b c -> p (a b c)"), C["c_rope"]).then_inc(const_in, 16)
            sp.dma_start(colsf[:, :], C["cols_f"]).then_inc(const_in, 16)
            for tt in range(TT):
                sp.dma_start(g01[:, 4 * tt:4 * tt + 4, :].rearrange("p k t -> p (k t)"), C["x"][0, tt * P:(tt + 1) * P, :]).then_inc(x_in, 16)
            sp.dma_start(qkv[0:32, 0:12], C["rel_bias_2"]).then_inc(step("bias_const_in"), 16)
            sp.dma_start(qkv[0:32, 512:1024], C["c_onehot"]).then_inc(step("bias_const_in"), 16)
            sp.dma_start(qkv[0:12, 1024:1536], C["c_offmask"]).then_inc(step("bias_const_in"), 16)
            sp.wait_ge(step("bias_row"), 1)
            sp.dma_start(C["bias_table"].rearrange("h (c o) -> h c o", o=511),
                         qkv[0:12, 1536:2047].unsqueeze(1).to_broadcast([12, 129, 511])).then_inc(step("bias_stored"), 16)
            for b, G in ((1, G1), (2, G2)):
                with sp.Fori(0, LAYERS) as i:
                    sp.wait_ge(step("layer_done"), layer(b, i) + 1)
                    sp.sem_inc(loads_cleared, 1)
                    lay = bass.ds(i, 1)
                    if b == 1:
                        sp.dma_start(cols1[:, :], C["cols_1"][lay, :, :].rearrange("a p c -> p (a c)")).then_inc(step("par_in1"), 16)
                        sp.dma_start(rows1[:, :], C["rows_1"][lay, :].to_broadcast([P, NR1])).then_inc(step("par_in1"), 16)
                        sp.dma_start(lam_row, C["lam_1"][lay, :].to_broadcast([P, 256])).then_inc(step("par_in1"), 16)
                        sp.dma_start(dtw[:, :, :], C["w_in"][lay, :, 3584:3600].rearrange("a (k p) n -> p (a k) n", p=P)).then_inc(step("par_in1"), 16)
                        sp.dma_start(wsn[:, :, :], C["gm_w_s"][lay, :, :, :].rearrange("a g t s -> t (a g) s")).then_inc(step("par_in1"), 16)
                    else:
                        sp.dma_start(cols2[:, :], C["cols_2"][lay, :, :].rearrange("a p c -> p (a c)")).then_inc(step("par_in2"), 16)
                        for s in range(TT):
                            sp.dma_start(band(s), C["c_band"][s, :, :]).then_inc(step("par_in2"), 16)
                    for n, g in enumerate(G):
                        slot = n % RAW
                        done = max(n - RAW + 1, 0)
                        sp.wait_ge(w_lo_dve, count(b, i, done))
                        sp.wait_ge(w_lo_pool, count(b, i, done))
                        sp.sem_inc(loads_cleared, 1)
                        sp.dma_start(group_view(raw, slot, g), weight_source(b, i, g)).then_inc(w_loaded[slot], 16)
                        if b == 2 and g["name"] in BIAS_AT:
                            bias_loads(sp, i, BIAS_AT[g["name"]])
            for tt in range(TT):
                sp.wait_ge(step("out_ready"), tt + 1)
                sp.dma_start(out[0, tt * P:(tt + 1) * P, :], g01[:, 4 * tt:4 * tt + 4, :].rearrange("p k t -> p (k t)")).then_inc(out_in, 16)
            sp.wait_ge(out_in, 16 * TT)
            sp.wait_ge(step("bias_stored"), 16)

        @block.gpsimd
        def _(pool):
            nc.gpsimd.memset(ones[:, :], 1.0 / D).then_inc(setup, 1)
            nc.gpsimd.memset(eps, EPS).then_inc(setup, 1)
            pool.sem_inc(w_lo_pool, 1)
            for b, G in ((1, G1), (2, G2)):
                with pool.Fori(0, LAYERS) as i:
                    for n in range(len(G)):
                        low_part(nc.gpsimd, b, i, n, G, True)

        @block.tensor
        def _(pe):
            mm = nc.tensor.matmul

            def proj(b, i, n, G):
                g = G[n]
                pe.wait_ge(w_lo_dve, count(b, i, n + 1))
                pe.wait_ge(w_lo_pool, count(b, i, n + 1))
                if g["opens"]:
                    old = max((q for q in range(n) if G[q]["closes"] and G[q]["bank"] == g["bank"]), default=None)
                    e = "dve" if old is None else G[old]["taker"]
                    pe.wait_ge(taken[e], taken_count(b, e, i, 0 if old is None else old + 1))
                hi, lo = group_view(whi, n % SPL, g), group_view(wlo, n % SPL, g)
                a0, kt = g["tile"], g["kt"]
                last = None
                if g["form"] == "A":
                    for t in range(g["cols"] // P):
                        half = t if g["cols"] == 256 else g["sub"] // 2
                        o = PJ[:, g["bank"], half * S:(half + 1) * S]
                        head = g["kind"] != "DN" or g["sub"] % 2 == 0
                        tail = g["kind"] != "DN" or g["sub"] % 2 == 1
                        for k in range(kt):
                            wh, wl = hi[:, k, t * P:(t + 1) * P], lo[:, k, t * P:(t + 1) * P]
                            mm(o, wh, ahi[:, a0 + k, :], start=head and k == 0, stop=False)
                            mm(o, wh, alo[:, a0 + k, :], start=False, stop=False)
                            last = mm(o, wl, ahi[:, a0 + k, :], start=False, stop=tail and k == kt - 1)
                else:
                    for t in range(TT):
                        o = PJ[:, g["bank"], t * 256:(t + 1) * 256]
                        for k in range(kt):
                            xh, xl = ahi[:, a0 + k, t * P:(t + 1) * P], alo[:, a0 + k, t * P:(t + 1) * P]
                            mm(o, xh, hi[:, k, :], start=k == 0, stop=False)
                            mm(o, xh, lo[:, k, :], start=False, stop=False)
                            last = mm(o, xl, hi[:, k, :], start=False, stop=k == kt - 1)
                last.then_inc(group_done, 1)

            def mean_square(b, i, sq, ready, done):
                pe.wait_ge(step(ready), layer(b, i) + 1)
                for k in range(KD):
                    last = mm(pC[:, 0:S], ones[:, :], sq[:, k, :], start=k == 0, stop=k == KD - 1)
                last.then_inc(step(done), 1)

            def dt_proj(i):
                for c in range(TT):
                    for k in range(KD):
                        last = mm(pC[:, 256 + 16 * c:272 + 16 * c], h32[:, k, c * P:(c + 1) * P], dtw[:, k, :],
                                  start=k == 0, stop=k == KD - 1)
                last.then_inc(step("dt_proj"), 1)

            def scan_open(i, c):
                pe.wait_ge(step("dta_ready"), i + 1)
                pe.wait_ge(step("xbc_ready"), i * 6 + 6)
                if c:
                    pe.wait_ge(step("y_taken"), i * 4 + 2)
                    pe.wait_ge(step("prev_ready"), i * 2 + 2)
                t = slice(c * P, (c + 1) * P)
                mm(pC[:, 0:16], tri[:, :], dtA[:, 16 * c:16 * c + 16], start=True, stop=True)
                for g in range(2):
                    mm(pC[:, 128 + 128 * g:256 + 128 * g], xbc[:, 8 + g, t], xbc[:, 10 + g, t], start=True, stop=True)
                    if c == 0:
                        nc.tensor.transpose(pB[:, 0, g * P:(g + 1) * P], xbc[:, 8 + g, t], ident[:, :])
                for k in range(8):
                    last = nc.tensor.transpose(pA[:, k // 4, (k % 4) * P:(k % 4 + 1) * P], xbc[:, k, t], ident[:, :])
                last.then_inc(step("scan_opened"), 1)

            def scan_rows(i, c, g):
                if (c, g) == (0, 0):
                    pe.wait_ge(step("chunk_ready"), i * 2 + 1)
                else:
                    pe.wait_ge(step("rows_taken"), i * 4 + 2 * c + g)
                for h in range(8):
                    last = mm(pB[:, h // 4, (h % 4) * P:(h % 4 + 1) * P],
                              dtA[:, 16 * c + 8 * g + h:16 * c + 8 * g + h + 1].to_broadcast([P, P]), tri[:, :], start=True, stop=True)
                last.then_inc(step("rows_ready"), 1)

            def scan_state(i, g):
                pe.wait_ge(step("xdtd_ready"), i * 2 + g + 1)
                pe.wait_ge(step("chunk_ready"), i * 2 + 1)
                if g:
                    pe.wait_ge(step("prev_ready"), i * 2 + 1)
                mm(pC[:, :], bT[:, g, :], cdec[:, 0:4, :].rearrange("p h t -> p (h t)"), start=True, stop=True).then_inc(step("state_ready"), 1)

            def scan_out(i, c, g):
                pe.wait_ge(step("dec_ready"), i * 4 + 2 * c + g + 1)
                if c:
                    pe.wait_ge(step("cdec_ready"), i * 2 + g + 1)
                for h in range(8):
                    r = slice((h % 2) * 64, (h % 2) * 64 + 64)
                    o = pA[r, g, (h // 2) * P:(h // 2 + 1) * P]
                    last = mm(o, xdt[:, (8 * g + h) * 64:(8 * g + h + 1) * 64], dec[:, h, :], start=True, stop=c == 0)
                    if c:
                        last = mm(o, prev[:, g, h * 64:(h + 1) * 64], cdec[:, h, :], start=False, stop=True)
                last.then_inc(step("y_ready"), 1)

            def gate_turn(i):
                pe.wait_ge(step("chunk_ready"), i * 2 + 2)
                for g in range(4):
                    last = nc.tensor.transpose(pC[:, g * P:(g + 1) * P], wsn[:, g, :], ident[:, :])
                last.then_inc(step("ws_turned"), 1)

            def gate_mix(i):
                pe.wait_ge(step("wsT_ready"), i + 1)
                pe.wait_ge(step("vn_ready"), i + 1)
                pe.wait_ge(step("y_taken"), i * 4 + 4)
                for n in range(TT):
                    for g in range(4):
                        last = mm(pA[:, n, g * P:(g + 1) * P], vg[:, n, g * P:(g + 1) * P], wsT[:, g, :], start=True, stop=True)
                last.then_inc(step("mixed"), 1)

            def attn_turn(i):
                pe.wait_ge(step("qk_normed"), i + 1)
                pe.wait_ge(step("ya_ready"), i + 1)
                for j in range(8):
                    for tt in range(TT):
                        o = PS[:, j // 2, (j % 2) * S + tt * P:(j % 2) * S + (tt + 1) * P]
                        last = nc.tensor.transpose(o, qk[:, tt, j * P:(j + 1) * P], ident[:, :])
                last.then_inc(step("qk_turned"), 1)

            def attn_scores(i, qt):
                W = (qt + 1) * P
                pe.wait_ge(step("qkT_ready"), i + 1)
                if qt:
                    pe.wait_ge(step("o_taken"), i * 2 + 1)
                for h in range(H1):
                    for m in range(2):
                        r = slice(m * 64, m * 64 + 64)
                        j = 4 * m + h
                        o = PS[:, j * W // 512, j * W % 512:j * W % 512 + W]
                        last = mm(o, qkT[r, h, qt * P:(qt + 1) * P], qkT[r, 4 + h, 0:W], start=True, stop=True)
                last.then_inc(step("scores"), 1)

            def attn_wturn(i, qt):
                pe.wait_ge(step("w_ready"), i * 2 + qt + 1)
                W = (qt + 1) * P
                pw = prob[:, 0:8 * W].rearrange("p (m h k) -> p m h k", h=H1, m=2)
                for h in range(H1):
                    for kt in range(qt + 1):
                        j = h * (qt + 1) + kt
                        last = nc.tensor.transpose(pB[:, j // 4, (j % 4) * P:(j % 4 + 1) * P], pw[:, 0, h, kt * P:(kt + 1) * P], ident[:, :])
                last.then_inc(step("w_turned"), 1)

            def attn_out(i, qt):
                pe.wait_ge(step("wT_ready"), i * 2 + qt + 1)
                for h in range(H1):
                    for kt in range(qt + 1):
                        last = mm(pA[:, 0, h * P:(h + 1) * P], wT[:, h * (qt + 1) + kt, :], vv[:, kt, h * P:(h + 1) * P],
                                  start=kt == 0, stop=kt == qt)
                last.then_inc(step("o_ready"), 1)

            def attn_oturn(i):
                pe.wait_ge(step("o_normed"), i + 1)
                for h in range(H1):
                    for tt in range(TT):
                        last = nc.tensor.transpose(pA[:, h // 2, (h % 2) * S + tt * P:(h % 2) * S + (tt + 1) * P],
                                                   o32[:, tt, h * P:(h + 1) * P], ident[:, :])
                last.then_inc(step("o_turned"), 1)

            pe.sem_inc(group_done, 1)
            pe.wait_ge(const_in, 80)
            pe.wait_ge(setup, 2)
            pe.wait_ge(x_in, 32)
            for k in range(KD):
                for tt in range(TT):
                    last = nc.tensor.transpose(PS[:, k // 2, (k % 2) * S + tt * P:(k % 2) * S + (tt + 1) * P],
                                               g01[:, 4 * tt:4 * tt + 4, :].rearrange("p k t -> p (k t)")[:, k * P:(k + 1) * P], ident[:, :])
            last.then_inc(step("x_turned"), 1)
            pe.wait_ge(step("bias_const_in"), 48)
            mm(pC[0:12, :], qkv[0:32, 0:12], qkv[0:32, 512:1024], start=True, stop=True).then_inc(step("bias_product"), 1)
            pe.wait_ge(step("bias_row"), 1)

            with pe.Fori(0, LAYERS) as i:
                mean_square(1, i, sq8, "n1_sq", "n1_ms")
                pe.wait_ge(step("h32_ready"), i * 2 + 2)
                pe.wait_ge(step("par_in1"), i * 80 + 80)
                dt_proj(i)
                after = dict(
                    QK0=lambda: scan_open(i, 0), QK1=lambda: scan_rows(i, 0, 0), QK2=lambda: scan_state(i, 0),
                    QK3=lambda: (scan_out(i, 0, 0), scan_rows(i, 0, 1)), V0=lambda: scan_state(i, 1),
                    V1=lambda: scan_out(i, 0, 1), GV0=lambda: scan_open(i, 1), GV1=lambda: scan_rows(i, 1, 0),
                    GU0=lambda: (gate_turn(i), scan_out(i, 1, 0)), GU1=lambda: scan_rows(i, 1, 1), Z0=lambda: scan_out(i, 1, 1),
                    Z2=lambda: gate_mix(i), GA0=lambda: mean_square(1, i, sq8, "yb_sq", "yb_ms"),
                    GA3=lambda: attn_turn(i), BA1=lambda: attn_scores(i, 0), GB0=lambda: attn_wturn(i, 0),
                    GB1=lambda: (attn_out(i, 0), attn_scores(i, 1)), BB0=lambda: attn_wturn(i, 1),
                    BB1=lambda: attn_out(i, 1), GC0=lambda: attn_oturn(i))
                before = dict(XBC0="h_ready", BA0="ya_ready", BB0="yb_ready", BC0="yc_ready", OUT0="mg_ready", DN0="gated_ready")
                for n, g in enumerate(G1):
                    if g["name"] == "UP0":
                        mean_square(1, i, sq8, "n2_sq", "n2_ms")
                        pe.wait_ge(step("h2_ready"), i + 1)
                    if g["name"] in before:
                        pe.wait_ge(step(before[g["name"]]), i + 1)
                    proj(1, i, n, G1)
                    if g["name"] in after:
                        after[g["name"]]()

            def pool_mix(i):
                pe.wait_ge(step("pu_ready"), i + 1)
                pe.wait_ge(step("par_in2"), i * 48 + 48)
                for k in range(KD):
                    for s in range(TT):
                        last = mm(PS[:, k // 2, (k % 2) * S:(k % 2 + 1) * S], uview[:, s, k * P:(k + 1) * P],
                                  band(s)[:, (k // 2) * S:(k // 2 + 1) * S], start=s == 0, stop=s == TT - 1)
                last.then_inc(step("pooled"), 1)

            uview = ug[:, :, :].rearrange("p k t -> p (k t)").rearrange("p (a c) -> p a c", a=TT)

            def b2_scores(i, u):
                j, qt = u // 2, u % 2
                if u == 0:
                    pe.wait_ge(step("qk2_ready"), i + 1)
                    pe.wait_ge(step("pd_ready"), i + 1)
                else:
                    pe.wait_ge(step("b2_PT_ready"), i * 8 + u)
                px = PS[:, 2 * (u % 2):2 * (u % 2) + 2, :]
                for g in range(3):
                    last = mm(px[:, g // 2, (g % 2) * S:(g % 2 + 1) * S], xbc[:, 4 * g + j, qt * P:(qt + 1) * P],
                              g01[:, 4 * g + j, :], start=True, stop=True)
                last.then_inc(step("b2_scores"), 1)

            def b2_turn(i, u):
                pe.wait_ge(step("b2_P_ready"), i * 8 + u + 1)
                px = PS[:, 2 * (u % 2):2 * (u % 2) + 2, :]
                for k in range(6):
                    last = nc.tensor.transpose(px[:, k // 4, (k % 4) * P:(k % 4 + 1) * P], b2_P[:, k * P:(k + 1) * P], ident[:, :])
                last.then_inc(step("b2_turned"), 1)

            def b2_values(i, j):
                pe.wait_ge(step("b2_PT_ready"), i * 8 + 2 * j + 2)
                if j:
                    pe.wait_ge(step("at_lo"), i * 4 + j)
                else:
                    pe.wait_ge(step("v2_ready"), i + 1)
                v2 = qkv[:, :].rearrange("p (a c) -> p a c", a=TT)
                for g in range(3):
                    for kt in range(TT):
                        last = mm(pC[:, 0:S], v2[:, kt, (4 * g + j) * P:(4 * g + j + 1) * P], b2_PT[:, 2 * g + kt, :],
                                  start=(g, kt) == (0, 0), stop=(g, kt) == (2, 1))
                last.then_inc(step("b2_out"), 1)

            with pe.Fori(0, LAYERS) as i:
                mean_square(2, i, sq8, "n1_sq", "n1_ms")
                before = dict(WP0="pd_ready", WA0="po_ready", WB0="at_ready")
                split_before = dict(PU0="h_ready", OUT0="mg_ready", DN0="gated_ready")
                for n, g in enumerate(G2):
                    if g["name"] == "UP0":
                        mean_square(2, i, sq8, "n2_sq", "n2_ms")
                        pe.wait_ge(step("h2_ready"), layer(2, i) + 1)
                    if g["name"] in before:
                        pe.wait_ge(step(before[g["name"]]), i + 1)
                    if g["name"] in split_before:
                        pe.wait_ge(step(split_before[g["name"]]), layer(2, i) + 1)
                    proj(2, i, n, G2)
                    if g["name"] == "Q0":
                        pool_mix(i)
                    if g["name"] in PV_AT:
                        b2_values(i, PV_AT[g["name"]])
                    if g["name"] in SC_AT:
                        b2_scores(i, SC_AT[g["name"]])
                    if g["name"] in TR_AT:
                        b2_turn(i, TR_AT[g["name"]])

            mean_square(2, LAYERS, sq8, "n1_sq", "n1_ms")
            pe.wait_ge(step("f_normed"), 1)
            for tt in range(TT):
                if tt:
                    pe.wait_ge(step("out_ready"), tt)
                for k in range(KD):
                    last = nc.tensor.transpose(pA[:, k // 4, (k % 4) * P:(k % 4 + 1) * P], h32[:, k, tt * P:(tt + 1) * P], ident[:, :])
                last.then_inc(step("out_turned"), 1)

        @block.scalar
        def _(act):
            A = nc.scalar.activation

            def squares(b, i, ready, done, src):
                act.wait_ge(step(ready), layer(b, i) + 1)
                A(sq8, src, ACT.Square).then_inc(step(done), 1)

            def root(b, i, ms, done):
                act.wait_ge(step(ms), layer(b, i) + 1)
                A(rstd[:, :], pC[:, 0:S], ACT.Sqrt, bias=eps).then_inc(step(done), 1)

            def small_root(i, sums, tile, n, done):
                act.wait_ge(step(sums), i + 1)
                A(tile, tile, ACT.Sqrt, scale=1.0 / n, bias=eps).then_inc(step(done), 1)

            def split_high(i, ready, value, tiles, src, done):
                act.wait_ge(step(ready), value)
                A(ahi[:, tiles, :], src, ACT.Copy).then_inc(step(done), 1)

            def norm_high(b, i, ready, a0, done):
                for q in range(2):
                    split_high(i, ready, layer(b, i) * 2 + q + 1, slice(a0 + 4 * q, a0 + 4 * q + 4), h32[:, 4 * q:4 * q + 4, :], done)

            def bank(g):
                return PJ[:, g["bank"], :]

            def arrived(b, i, n):
                act.wait_ge(group_done, count(b, i, n + 1))

            def conv_open(b, i, g, wkey, bkey, taps, tap, tiles, dst, done):
                for t in range(2):
                    last = A(dst[t], bank(g)[:, t * S:(t + 1) * S], ACT.Identity, bias=col(b, bkey, tiles[t]),
                             scale=col(b, wkey, tiles[t] * taps + tap))
                last.then_inc(step(done), 1)

            act.sem_inc(taken["act"], 1)
            with act.Fori(0, LAYERS) as i:
                squares(1, i, "x_ready", "n1_sq", x[:, :, :])
                high_part(act, 1, i, 0, G1)
                high_part(act, 1, i, 1, G1)
                root(1, i, "n1_ms", "n1_root")
                norm_high(1, i, "h32_ready", A_H, "h_hi")
                high_part(act, 1, i, 2, G1)

                def dt_exp():
                    act.wait_ge(step("dt_abs"), i + 1)
                    A(dte, dta, ACT.Exp, scale=-1.0).then_inc(step("dt_exp"), 1)
                    A(aexp, row("alog"), ACT.Exp).then_inc(step("a_exp"), 1)

                def dt_ln():
                    act.wait_ge(step("dt_one"), i + 1)
                    A(dtl, dtu, ACT.Ln).then_inc(step("dt_ln"), 1)

                def xbc_silu(n):
                    act.wait_ge(step("xbc_conv"), i * 6 + n + 1)
                    v = xbc[:, 2 * n:2 * n + 2, :]
                    A(v, v, ACT.Silu).then_inc(step("xbc_ready"), 1)

                def rows_exp(c, g):
                    act.wait_ge(step("seg_ready"), i * 4 + 2 * c + g + 1)
                    A(dec, dec, ACT.Exp).then_inc(step("dec_exp"), 1)
                    if c == 0:
                        A(dend, dend, ACT.Exp).then_inc(step("dend_exp"), 1)
                    else:
                        if g:
                            act.wait_ge(step("y_ready"), i * 4 + 3)
                        else:
                            act.wait_ge(step("state_ready"), i * 2 + 2)
                        A(cdec, pB.rearrange("p a (h t) -> p (a h) t", t=P), ACT.Exp).then_inc(step("cdec_exp"), 1)

                def gm_square():
                    act.wait_ge(step("vg_ready"), i + 1)
                    for tt in range(TT):
                        A(wsT[:, :, :].rearrange("p g t -> p (g t)"), vg[:, tt, :], ACT.Square, accum_out=gms[:, tt:tt + 1])
                        if tt == 0:
                            act.drain()
                    act.drain()
                    A(gms, gms, ACT.Sqrt, scale=1.0 / 512, bias=eps).then_inc(step("gm_root"), 1)

                def lam_exp():
                    act.wait_ge(step("lam_sums"), i + 1)
                    A(lms, lms, ACT.Exp).then_inc(step("lam_exp"), 1)

                def yb_square():
                    squares(1, i, "yz_ready", "yb_sq", xbc[:, 0:8, :])

                def qk_square():
                    act.wait_ge(step("yb_ms"), i + 1)
                    act.wait_ge(step("qk_in"), i + 1)
                    A(prob, qkv[:, 0:2048], ACT.Square).then_inc(step("qk_sq"), 1)

                def qk_copy():
                    act.wait_ge(step("qk_turned"), i + 1)
                    A(qkT, PS[:, 0:4, :].rearrange("p a (j t) -> p (a j) t", t=S), ACT.Copy).then_inc(step("qkT_ready"), 1)

                def attn_exp(qt):
                    W = (qt + 1) * P
                    act.wait_ge(step("max_ready"), i * 2 + qt + 1)
                    for j in range(8):
                        v = prob[:, j * W:(j + 1) * W]
                        last = A(v, v, ACT.Exp, bias=nb[:, j:j + 1], scale=0.125, accum_out=ps_[:, j:j + 1])
                    last.then_inc(step("attn_exp"), 1)

                def o_square():
                    act.wait_ge(step("o_taken"), i * 2 + 2)
                    A(prob[:, 0:1024], qkv[:, 0:1024], ACT.Square).then_inc(step("o_sq"), 1)

                def yc_high():
                    act.wait_ge(step("o_turned"), i + 1)
                    A(ahi[:, A_YC:A_YC + 4, :], pA.rearrange("p a (j t) -> p (a j) t", t=S), ACT.Copy).then_inc(step("yc_hi"), 1)

                after = dict(
                    XBC0=dt_exp, XBC1=lambda: (xbc_silu(0), dt_ln()), XBC2=lambda: xbc_silu(1), XBC3=lambda: xbc_silu(2),
                    XBC4=lambda: xbc_silu(3), XBC5=lambda: (xbc_silu(4), xbc_silu(5)),
                    QK2=lambda: rows_exp(0, 0), QK3=lam_exp, V0=lambda: rows_exp(0, 1),
                    GU0=lambda: rows_exp(1, 0), GU1=gm_square, Z0=lambda: rows_exp(1, 1),
                    Z3=lambda: split_high(i, "ya32_ready", i + 1, slice(A_YA, A_YA + 4), uu, "ya_hi"),
                    GA0=yb_square, GA1=lambda: root(1, i, "yb_ms", "yb_root"),
                    GA2=lambda: (split_high(i, "yb32_ready", i + 1, slice(A_YB, A_YB + 8), xbc[:, 0:8, :], "yb_hi"), qk_square()),
                    GA3=lambda: small_root(i, "qk_sums", qs, 64, "qk_root"), BA0=qk_copy, BA2=lambda: attn_exp(0),
                    GB2=lambda: attn_exp(1), BB1=o_square, BB2=lambda: small_root(i, "o_sums", os_, P, "o_root"), GC1=yc_high,
                    BC3=lambda: split_high(i, "mg32_ready", i + 1, slice(A_MG, A_MG + 8), G0, "mg_hi"))

                def take(n, g):
                    kind, m = g["kind"], g["n"]
                    if g["taker"] == "act" or kind in ("XBC", "UP"):
                        arrived(1, i, n)
                    pair = bank(g).rearrange("p (k t) -> p k t", t=S)
                    if kind == "XBC":
                        conv_open(1, i, g, "cw", "cb", 4, 3, (2 * m, 2 * m + 1), (xbc[:, 2 * m, :], xbc[:, 2 * m + 1, :]), "xbc_open")
                    elif kind == "QK":
                        last = A(qk[:, :, 256 * m:256 * m + 256], pair, ACT.Copy)
                        last.then_inc(taken["act"], 1)
                        if m == 3:
                            act.drain().then_inc(step("qk_in"), 1)
                    elif kind == "V":
                        A(vv[:, :, 256 * m:256 * m + 256], pair, ACT.Copy).then_inc(taken["act"], 1)
                        if m == 1:
                            act.drain().then_inc(step("v_in"), 1)
                    elif kind == "GV":
                        A(vg[:, :, 256 * m:256 * m + 256], pair, ACT.Gelu_apprx_tanh).then_inc(taken["act"], 1)
                        if m == 1:
                            act.drain().then_inc(step("vg_ready"), 1)
                    elif kind == "GU":
                        A(uu[:, 2 * m:2 * m + 2, :], pair, ACT.Gelu_apprx_tanh).then_inc(taken["act"], 1)
                        if m == 1:
                            act.drain().then_inc(step("u_ready"), 1)
                    elif kind == "Z":
                        A(SZ[:, 2 * m:2 * m + 2, :], pair, ACT.Silu).then_inc(taken["act"], 1)
                        if m == 3:
                            act.drain().then_inc(step("z_ready"), 1)
                    elif kind in ("GA", "GB", "GC"):
                        if kind == "GB" and m == 0:
                            act.wait_ge(step("ya_ready"), i + 1)
                        if kind == "GC" and m == 0:
                            act.wait_ge(step("yb_ready"), i + 1)
                        if kind == "GA" and m == 0:
                            act.wait_ge(step("mixed"), i + 1)
                        reg = dict(GA=G0, GB=ug[:, :, :], GC=SZ)[kind]
                        A(reg[:, 2 * m:2 * m + 2, :], pair, ACT.Sigmoid).then_inc(taken["act"], 1)
                    elif kind == "UP":
                        up_open(1, i, g)

                def up_open(b, i, g):
                    m, val = g["n"] // 2, g["n"] % 2
                    if g["n"] >= 4:
                        act.wait_ge(step("up_free"), layer(b, i) * FP + m - 1)
                    buf = ypair(m % 2, val)
                    t0 = 2 * m + val * FT
                    conv_open(b, i, g, "fw", "fb", 3, 2 if b == 1 else 1, (t0, t0 + 1), (buf[:, 0, :], buf[:, 1, :]), f"up_open{b}")

                def up_act(b, i, m, func):
                    act.wait_ge(step("up_conv"), layer(b, i) * FP + m + 1)
                    v = ypair(m % 2, 0)
                    A(v, v, func).then_inc(step("up_act"), 1)

                def gated_high(b, i, m):
                    split_high(i, "gated32", layer(b, i) * FP + m + 1, slice(A_G + 2 * m, A_G + 2 * m + 2), ypair(m % 2, 0), "gated_hi")

                for n, g in enumerate(G1):
                    if g["name"] == "UP0":
                        squares(1, i, "x_mid", "n2_sq", x[:, :, :])
                        root(1, i, "n2_ms", "n2_root")
                        norm_high(1, i, "h2_32_ready", A_H2, "h2_hi")
                    take(n, g)
                    high_part(act, 1, i, n + SPL, G1)
                    if g["name"] in after:
                        after[g["name"]]()
                    if g["kind"] == "UP":
                        if g["n"] % 2 == 1:
                            up_act(1, i, g["n"] // 2, ACT.Silu)
                        elif g["n"] >= 2:
                            gated_high(1, i, g["n"] // 2 - 1)
                        if g["n"] == 2 * FP - 1:
                            gated_high(1, i, FP - 1)

            with act.Fori(0, LAYERS) as i:
                squares(2, i, "x_ready", "n1_sq", x[:, :, :])
                high_part(act, 2, i, 0, G2)
                high_part(act, 2, i, 1, G2)
                root(2, i, "n1_ms", "n1_root")
                norm_high(2, i, "h32_ready", A_H, "h_hi")
                high_part(act, 2, i, 2, G2)
                uview = ug[:, :, :].rearrange("p k t -> p (k t)").rearrange("p (a c) -> p a c", a=TT)
                v2 = qkv[:, :].rearrange("p (a c) -> p a c", a=TT)

                def b2_exp(u):
                    act.wait_ge(step("b2_max"), i * 8 + u + 1)
                    A(b2_P, b2_P, ACT.Exp, bias=bnm[:, 0:1], accum_out=bsm[:, 0:1]).then_inc(step("b2_exp"), 1)

                def b2_PT_copy(u):
                    act.wait_ge(step("b2_turned"), i * 8 + u + 1)
                    if u >= 2 and u % 2 == 0:
                        act.wait_ge(step("b2_out"), i * 4 + u // 2)
                    px = PS[:, 2 * (u % 2):2 * (u % 2) + 2, :].rearrange("p a c -> p (a c)")[:, 0:768]
                    A(b2_PT[:, :, (u % 2) * P:(u % 2 + 1) * P], px.rearrange("p (k q) -> p k q", q=P), ACT.Copy).then_inc(step("b2_PT_ready"), 1)

                def at_high(j):
                    act.wait_ge(step("b2_out"), i * 4 + j + 1)
                    A(ahi[:, A_AT + j, :], pC[:, 0:S], ACT.Copy).then_inc(step("at_hi"), 1)

                def pd_high():
                    act.wait_ge(step("pooled"), i + 1)
                    A(ahi[:, A_PD:A_PD + 8, :], PS[:, 0:4, :].rearrange("p a (k t) -> p (a k) t", t=S), ACT.Copy).then_inc(step("pd_hi"), 1)

                def take2(n, g):
                    kind, m = g["kind"], g["n"]
                    if g["taker"] == "act" or kind in ("WP", "UP"):
                        arrived(2, i, n)
                    pair = bank(g).rearrange("p (k t) -> p k t", t=S)
                    if kind == "PU":
                        A(uview[:, :, 256 * m:256 * m + 256], pair, ACT.Copy).then_inc(taken["act"], 1)
                        if m == 3:
                            act.drain().then_inc(step("pu_ready"), 1)
                    elif kind == "Q":
                        if m == 0:
                            act.wait_ge(step("pooled"), i + 1)
                        A(xbc[:, 2 * m:2 * m + 2, :], pair, ACT.Copy).then_inc(taken["act"], 1)
                    elif kind == "K":
                        A(g01[:, 2 * m:2 * m + 2, :], pair, ACT.Copy).then_inc(taken["act"], 1)
                        if m == 5:
                            act.drain().then_inc(step("qk2_ready"), 1)
                    elif kind == "V":
                        A(v2[:, :, 256 * m:256 * m + 256], pair, ACT.Copy).then_inc(taken["act"], 1)
                        if m == 5:
                            act.drain().then_inc(step("v2_ready"), 1)
                    elif kind in ("GP", "GT"):
                        reg = ug if kind == "GP" else xbc
                        if kind == "GT" and m == 0:
                            act.wait_ge(step("b2_scores"), i * 8 + 8)
                        A(reg[:, 2 * m:2 * m + 2, :], pair, ACT.Sigmoid).then_inc(taken["act"], 1)
                    elif kind == "WP":
                        for t in range(2):
                            last = A(ahi[:, A_PO + 2 * m + t, :], pair[:, t, :], ACT.Copy, scale=col(2, "ps", 2 * m + t))
                        last.then_inc(step("po_hi"), 1)
                    elif kind == "UP" and m % 2 == 0:
                        up_open(2, i, g)

                for n, g in enumerate(G2):
                    if g["name"] == "UP0":
                        squares(2, i, "x_mid", "n2_sq", x[:, :, :])
                        root(2, i, "n2_ms", "n2_root")
                        norm_high(2, i, "h2_32_ready", A_H2, "h2_hi")
                    take2(n, g)
                    high_part(act, 2, i, n + SPL, G2)
                    if g["name"] == "Q0":
                        pd_high()
                    if g["name"] in PV_AT:
                        at_high(PV_AT[g["name"]])
                    if g["name"] in SC_AT:
                        b2_exp(SC_AT[g["name"]])
                    if g["name"] in TR_AT:
                        b2_PT_copy(TR_AT[g["name"]])
                    if g["name"] == "WB3":
                        split_high(i, "mg32_ready", layer(2, i) + 1, slice(A_MG, A_MG + 8), ug[:, :, :], "mg_hi")
                    if g["kind"] == "UP":
                        if g["n"] % 2 == 0:
                            up_act(2, i, g["n"] // 2, ACT.Gelu_apprx_tanh)
                        else:
                            gated_high(2, i, g["n"] // 2)
            squares(2, LAYERS, "x_ready", "n1_sq", x[:, :, :])
            root(2, LAYERS, "n1_ms", "n1_root")

        @block.vector
        def _(dve):
            V = nc.vector
            TTo = V.tensor_tensor
            STT = V.scalar_tensor_tensor

            def ordered():
                dve.drain()

            def rstd_of(i, root):
                dve.wait_ge(step(root), i + 1)
                V.reciprocal(rstd[:, :], rstd[:, :])
                ordered()

            def norm(b, i, root, gain, ready32):
                rstd_of(layer(b, i), root)
                for k in range(KD):
                    last = STT(h32[:, k, :], x[:, k, :], col(b, gain, k), rstd[:, :], ALU.mult, ALU.mult)
                    if k % 4 == 3:
                        last.then_inc(step(ready32), 1)

            def norm_low(b, i, a0, hi, done):
                for q in range(2):
                    dve.wait_ge(step(hi), layer(b, i) * 2 + q + 1)
                    last = TTo(alo[:, a0 + 4 * q:a0 + 4 * q + 4, :], h32[:, 4 * q:4 * q + 4, :],
                               ahi[:, a0 + 4 * q:a0 + 4 * q + 4, :].bitcast(f32), ALU.subtract)
                last.then_inc(step(done), 1)

            def split_low(hi, value, tiles, src, done):
                dve.wait_ge(step(hi), value)
                TTo(alo[:, tiles, :], src, ahi[:, tiles, :].bitcast(f32), ALU.subtract).then_inc(step(done), 1)

            def bank(g):
                return PJ[:, g["bank"], :]

            def arrived(b, i, n):
                dve.wait_ge(group_done, count(b, i, n + 1))

            def conv_taps(b, i, g, wkey, taps, shifts, tiles, dst):
                for tap, sh in shifts:
                    for t in range(2):
                        src = bank(g)[:, t * S:(t + 1) * S]
                        o, s = (slice(sh, S), slice(0, S - sh)) if sh > 0 else (slice(0, S + sh), slice(-sh, S))
                        last = STT(dst[t][:, o], src[:, s], col(b, wkey, tiles[t] * taps + tap), dst[t][:, o], ALU.mult, ALU.add)
                    if (tap, sh) != shifts[-1]:
                        ordered()
                return last

            def layer_end(b, i):
                dve.wait_ge(step("x_end"), layer(b, i) + 1)
                dve.sem_inc(step("layer_done"), 1)
                dve.sem_inc(step("x_ready"), 1)

            dve.sem_inc(taken["dve"], 1)
            dve.sem_inc(w_lo_dve, 1)
            dve.sem_inc(step("b2_bias_free"), 1)
            dve.wait_ge(step("x_turned"), 1)
            dve.sem_inc(step("layer_done"), 1)
            V.tensor_copy(x[:, :, :], PS[:, 0:4, :].rearrange("p a (k t) -> p (a k) t", t=S)).then_inc(step("x_ready"), 1)
            dve.wait_ge(step("bias_product"), 1)
            TTo(qkv[0:12, 1536:2048], pC[0:12, :], qkv[0:12, 1024:1536], ALU.add).then_inc(step("bias_row"), 1)

            with dve.Fori(0, LAYERS) as i:
                dve.wait_ge(step("par_in1"), i * 80 + 80)
                norm(1, i, "n1_root", "norm1", "h32_ready")
                low_part(V, 1, i, 0, G1, False)
                norm_low(1, i, A_H, "h_hi", "h_ready")
                low_part(V, 1, i, 1, G1, False)
                low_part(V, 1, i, 2, G1, False)

                def dt_abs():
                    dve.wait_ge(step("dt_proj"), i + 1)
                    TTo(dtx.rearrange("p (c h) -> p c h", c=TT), pC[:, 256:288].rearrange("p (c h) -> p c h", c=TT),
                        bc(row("dtb"), [P, TT, 16], 1), ALU.add)
                    ordered()
                    STT(dta, dtx, -1.0, dtx, ALU.mult, ALU.max).then_inc(step("dt_abs"), 1)

                def dt_one():
                    dve.wait_ge(step("dt_exp"), i + 1)
                    V.tensor_scalar(dtu, dte, 1.0, None, ALU.add).then_inc(step("dt_one"), 1)

                def dt_finish():
                    dve.wait_ge(step("dt_ln"), i + 1)
                    STT(dtv, dtu, -1.0, dte, ALU.add, ALU.subtract)
                    STT(dtx, dtx, 0.0, dtl, ALU.max, ALU.add)
                    V.reciprocal(dta, dtu)
                    ordered()
                    TTo(dtv, dtv, dta, ALU.mult)
                    ordered()
                    TTo(dtv, dtx, dtv, ALU.subtract)
                    ordered()
                    dve.wait_ge(step("a_exp"), i + 1)
                    STT(dtA.rearrange("p (c h) -> p c h", c=TT), dtv.rearrange("p (c h) -> p c h", c=TT), -1.0,
                        bc(aexp, [P, TT, 16], 1), ALU.mult, ALU.mult).then_inc(step("dta_ready"), 1)

                def lam_sums():
                    lv = lam_row.rearrange("p (a b d) -> p a b d", a=2, b=2)
                    TTo(lmp.rearrange("p (a d) -> p a d", a=2), lv[:, :, 0, :], lv[:, :, 1, :], ALU.mult)
                    ordered()
                    V.tensor_reduce(lms, lmp.rearrange("p (a d) -> p a d", a=2), AX.X, ALU.add).then_inc(step("lam_sums"), 1)

                def lam_value():
                    dve.wait_ge(step("lam_exp"), i + 1)
                    TTo(lmv, lms[:, 0:1], lms[:, 1:2], ALU.subtract)
                    ordered()
                    TTo(lmv, lmv, row("li")[:, 0:1], ALU.add)

                def chunk_open(c):
                    dve.wait_ge(step("scan_opened"), i * 2 + c + 1)
                    V.tensor_copy(acum, pC[:, 0:16])
                    for g in range(2):
                        TTo(cbm[:, g, :], pC[:, 128 + 128 * g:256 + 128 * g], tri[:, :], ALU.mult)
                    if c == 0:
                        V.tensor_copy(bT[:, :, :], pB[:, 0, 0:256].rearrange("p (g n) -> p g n", g=2))
                    else:
                        pass
                    TTo(xdt.rearrange("p (h q) -> p h q", q=64), pA.rearrange("p a (h q) -> p (a h) q", q=64),
                        bc(dtv[:, 16 * c:16 * c + 16], [P, 16, 64], 2), ALU.mult).then_inc(step("chunk_ready"), 1)

                def seg(c, g):
                    dve.wait_ge(step("rows_ready"), i * 4 + 2 * c + g + 1)
                    if (c, g) != (0, 0):
                        dve.wait_ge(step("y_ready"), i * 4 + 2 * c + g)
                    rows = pB.rearrange("p a (h t) -> p (a h) t", t=P)
                    TTo(dec, rows, bc(acum[:, 8 * g:8 * g + 8], [P, 8, P], 2), ALU.subtract)
                    if c == 0:
                        TTo(dend, rows[:, :, P - 1], acum[:, 8 * g:8 * g + 8], ALU.subtract)
                    ordered()
                    V.tensor_scalar(dec, dec, 0.0, None, ALU.min).then_inc(step("seg_ready"), 1)

                def dec_mul(c, g):
                    dve.wait_ge(step("dec_exp"), i * 4 + 2 * c + g + 1)
                    last = TTo(dec, dec, bc(cbm[:, g, :], [P, 8, P], 1), ALU.mult)
                    last.then_inc(step("dec_ready"), 1)
                    if c == 0:
                        dve.wait_ge(step("dend_exp"), i * 2 + g + 1)
                        if g:
                            dve.wait_ge(step("state_ready"), i * 2 + 1)
                        TTo(cdec[:, 0:4, :].rearrange("p h t -> p (h t)").rearrange("p (h q) -> p h q", q=64),
                            xdt[:, 512 * g:512 * g + 512].rearrange("p (h q) -> p h q", q=64),
                            bc(dend, [P, 8, 64], 2), ALU.mult).then_inc(step("xdtd_ready"), 1)
                    else:
                        dve.wait_ge(step("cdec_exp"), i * 2 + g + 1)
                        TTo(cdec, cdec, bc(xbc[:, 10 + g, P:2 * P], [P, 8, P], 1), ALU.mult).then_inc(step("cdec_ready"), 1)
                    rows_release()

                def rows_release():
                    ordered()
                    V.tensor_copy(gmr[:, 0:1], acum[:, 0:1]).then_inc(step("rows_taken"), 1)

                def state_copy(g):
                    dve.wait_ge(step("state_ready"), i * 2 + g + 1)
                    V.tensor_copy(prev[:, g, :], pC[:, :]).then_inc(step("prev_ready"), 1)

                def y_take(c, g):
                    dve.wait_ge(step("y_ready"), i * 4 + 2 * c + g + 1)
                    for k in range(4):
                        v = xbc[:, 4 * g + k, c * P:(c + 1) * P]
                        last = STT(v, v, col(1, "sd", 4 * g + k), pA[:, g, k * P:(k + 1) * P], ALU.mult, ALU.add)
                    last.then_inc(step("y_taken"), 1)

                def gm_norm():
                    dve.wait_ge(step("gm_root"), i + 1)
                    V.reciprocal(gmr, gms)
                    ordered()
                    for tt in range(TT):
                        last = STT(vg[:, tt, :], vg[:, tt, :], gmr[:, tt:tt + 1], row("gvg"), ALU.mult, ALU.mult)
                    last.then_inc(step("vn_ready"), 1)
                    dve.wait_ge(step("ws_turned"), i + 1)
                    TTo(wsT[:, :, :], pC.rearrange("p (g t) -> p g t", g=4), bc(tri[:, :], [P, 4, P], 1), ALU.mult).then_inc(step("wsT_ready"), 1)

                def gm_out():
                    dve.wait_ge(step("mixed"), i + 1)
                    dve.wait_ge(step("u_ready"), i + 1)
                    t512 = vg
                    for n in range(TT):
                        TTo(t512[:, n, :], pA[:, n, :], row("gb"), ALU.add)
                    ordered()
                    for n in range(TT):
                        v = uu[:, :, n * P:(n + 1) * P]
                        last = TTo(v, v, t512[:, n, :].rearrange("p (g t) -> p g t", g=4), ALU.mult)
                    last.then_inc(step("ya32_ready"), 1)

                def yz():
                    dve.wait_ge(step("z_ready"), i + 1)
                    TTo(xbc[:, 0:8, :], xbc[:, 0:8, :], SZ, ALU.mult).then_inc(step("yz_ready"), 1)

                def yb_norm():
                    rstd_of(i, "yb_root")
                    for k in range(KD):
                        last = STT(xbc[:, k, :], xbc[:, k, :], col(1, "sg", k), rstd[:, :], ALU.mult, ALU.mult)
                    last.then_inc(step("yb32_ready"), 1)

                def qk_sums():
                    dve.wait_ge(step("qk_sq"), i + 1)
                    V.tensor_reduce(qs, prob.rearrange("p (j d) -> p j d", d=64), AX.X, ALU.add).then_inc(step("qk_sums"), 1)

                def qk_norm():
                    v = qk.rearrange("p a (j d) -> p (a j) d", d=64)
                    dve.wait_ge(step("qk_root"), i + 1)
                    V.reciprocal(qr, qs)
                    ordered()
                    TTo(v, v, bc(qr, [P, 32, 64], 2), ALU.mult)
                    ordered()
                    for tt in range(TT):
                        for m, key in ((0, "qg"), (1, "kg")):
                            w = qk[:, tt, 512 * m:512 * m + 512].rearrange("p (j d) -> p j d", d=64)
                            TTo(w, w, bc(row(key), [P, 8, 64], 1), ALU.mult)
                    ordered()
                    r4 = [prob[:, 256 * q:256 * q + 256].rearrange("p (j d) -> p j d", d=8) for q in range(4)]
                    for tt in range(TT):
                        w = qk[:, tt, :].rearrange("p (j d) -> p j d", d=64)
                        t1, t2 = w[:, :, 0:8], w[:, :, 8:16]
                        cs, sn = bc(rope[:, tt, 0, :], [P, 16, 8], 1), bc(rope[:, tt, 1, :], [P, 16, 8], 1)
                        z = slice(16 * tt, 16 * tt + 16)
                        TTo(r4[0][:, z, :], t1, cs, ALU.mult)
                        TTo(r4[1][:, z, :], t2, sn, ALU.mult)
                        TTo(r4[2][:, z, :], t2, cs, ALU.mult)
                        TTo(r4[3][:, z, :], t1, sn, ALU.mult)
                    ordered()
                    TTo(v[:, :, 0:8], r4[0], r4[1], ALU.subtract)
                    TTo(v[:, :, 8:16], r4[2], r4[3], ALU.add).then_inc(step("qk_normed"), 1)

                def attn_max(qt):
                    W = (qt + 1) * P
                    dve.wait_ge(step("scores"), i * 2 + qt + 1)
                    if qt:
                        dve.wait_ge(step("w_turned"), i * 2 + 1)
                    pv = prob[:, 0:8 * W].rearrange("p (j k) -> p j k", j=8)
                    nb_banks = 8 * W // 512
                    TTo(pv, PS[:, 0:nb_banks, :].rearrange("p a (j k) -> p (a j) k", k=W), bc(amask[:, S - W:S], [P, 8, W], 1), ALU.add)
                    ordered()
                    V.tensor_reduce(mx, pv, AX.X, ALU.max)
                    ordered()
                    V.tensor_scalar(nb, mx, -0.125, None, ALU.mult).then_inc(step("max_ready"), 1)

                def attn_weights(qt):
                    W = (qt + 1) * P
                    dve.wait_ge(step("attn_exp"), i * 2 + qt + 1)
                    V.reciprocal(pr, ps_)
                    ordered()
                    odd = pr[:, 4:8]
                    V.tensor_scalar(odd, odd, lmv, None, ALU.mult)
                    ordered()
                    pv = prob[:, 0:8 * W].rearrange("p (j k) -> p j k", j=8)
                    TTo(pv, pv, bc(pr, [P, 8, W], 2), ALU.mult)
                    ordered()
                    pw = prob[:, 0:8 * W].rearrange("p (m h k) -> p m h k", h=H1, m=2)
                    TTo(pw[:, 0, :, :], pw[:, 0, :, :], pw[:, 1, :, :], ALU.subtract).then_inc(step("w_ready"), 1)

                def wT_copy(qt):
                    dve.wait_ge(step("w_turned"), i * 2 + qt + 1)
                    J = 4 * (qt + 1)
                    V.tensor_copy(wT[:, 0:J, :], pB.rearrange("p a (j t) -> p (a j) t", t=P)[:, 0:J, :]).then_inc(step("wT_ready"), 1)

                def o_take(qt):
                    dve.wait_ge(step("o_ready"), i * 2 + qt + 1)
                    V.tensor_copy(o32[:, qt, :], pA[:, 0, :]).then_inc(step("o_taken"), 1)

                def o_sums():
                    dve.wait_ge(step("o_sq"), i + 1)
                    V.tensor_reduce(os_, prob[:, 0:1024].rearrange("p (j d) -> p j d", d=P), AX.X, ALU.add).then_inc(step("o_sums"), 1)

                def o_norm():
                    dve.wait_ge(step("o_root"), i + 1)
                    V.reciprocal(orr, os_)
                    ordered()
                    V.tensor_scalar(orr, orr, row("li")[:, 1:2], None, ALU.mult)
                    ordered()
                    v = o32.rearrange("p a (h d) -> p (a h) d", d=P)
                    TTo(v, v, bc(orr, [P, 8, P], 2), ALU.mult)
                    ordered()
                    TTo(v, v, bc(row("sub"), [P, 8, P], 1), ALU.mult).then_inc(step("o_normed"), 1)

                def yc_low():
                    split_low("yc_hi", i + 1, slice(A_YC, A_YC + 4), pA.rearrange("p a (j t) -> p (a j) t", t=S), "yc_ready")

                after = dict(
                    XBC0=lambda: (dt_abs(), dt_one()), XBC1=lambda: dt_finish(), XBC2=lam_sums,
                    QK0=lambda: chunk_open(0), QK1=lambda: seg(0, 0), QK2=lambda: dec_mul(0, 0),
                    QK3=lambda: (state_copy(0), lam_value(), y_take(0, 0), seg(0, 1)), V0=lambda: dec_mul(0, 1),
                    V1=lambda: (state_copy(1), y_take(0, 1)), GV0=lambda: chunk_open(1), GV1=lambda: seg(1, 0),
                    GU0=lambda: dec_mul(1, 0), GU1=lambda: (y_take(1, 0), seg(1, 1), gm_norm()),
                    Z0=lambda: dec_mul(1, 1), Z1=lambda: y_take(1, 1), Z3=lambda: (gm_out(), yz()),
                    GA0=lambda: split_low("ya_hi", i + 1, slice(A_YA, A_YA + 4), uu, "ya_ready"), GA1=yb_norm,
                    GA2=lambda: (split_low("yb_hi", i + 1, slice(A_YB, A_YB + 8), xbc[:, 0:8, :], "yb_ready"), qk_sums()),
                    GA3=qk_norm, BA2=lambda: attn_max(0), BA3=lambda: attn_weights(0), GB0=lambda: wT_copy(0),
                    GB1=lambda: o_take(0), GB2=lambda: attn_max(1), GB3=lambda: attn_weights(1), BB0=lambda: wT_copy(1),
                    BB1=lambda: o_take(1), BB2=o_sums, BB3=o_norm, GC1=yc_low)

                def take(n, g):
                    kind, m = g["kind"], g["n"]
                    if g["taker"] != "dve" or not g["closes"]:
                        return
                    pair = bank(g).rearrange("p (k t) -> p k t", t=S)
                    if kind == "XBC":
                        dve.wait_ge(step("xbc_open"), i * 6 + m + 1)
                        conv_taps(1, i, g, "cw", 4, ((2, 1), (1, 2), (0, 3)), (2 * m, 2 * m + 1),
                                  (xbc[:, 2 * m, :], xbc[:, 2 * m + 1, :])).then_inc(step("xbc_conv"), 1)
                        ordered()
                        dve.drain().then_inc(taken["dve"], 1)
                    elif kind == "BA":
                        arrived(1, i, n)
                        v = G0[:, 2 * m:2 * m + 2, :]
                        TTo(v, pair, v, ALU.mult).then_inc(taken["dve"], 1)
                    elif kind in ("BB", "BC"):
                        arrived(1, i, n)
                        v = (ug[:, 2 * m:2 * m + 2, :] if kind == "BB" else SZ[:, 2 * m:2 * m + 2, :])
                        TTo(v, pair, v, ALU.mult).then_inc(taken["dve"], 1)
                        ordered()
                        o = G0[:, 2 * m:2 * m + 2, :]
                        last = TTo(o, o, v, ALU.add)
                        if kind == "BC" and m == 3:
                            last.then_inc(step("mg32_ready"), 1)
                    elif kind in ("OUT", "DN"):
                        residual(1, i, n, g)
                    elif kind == "UP":
                        up_take(1, i, n, g)

                def residual(b, i, n, g):
                    arrived(b, i, n)
                    m = g["n"] if g["kind"] == "OUT" else g["n"] // 4
                    pair = bank(g).rearrange("p (k t) -> p k t", t=S)
                    v = x[:, 2 * m:2 * m + 2, :]
                    last = TTo(v, pair, v, ALU.add)
                    last.then_inc(taken["dve"], 1)
                    if m == 3:
                        name = "x_mid" if g["kind"] == "OUT" else "x_end"
                        dve.drain().then_inc(step(name), 1)

                def up_take(b, i, n, g):
                    m, val = g["n"] // 2, g["n"] % 2
                    buf = ypair(m % 2, val)
                    t0 = 2 * m + val * FT
                    if b == 1:
                        dve.wait_ge(step("up_open1"), i * (2 * FP) + g["n"] + 1)
                        last = conv_taps(1, i, g, "fw", 3, ((1, 1), (0, 2)), (t0, t0 + 1), (buf[:, 0, :], buf[:, 1, :]))
                        last.then_inc(taken["dve"], 1)
                        if not val:
                            dve.drain().then_inc(step("up_conv"), 1)
                    elif not val:
                        dve.wait_ge(step("up_open2"), i * FP + m + 1)
                        last = conv_taps(2, i, g, "fw", 3, ((0, 1), (2, -1)), (t0, t0 + 1), (buf[:, 0, :], buf[:, 1, :]))
                        last.then_inc(taken["dve"], 1)
                        dve.drain().then_inc(step("up_conv"), 1)

                def gate_up(b, i, n, g):
                    m = g["n"] // 2
                    v = ypair(m % 2, 0)
                    if b == 1:
                        ordered()
                    dve.wait_ge(step("up_act"), layer(b, i) * FP + m + 1)
                    if b == 1:
                        TTo(v, v, ypair(m % 2, 1), ALU.mult).then_inc(step("gated32"), 1)
                    else:
                        arrived(2, i, n)
                        TTo(v, bank(g).rearrange("p (k t) -> p k t", t=S), v, ALU.mult).then_inc(taken["dve"], 1)
                        dve.drain().then_inc(step("gated32"), 1)

                def gated_low(b, i, m):
                    dve.wait_ge(step("gated_hi"), layer(b, i) * FP + m + 1)
                    t = slice(A_G + 2 * m, A_G + 2 * m + 2)
                    last = TTo(alo[:, t, :], ypair(m % 2, 0), ahi[:, t, :].bitcast(f32), ALU.subtract)
                    last.then_inc(step("up_free"), 1)
                    if m == FP - 1:
                        dve.drain().then_inc(step("gated_ready"), 1)

                def up_stream(b, i, n, g, G):
                    if g["n"] % 2 == 1:
                        gate_up(b, i, n, g)
                        if b == 2:
                            pass
                    elif g["n"] >= 2:
                        gated_low(b, i, g["n"] // 2 - 1)
                    if g["n"] == 2 * FP - 1:
                        gated_low(b, i, FP - 1)

                for n, g in enumerate(G1):
                    if g["name"] == "OUT0":
                        split_low("mg_hi", i + 1, slice(A_MG, A_MG + 8), G0, "mg_ready")
                    if g["name"] == "UP0":
                        norm(1, i, "n2_root", "norm2", "h2_32_ready")
                        norm_low(1, i, A_H2, "h2_hi", "h2_ready")
                    take(n, g)
                    low_part(V, 1, i, n + SPL, G1, False)
                    if g["name"] in after:
                        ordered()
                        after[g["name"]]()
                    if g["kind"] == "UP":
                        up_stream(1, i, n, g, G1)
                layer_end(1, i)

            with dve.Fori(0, LAYERS) as i:
                dve.wait_ge(step("par_in2"), i * 48 + 48)
                norm(2, i, "n1_root", "norm1", "h32_ready")
                low_part(V, 2, i, 0, G2, False)
                norm_low(2, i, A_H, "h_hi", "h_ready")
                low_part(V, 2, i, 1, G2, False)
                low_part(V, 2, i, 2, G2, False)

                def b2_max(u):
                    dve.wait_ge(step("b2_scores"), i * 8 + u + 1)
                    dve.wait_ge(step("b2_bias_in"), i * 384 + 48 * (u + 1))
                    px = PS[:, 2 * (u % 2):2 * (u % 2) + 2, :].rearrange("p a c -> p (a c)")[:, 0:768]
                    if u:
                        dve.wait_ge(step("b2_turned"), i * 8 + u)
                    STT(b2_P, px, float(P) ** -0.5, b2_bias.rearrange("p g k -> p (g k)"), ALU.mult, ALU.add).then_inc(step("b2_bias_free"), 1)
                    ordered()
                    V.tensor_reduce(bmx[:, 0:1], b2_P, AX.X, ALU.max)
                    ordered()
                    V.tensor_scalar(bnm[:, 0:1], bmx[:, 0:1], -1.0, None, ALU.mult).then_inc(step("b2_max"), 1)

                def b2_norm(u):
                    dve.wait_ge(step("b2_exp"), i * 8 + u + 1)
                    V.reciprocal(brr[:, 0:1], bsm[:, 0:1])
                    ordered()
                    V.tensor_scalar(b2_P, b2_P, brr[:, 0:1], None, ALU.mult).then_inc(step("b2_P_ready"), 1)

                def at_low(j):
                    dve.wait_ge(step("at_hi"), i * 4 + j + 1)
                    last = TTo(alo[:, A_AT + j, :], pC[:, 0:S], ahi[:, A_AT + j, :].bitcast(f32), ALU.subtract)
                    last.then_inc(step("at_lo"), 1)
                    if j == 3:
                        dve.drain().then_inc(step("at_ready"), 1)

                def take2(n, g):
                    kind, m = g["kind"], g["n"]
                    if g["taker"] != "dve" or not g["closes"]:
                        return
                    pair = bank(g).rearrange("p (k t) -> p k t", t=S)
                    if kind == "WP":
                        dve.wait_ge(step("po_hi"), i * 4 + m + 1)
                        for t in range(2):
                            k = A_PO + 2 * m + t
                            last = STT(alo[:, k, :], pair[:, t, :], col(2, "ps", 2 * m + t), ahi[:, k, :].bitcast(f32), ALU.mult, ALU.subtract)
                        last.then_inc(taken["dve"], 1)
                        if m == 3:
                            dve.drain().then_inc(step("po_ready"), 1)
                    elif kind == "WA":
                        arrived(2, i, n)
                        v = ug[:, 2 * m:2 * m + 2, :]
                        TTo(v, pair, v, ALU.mult).then_inc(taken["dve"], 1)
                    elif kind == "WB":
                        arrived(2, i, n)
                        v, o = xbc[:, 2 * m:2 * m + 2, :], ug[:, 2 * m:2 * m + 2, :]
                        TTo(v, pair, v, ALU.mult).then_inc(taken["dve"], 1)
                        ordered()
                        last = TTo(o, o, v, ALU.add)
                        if m == 3:
                            last.then_inc(step("mg32_ready"), 1)
                    elif kind in ("OUT", "DN"):
                        residual(2, i, n, g)
                    elif kind == "UP":
                        up_take(2, i, n, g)

                for n, g in enumerate(G2):
                    if g["name"] == "OUT0":
                        split_low("mg_hi", layer(2, i) + 1, slice(A_MG, A_MG + 8), ug[:, :, :], "mg_ready")
                    if g["name"] == "UP0":
                        norm(2, i, "n2_root", "norm2", "h2_32_ready")
                        norm_low(2, i, A_H2, "h2_hi", "h2_ready")
                    take2(n, g)
                    low_part(V, 2, i, n + SPL, G2, False)
                    if g["name"] in PV_AT:
                        at_low(PV_AT[g["name"]])
                    if g["name"] in SC_AT:
                        b2_max(SC_AT[g["name"]])
                    if g["name"] in TR_AT:
                        pass
                    if g["name"] in SC_AT:
                        b2_norm(SC_AT[g["name"]])
                    if g["name"] == "Q0":
                        split_low("pd_hi", i + 1, slice(A_PD, A_PD + 8), PS[:, 0:4, :].rearrange("p a (k t) -> p (a k) t", t=S), "pd_ready")
                    if g["kind"] == "UP":
                        up_stream(2, i, n, g, G2)
                layer_end(2, i)

            rstd_of(2 * LAYERS, "n1_root")
            for k in range(KD):
                last = STT(h32[:, k, :], x[:, k, :], colsf[:, k:k + 1], rstd[:, :], ALU.mult, ALU.mult)
            last.then_inc(step("f_normed"), 1)
            for tt in range(TT):
                dve.wait_ge(step("out_turned"), tt + 1)
                V.tensor_copy(g01[:, 4 * tt:4 * tt + 4, :].rearrange("p k t -> p (k t)"), pA.rearrange("p a c -> p (a c)")).then_inc(step("out_ready"), 1)


def kernel(**inputs):
    import numpy as np
    import concourse.bacc as bacc
    from concourse import mybir
    from concourse.bass_utils import run_bass_kernel_spmd as run

    f32 = mybir.dt.float32
    a = {k: np.ascontiguousarray(v) for k, v in inputs.items()}
    L, S, P = 2, 256, 128

    def by_feature(v):
        v = v.reshape(L, -1, P, *v.shape[2:])
        return np.moveaxis(v, 2, 1).reshape(L, P, -1)

    cols_1 = np.concatenate([by_feature(a["attn_norm_g"]), by_feature(a["ssm_conv_w"]), by_feature(a["ssm_conv_b"]),
                             by_feature(a["ssm_norm_g"]), by_feature(np.repeat(a["ssm_d"], 64, axis=1)),
                             by_feature(a["ffn_norm_g"]), by_feature(a["ffn_conv_w"]), by_feature(a["ffn_conv_b"])], axis=2)
    cols_2 = np.concatenate([by_feature(a["norm1_2"]), by_feature(a["pool_scale_2"]), by_feature(a["norm2_2"]),
                             by_feature(np.moveaxis(a["conv_w_2"], 1, 2)), by_feature(a["conv_b_2"])], axis=2)
    cols_f = np.ascontiguousarray(a["norm_f_2"].reshape(8, P).T)
    li = np.array([[0.8 - 0.6 * np.exp(-0.3 * n)] for n in range(L)])
    li = np.concatenate([li, 1.0 - li], axis=1).astype(np.float32)
    rows_1 = np.concatenate([a["gm_v_norm_g"], a["gm_b_s"].reshape(L, -1), a["da_q_norm_g"], a["da_k_norm_g"], a["da_subln_g"],
                             a["ssm_dt_bias"], a["ssm_a_log"], li], axis=1)
    p = np.arange(P)
    ident = np.eye(P, dtype=np.float32)
    tri = (p[:, None] <= p[None, :]).astype(np.float32)
    amask = np.concatenate([np.zeros((P, P)), np.where(p[None, :] <= p[:, None], 0.0, -1e30)], axis=1).astype(np.float32)
    inv = (1.0 / (np.float32(500000.0) ** (np.arange(0, 16, 2, dtype=np.float32) / np.float32(16)))).astype(np.float32)
    ang = (np.arange(S, dtype=np.float32)[:, None] * inv[None, :]).astype(np.float32).astype(np.float64)
    rope = np.stack([np.cos(ang), np.sin(ang)], axis=1).astype(np.float32).reshape(2, P, 2, 8)
    rope = np.ascontiguousarray(np.moveaxis(rope, 0, 1)).reshape(P, 32)
    off = np.arange(511) - 255
    n = -off
    mag = np.abs(n)
    large = np.minimum(8 + (np.log(np.maximum(mag, 1) / 8) / np.log(1024 / 8) * 8).astype(np.int32), 15)
    bucket = (n < 0) * 16 + np.where(mag < 8, mag, large)
    onehot = np.zeros((32, 512), np.float32)
    onehot[bucket, np.arange(511)] = 1.0
    offmask = np.full((12, 512), -1e30, np.float32)
    for g, (window, dilation) in enumerate(((128, 1), (512, 4), (2048, 16))):
        ok = (off % dilation == 0) & (mag <= window // (2 * dilation) * dilation)
        offmask[4 * g:4 * g + 4, :511] = np.where(ok, 0.0, -1e30)
    band = np.zeros((S, 4, S), np.float64)
    for g, w in enumerate((2, 4, 8, 16)):
        for t in range(S):
            lo, hi = max(t - w // 2, 0), min(t - w // 2 + w, S)
            band[lo:hi, g, t] = 1.0 / (hi - lo)
            band[t, g, t] -= 1.0
    band = band.astype(np.float32).reshape(2, P, 4 * S)

    feeds = {k: a[k] for k in ("x", "w_in", "gm_w_s", "w_branch_a", "w_branch_b", "w_branch_c", "w_out", "ffn_w_up", "ffn_w_down",
                               "w_in_2", "w_pool_2", "w_a_2", "w_b_2", "w_o_2", "w_up_2", "w_down_2", "rel_bias_2")}
    feeds.update(cols_1=cols_1, cols_2=cols_2, cols_f=cols_f, rows_1=rows_1, lam_1=a["da_lambda"].reshape(L, -1), c_ident=ident, c_tri=tri, c_amask=amask, c_rope=rope,
                 c_onehot=onehot, c_offmask=offmask, c_band=band)
    nc = bacc.Bacc("TRN2", target_bir_lowering=False, num_devices=1)
    arrays, t_in = {}, {}
    for name, v in feeds.items():
        arrays[f"in_{name}"] = np.ascontiguousarray(v)
        t_in[name] = nc.dram_tensor(f"in_{name}", v.shape, f32, kind="ExternalInput").ap()
    t_in["bias_table"] = nc.dram_tensor("bias_table", (12, 129 * 511), f32, kind="Internal").ap()
    out = nc.dram_tensor("out", (1, S, 1024), f32, kind="ExternalOutput").ap()
    build_program(nc, t_in, out)
    r = run(nc, [arrays], core_ids=[0])
    return r.results[0]["out"]
```

```python
def plan_block(names, first_bank=0):
    groups = []
    bank = first_bank
    for name, count, kt, cols, tile, form, taker in names:
        for n in range(count):
            per_bank = 4 if name == "DN" else 1
            sub = n % per_bank
            groups.append(dict(name=f"{name}{n}", kind=name, n=n, kt=kt, cols=cols, form=form, taker=taker,
                               tile=tile(n), bank=bank % 3, opens=sub == 0, closes=sub == per_bank - 1, sub=sub))
            if sub == per_bank - 1:
                bank += 1
    return groups


def build_program(nc, t_in, out):
    import concourse.bass as bass
    from concourse import mybir
    from contextlib import ExitStack

    f32, f32r = mybir.dt.float32, mybir.dt.float32r
    ACT = mybir.ActivationFunctionType
    ALU = mybir.AluOpType
    AX = mybir.AxisListType

    P = 128
    S = 256
    TT = S // P
    D = 1024
    KD = D // P
    PAIRS = KD // 2
    LAYERS = 2
    EPS = 1e-6
    RAW, SPL = 2, 3
    SLOT = 2048
    BANKS = 3
    FF = 2816
    FP = FF // 256
    FT = FF // P
    DNK = FT // 2
    H1 = 4
    NEG = -1e30

    A_H, A_YA, A_YB, A_YC, A_MG, A_H2, A_G = 0, 8, 12, 20, 0, 22, 0
    A_PD, A_PO, A_AT = 8, 16, 24

    const = lambda v: (lambda n: v)
    G1 = plan_block([
        ("XBC", 6, 8, 256, const(A_H), "A", "dve"),
        ("QK", 4, 8, 256, const(A_H), "B", "act"),
        ("V", 2, 8, 256, const(A_H), "B", "act"),
        ("Z", 4, 8, 256, const(A_H), "A", "act"),
        ("GV", 2, 8, 256, const(A_H), "B", "act"),
        ("GU", 2, 8, 256, const(A_H), "A", "act"),
        ("GA", 4, 8, 256, const(A_H), "A", "act"),
        ("GB", 4, 8, 256, const(A_H), "A", "act"),
        ("GC", 4, 8, 256, const(A_H), "A", "act"),
        ("BA", 4, 4, 256, const(A_YA), "A", "dve"),
        ("BB", 4, 8, 256, const(A_YB), "A", "dve"),
        ("BC", 4, 4, 256, const(A_YC), "A", "dve"),
        ("OUT", 4, 8, 256, const(A_MG), "A", "dve"),
        ("UP", 2 * FP, 8, 256, const(A_H2), "A", "dve"),
        ("DN", 16, DNK, 128, lambda n: A_G + DNK * (n % 4 // 2), "A", "dve"),
    ])
    G2 = plan_block([
        ("PU", 4, 8, 256, const(A_H), "B", "act"),
        ("Q", 6, 8, 256, const(A_H), "A", "act"),
        ("K", 6, 8, 256, const(A_H), "A", "act"),
        ("WP", 4, 2, 256, lambda n: A_PD + 2 * n, "A", "dve"),
        ("V", 6, 8, 256, const(A_H), "B", "act"),
        ("GP", 4, 8, 256, const(A_H), "A", "act"),
        ("WA", 4, 8, 256, const(A_PO), "A", "dve"),
        ("GT", 4, 8, 256, const(A_H), "A", "act"),
        ("WB", 4, 4, 256, const(A_AT), "A", "dve"),
        ("OUT", 4, 8, 256, const(A_MG), "A", "dve"),
        ("UP", 2 * FP, 8, 256, const(A_H2), "A", "dve"),
        ("DN", 16, DNK, 128, lambda n: A_G + DNK * (n % 4 // 2), "A", "dve"),
    ])
    assert len({g["name"] for g in G1}) == len(G1)

    C = t_in
    COLS1 = dict(norm1=(0, 8), cw=(8, 48), cb=(56, 12), sg=(68, 8), sd=(76, 8), norm2=(84, 8), fw=(92, 132), fb=(224, 44))
    COLS2 = dict(norm1=(0, 8), ps=(8, 8), norm2=(16, 8), fw=(24, 66), fb=(90, 22))
    ROWS1 = dict(gvg=(0, 512), gb=(512, 512), qg=(1024, 64), kg=(1088, 64), sub=(1152, 128), dtb=(1280, 16),
                 alog=(1296, 16), li=(1312, 2))
    NC1, NC2, NR1 = 268, 112, 1314

    ctx = ExitStack()
    with ctx:
        def sb(name, shape, dt=f32):
            return ctx.enter_context(nc.sbuf_tensor(name, shape, dt))

        def sem(name):
            return ctx.enter_context(nc.semaphore(name))

        raw = sb("w_raw", [P, RAW, SLOT])
        whi = sb("w_hi", [P, SPL, SLOT], f32r)
        wlo = sb("w_lo", [P, SPL, SLOT], f32r)
        ahi = sb("act_hi", [P, 30, S], f32r)
        alo = sb("act_lo", [P, 30, S], f32r)
        x = sb("x", [P, KD, S])
        g01 = sb("gates_01", [P, 2 * KD, S])
        ug = sb("spatial_uv", [P, KD, S])
        xbc = sb("xbc", [P, 12, S])
        qkv = sb("qkv", [P, 12 * S])
        tmp = sb("tmp", [P, 16 * S])
        cols1 = sb("cols1", [P, NC1])
        cols2 = cols1[:, 0:NC2]
        rows1 = sb("rows1", [P, NR1])
        colsf = sb("colsf", [P, KD])
        ident, tri = sb("ident", [P, P]), sb("tri", [P, P])
        amask = sb("amask", [P, S])
        ones = sb("ones", [P, P])
        rope = sb("rope", [P, TT, 2, 8])
        zero = sb("zero", [P, P // 2], f32r)
        rstd = sb("rstd", [P, S])
        sm = sb("small", [P, 400])
        eps = sm[:, 399:400]

        PS = ctx.enter_context(nc.psum_tensor("chain_ps", [P, 5, 512], f32))
        PJ = ctx.enter_context(nc.psum_tensor("proj_ps", [P, BANKS, 512], f32))
        pA, pB, pC = PS[:, 0:2, :], PS[:, 2:4, :], PS[:, 4, :]

        quarter = lambda q, n=1: tmp[:, q * 1024:(q + n) * 1024]
        sq8 = quarter(0, 2).rearrange("p (k t) -> p k t", t=S)
        h32 = quarter(2, 2).rearrange("p (k t) -> p k t", t=S)
        xdt = quarter(0)
        dec = quarter(1).rearrange("p (h t) -> p h t", t=P)
        cdec = quarter(2).rearrange("p (h t) -> p h t", t=P)
        prev = quarter(3).rearrange("p (g q) -> p g q", g=2)
        qkT = quarter(0, 2).rearrange("p (j t) -> p j t", t=S)
        prob = quarter(2, 2)
        qk = qkv[:, 0:2048].rearrange("p (a c) -> p a c", a=TT)
        vv = qkv[:, 2048:3072].rearrange("p (a c) -> p a c", a=TT)
        o32 = qkv[:, 0:1024].rearrange("p (a c) -> p a c", a=TT)
        wT = qkv[:, 1024:2048].rearrange("p (j t) -> p j t", t=P)
        vg = ug[:, 0:4, :].rearrange("p k t -> p (k t)").rearrange("p (a c) -> p a c", a=TT)
        uu = ug[:, 4:8, :]
        G0, SZ = g01[:, 0:8, :], g01[:, 8:16, :]

        at = [0]

        def small(n):
            at[0] += n
            return sm[:, at[0] - n:at[0]]
        dtx, dta, dte, dtu, dtl, dtv, dtA = [small(32) for _ in range(7)]
        aexp, acum = small(16), small(16)
        dend = small(8)
        gms, gmr = small(2), small(2)
        qs, qr = small(32), small(32)
        mx, nb, ps_, pr = small(8), small(8), small(8), small(8)
        os_, orr = small(8), small(8)
        lms, lmv = small(2), small(1)
        bmx, bnm, bsm, brr = [small(2) for _ in range(4)]
        early = g01[:, 0:8, :].rearrange("p k t -> p (k t)")
        cbm = early[:, 0:256].rearrange("p (g t) -> p g t", g=2)
        bT = early[:, 256:512].rearrange("p (g n) -> p g n", g=2)
        wsT = early[:, 512:1024].rearrange("p (g t) -> p g t", g=4)
        wsn = early[:, 1024:1536].rearrange("p (g s) -> p g s", g=4)
        lmp = early[:, 1536:1664]
        dtw = early[:, 1664:1792].rearrange("p (k h) -> p k h", k=KD)
        lam_row = early[:, 1792:2048]

        w_loaded = [sem(f"w_loaded{n}") for n in range(RAW)]
        w_hi, w_lo_dve, w_lo_pool, group_done = sem("w_hi"), sem("w_lo_dve"), sem("w_lo_pool"), sem("group_done")
        taken = dict(act=sem("taken_act"), dve=sem("taken_dve"))
        loads_cleared = sem("loads_cleared")
        const_in, ident_in, x_in, setup = sem("const_in"), sem("ident_in"), sem("x_in"), sem("setup")
        out_in = sem("out_stored")
        STEPS = {}

        def step(name):
            if name not in STEPS:
                STEPS[name] = sem(name)
            return STEPS[name]

        def layer(b, i):
            return i + LAYERS if b == 2 else i

        def norm_count(b, i, which, pair):
            return layer(b, i) * (2 * PAIRS) + (PAIRS * which + pair)

        NG = {1: len(G1), 2: len(G2)}
        BASE = {1: 0, 2: LAYERS * len(G1)}
        NTAKE = {b: {e: sum(1 for g in G if g["taker"] == e and g["closes"]) for e in ("act", "dve")}
                 for b, G in ((1, G1), (2, G2))}
        NLOAD = {b: [len(range(s, NG[b], RAW)) for s in range(RAW)] for b in (1, 2)}

        def count(b, i, k):
            return i * NG[b] + (BASE[b] + k + 1)

        def plain_count(b, i, k):
            return i * NG[b] + (BASE[b] + k)

        def taken_count(b, e, i, g):
            G = G1 if b == 1 else G2
            k = sum(1 for q in G[:g] if q["taker"] == e and q["closes"])
            base = LAYERS * NTAKE[1][e] if b == 2 else 0
            return i * NTAKE[b][e] + (base + k + 1)

        block = ctx.enter_context(nc.Block())

        def group_view(t, slot, g):
            return t[:, slot, 0:g["kt"] * g["cols"]].rearrange("p (k n) -> p k n", k=g["kt"])

        def weight_source(b, i, g):
            kind, n, c = g["kind"], g["n"], g["cols"]
            lay = bass.ds(i, 1)

            def of(name, k0, k1, c0):
                return C[name][lay, k0:k1, c0:c0 + c].rearrange("a (k p) n -> p (a k) n", p=P)
            if kind == "UP":
                return of("ffn_w_up" if b == 1 else "w_up_2", 0, D, (n % 2) * FF + (n // 2) * 256)
            if kind == "DN":
                return of("ffn_w_down" if b == 1 else "w_down_2", (n % 4 // 2) * DNK * P, (n % 4 // 2 + 1) * DNK * P, (n // 4 * 2 + n % 2) * P)
            if b == 1:
                first = dict(GU=0, GV=512, Z=1024, XBC=2048, QK=3600, V=4624, GA=5136, GB=6160, GC=7184)
                if kind in first:
                    return of("w_in", 0, D, first[kind] + 256 * n)
                name = dict(BA="w_branch_a", BB="w_branch_b", BC="w_branch_c", OUT="w_out")[kind]
                return of(name, 0, g["kt"] * P, 256 * n)
            first = dict(PU=0, Q=1024, K=2560, V=4096, GP=5632, GT=6656)
            if kind in first:
                return of("w_in_2", 0, D, first[kind] + 256 * n)
            if kind == "WP":
                return C["w_pool_2"][lay, n, :, :].rearrange("a (k p) n -> p (a k) n", p=P)
            name = dict(WA="w_a_2", WB="w_b_2", OUT="w_o_2")[kind]
            return of(name, 0, g["kt"] * P, 256 * n)

        def bias_loads(sp, i, u):
            sp.wait_ge(step("b2_bias_free"), i * 8 + (u + 1))
            sp.sem_inc(loads_cleared, 1)
            j, qt = u // 2, u % 2
            for g in range(3):
                row = C["bias_table"][4 * g + j, 255 - qt * P:255 - qt * P + P * 510]
                sp.dma_start(b2_bias[:, g, :], row.rearrange("(q f) -> q f", f=510)[:, 0:S]).then_inc(step("b2_bias_in"), 16)

        def gate_t(m):
            return xbc[:, 4 * m:4 * m + 2, :] if m < 3 else xbc[:, 2:7:4, :]

        b2_bias = tmp[:, 0:768].rearrange("p (g k) -> p g k", g=3)
        b2_P = tmp[:, 768:1536]
        b2_PT = tmp[:, 1536:3072].rearrange("p (k q) -> p k q", q=S)

        POOL_K = {8: 4, 4: 2, 2: 1, DNK: 6}

        def low_part(eng, b, i, n, G, on_pool):
            if n >= len(G):
                return
            g = G[n]
            cut = g["kt"] - POOL_K[g["kt"]]
            ks = slice(cut, g["kt"]) if on_pool else slice(0, cut)
            eng.wait_ge(w_hi, plain_count(b, i, n + 1))
            eng.tensor_tensor(group_view(wlo, n % SPL, g)[:, ks, :], group_view(raw, n % RAW, g)[:, ks, :],
                              group_view(whi, n % SPL, g)[:, ks, :].bitcast(f32), ALU.subtract
                              ).then_inc(w_lo_pool if on_pool else w_lo_dve, 1)

        def high_part(act, b, i, n, G):
            if n >= len(G):
                return
            g = G[n]
            slot = n % RAW
            before = LAYERS * NLOAD[1][slot] if b == 2 else 0
            act.wait_ge(w_loaded[slot], i * (16 * NLOAD[b][slot]) + 16 * (before + n // RAW + 1))
            act.wait_ge(group_done, count(b, i, max(n - SPL + 1, 0)))
            act.activation(group_view(whi, n % SPL, g), group_view(raw, n % RAW, g), ACT.Copy).then_inc(w_hi, 1)

        def col(b, key, k):
            t, o = (cols1, COLS1) if b == 1 else (cols2, COLS2)
            return t[:, o[key][0] + k:o[key][0] + k + 1]

        def row(key):
            return rows1[:, ROWS1[key][0]:ROWS1[key][0] + ROWS1[key][1]]

        def bc(ap, dims, axis):
            return ap.unsqueeze(axis).to_broadcast(dims)

        def band(s):
            return xbc[:, 4 * s:4 * s + 4, :].rearrange("p k t -> p (k t)")

        def ypair(buf, val):
            q = 2 * buf + val
            return tmp[:, q * 512:(q + 1) * 512].rearrange("p (k t) -> p k t", t=S)

        BIAS_AT = {}
        SC_AT, TR_AT, PV_AT = {}, {}, {}
        hooks2 = [f"V{n}" for n in range(1, 6)] + [f"{w}{n}" for w in ("GP", "WA", "GT") for n in range(4)]
        for u in range(8):
            SC_AT[hooks2[2 * u]] = u
            TR_AT[hooks2[2 * u + 1]] = u
            at2 = [g["name"] for g in G2]
            BIAS_AT["K0" if u == 0 else at2[at2.index(hooks2[2 * u - 2]) + SPL]] = u
            if u % 2:
                PV_AT[hooks2[min(2 * u + 3, len(hooks2) - 1)]] = u // 2

        @block.sync
        def _(sp):
            sp.dma_start(ident[:, :], C["c_ident"]).then_inc(ident_in, 16)
            for tt in range(TT):
                sp.dma_start(g01[:, 4 * tt:4 * tt + 4, :].rearrange("p k t -> p (k t)"), C["x"][0, tt * P:(tt + 1) * P, :]).then_inc(x_in, 16)
            for dst, name in ((tri, "c_tri"), (amask, "c_amask"), (colsf, "cols_f")):
                sp.dma_start(dst[:, :], C[name]).then_inc(const_in, 16)
            sp.dma_start(rope[:, :, :, :].rearrange("p a b c -> p (a b c)"), C["c_rope"]).then_inc(const_in, 16)
            for b, G in ((1, G1), (2, G2)):
                if b == 2:
                    sp.wait_ge(step("bias_stored"), 16)
                    sp.sem_inc(loads_cleared, 1)
                with sp.Fori(0, LAYERS) as i:
                    sp.wait_ge(step("layer_done"), layer(b, i) + 1)
                    sp.sem_inc(loads_cleared, 1)
                    lay = bass.ds(i, 1)
                    if b == 1:
                        sp.dma_start(cols1[:, :], C["cols_1"][lay, :, :].rearrange("a p c -> p (a c)")).then_inc(step("cols_in1"), 16)
                    else:
                        sp.dma_start(cols2[:, :], C["cols_2"][lay, :, :].rearrange("a p c -> p (a c)")).then_inc(step("par_in2"), 16)
                        for s in range(TT):
                            sp.dma_start(band(s), C["c_band"][s, :, :]).then_inc(step("par_in2"), 16)
                    for n, g in enumerate(G):
                        slot = n % RAW
                        done = max(n - RAW + 1, 0)
                        sp.wait_ge(w_lo_dve, count(b, i, done))
                        sp.wait_ge(w_lo_pool, count(b, i, done))
                        sp.sem_inc(loads_cleared, 1)
                        sp.dma_start(group_view(raw, slot, g), weight_source(b, i, g)).then_inc(w_loaded[slot], 16)
                        if b == 1 and n == 1:
                            sp.wait_ge(step("x_turned"), PAIRS)
                            sp.sem_inc(loads_cleared, 1)
                            sp.dma_start(rows1[:, :], C["rows_1"][lay, :].to_broadcast([P, NR1])).then_inc(step("par_in1"), 16)
                            sp.dma_start(lam_row, C["lam_1"][lay, :].to_broadcast([P, 256])).then_inc(step("par_in1"), 16)
                            sp.dma_start(dtw[:, :, :], C["w_in"][lay, :, 3584:3600].rearrange("a (k p) n -> p (a k) n", p=P)).then_inc(step("par_in1"), 16)
                            sp.dma_start(wsn[:, :, :], C["gm_w_s"][lay, :, :, :].rearrange("a g t s -> t (a g) s")).then_inc(step("par_in1"), 16)
                        if b == 2 and g["name"] in BIAS_AT:
                            bias_loads(sp, i, BIAS_AT[g["name"]])
            for tt in range(TT):
                sp.wait_ge(step(f"out_ready_{tt}"), 1)
                sp.dma_start(out[0, tt * P:(tt + 1) * P, :], g01[:, 4 * tt:4 * tt + 4, :].rearrange("p k t -> p (k t)")).then_inc(out_in, 16)
            sp.wait_ge(out_in, 16 * TT)
            sp.wait_ge(step("bias_stored"), 16)

        @block.gpsimd
        def _(pool):
            nc.gpsimd.memset(ones[:, :], 1.0 / D).then_inc(setup, 1)
            nc.gpsimd.memset(eps, EPS).then_inc(setup, 1)
            pool.sem_inc(w_lo_pool, 1)
            for b, G in ((1, G1), (2, G2)):
                with pool.Fori(0, LAYERS) as i:
                    for n in range(len(G)):
                        low_part(nc.gpsimd, b, i, n, G, True)

        @block.tensor
        def _(pe):
            mm = nc.tensor.matmul

            def proj_waits(b, i, n, G):
                g = G[n]
                pe.wait_ge(w_lo_dve, count(b, i, n + 1))
                pe.wait_ge(w_lo_pool, count(b, i, n + 1))
                if g["opens"]:
                    old = max((q for q in range(n) if G[q]["closes"] and G[q]["bank"] == g["bank"]), default=None)
                    e = "dve" if old is None else G[old]["taker"]
                    pe.wait_ge(taken[e], taken_count(b, e, i, 0 if old is None else old + 1))

            def open_bank(g):
                mm(PJ[:, g["bank"], :], zero[:, 0:1].to_broadcast([P, P]),
                   zero[:, :].unsqueeze(1).to_broadcast([P, 8, P // 2]), start=True, stop=False)

            def products(g, n, t, ks, start, stop):
                hi, lo = group_view(whi, n % SPL, g), group_view(wlo, n % SPL, g)
                a0 = g["tile"]
                half = g["sub"] % 2 if g["kind"] == "DN" else t
                o = PJ[:, g["bank"], half * 256:(half + 1) * 256]
                for k in ks:
                    if g["form"] == "A":
                        wh, wl = hi[:, k, t * P:(t + 1) * P], lo[:, k, t * P:(t + 1) * P]
                        xh, xl = ahi[:, a0 + k, :], alo[:, a0 + k, :]
                        three = ((wh, xh), (wh, xl), (wl, xh))
                    else:
                        xh, xl = ahi[:, a0 + k, t * P:(t + 1) * P], alo[:, a0 + k, t * P:(t + 1) * P]
                        three = ((xh, hi[:, k, :]), (xh, lo[:, k, :]), (xl, hi[:, k, :]))
                    for q, (held, moved) in enumerate(three):
                        last = mm(o, held, moved, start=start and k == ks[0] and q == 0, stop=stop and k == ks[-1] and q == 2)
                return last

            def proj(b, i, n, G):
                g = G[n]
                proj_waits(b, i, n, G)
                if g["kind"] == "DN":
                    if g["opens"]:
                        open_bank(g)
                    last = products(g, n, 0, range(g["kt"]), False, g["closes"])
                else:
                    for t in range(2):
                        last = products(g, n, t, range(g["kt"]), True, True)
                last.then_inc(group_done, 1)

            def proj_two(b, i, n, G, ready, before):
                proj_waits(b, i, n, G)
                open_bank(G[n])
                proj_waits(b, i, n + 1, G)
                open_bank(G[n + 1])
                for p in range(PAIRS):
                    pe.wait_ge(step(ready), before + (p + 1))
                    for q in (n, n + 1):
                        for t in range(2):
                            last = products(G[q], q, t, range(2 * p, 2 * p + 2), False, p == PAIRS - 1 and t == 1)
                        if p == PAIRS - 1:
                            last.then_inc(group_done, 1)

            def mean_pair(b, i, which, p):
                pe.wait_ge(step("sq"), norm_count(b, i, which, p + 1))
                for k in (2 * p, 2 * p + 1):
                    last = mm(pC[:, 0:S], ones[:, :], sq8[:, k, :], start=k == 0, stop=k == KD - 1)
                if p == PAIRS - 1:
                    last.then_inc(step("ms"), 1)

            MEAN_AT = dict(OUT1=(1, 0), OUT2=(1, 1), OUT3=(1, 2), DN5=(2, 0), DN9=(2, 1), DN13=(2, 2))

            def mean_square(b, i, sq, ready, done):
                pe.wait_ge(step(ready), layer(b, i) + 1)
                for k in range(KD):
                    last = mm(pC[:, 0:S], ones[:, :], sq[:, k, :], start=k == 0, stop=k == KD - 1)
                last.then_inc(step(done), 1)

            def dt_proj(i):
                pe.wait_ge(step("par_in1"), i * 64 + 64)
                for c in range(TT):
                    for k in range(KD):
                        last = mm(pC[:, 256 + 16 * c:272 + 16 * c], h32[:, k, c * P:(c + 1) * P], dtw[:, k, :],
                                  start=k == 0, stop=k == KD - 1)
                last.then_inc(step("dt_proj"), 1)

            def scan_open(i, c):
                pe.wait_ge(step("dta_ready"), i + 1)
                pe.wait_ge(step("xbc_ready"), i * 6 + 6)
                if c:
                    pe.wait_ge(step("y_taken"), i * 4 + 2)
                    pe.wait_ge(step("prev_ready"), i * 2 + 2)
                t = slice(c * P, (c + 1) * P)
                mm(pC[:, 0:16], tri[:, :], dtA[:, 16 * c:16 * c + 16], start=True, stop=True)
                for g in range(2):
                    mm(pC[:, 128 + 128 * g:256 + 128 * g], xbc[:, 8 + g, t], xbc[:, 10 + g, t], start=True, stop=True)
                    if c == 0:
                        nc.tensor.transpose(pB[:, 0, g * P:(g + 1) * P], xbc[:, 8 + g, t], ident[:, :])
                for k in range(8):
                    last = nc.tensor.transpose(pA[:, k // 4, (k % 4) * P:(k % 4 + 1) * P], xbc[:, k, t], ident[:, :])
                last.then_inc(step("scan_opened"), 1)

            def scan_rows(i, c, g):
                if (c, g) == (0, 0):
                    pe.wait_ge(step("chunk_ready"), i * 2 + 1)
                else:
                    pe.wait_ge(step("rows_taken"), i * 4 + 2 * c + g)
                for h in range(8):
                    last = mm(pB[:, h // 4, (h % 4) * P:(h % 4 + 1) * P],
                              dtA[:, 16 * c + 8 * g + h:16 * c + 8 * g + h + 1].to_broadcast([P, P]), tri[:, :], start=True, stop=True)
                last.then_inc(step("rows_ready"), 1)

            def scan_state(i, g):
                pe.wait_ge(step("xdtd_ready"), i * 2 + g + 1)
                pe.wait_ge(step("chunk_ready"), i * 2 + 1)
                if g:
                    pe.wait_ge(step("prev_ready"), i * 2 + 1)
                mm(pC[:, :], bT[:, g, :], cdec[:, 0:4, :].rearrange("p h t -> p (h t)"), start=True, stop=True).then_inc(step("state_ready"), 1)

            def scan_out(i, c, g):
                pe.wait_ge(step("dec_ready"), i * 4 + 2 * c + g + 1)
                if c:
                    pe.wait_ge(step("cdec_ready"), i * 2 + g + 1)
                for h in range(8):
                    r = slice((h % 2) * 64, (h % 2) * 64 + 64)
                    o = pA[r, g, (h // 2) * P:(h // 2 + 1) * P]
                    last = mm(o, xdt[:, (8 * g + h) * 64:(8 * g + h + 1) * 64], dec[:, h, :], start=True, stop=c == 0)
                    if c:
                        last = mm(o, prev[:, g, h * 64:(h + 1) * 64], cdec[:, h, :], start=False, stop=True)
                last.then_inc(step("y_ready"), 1)

            def gate_turn(i):
                pe.wait_ge(step("chunk_ready"), i * 2 + 2)
                for g in range(4):
                    last = nc.tensor.transpose(pC[:, g * P:(g + 1) * P], wsn[:, g, :], ident[:, :])
                last.then_inc(step("ws_turned"), 1)

            def gate_mix(i):
                pe.wait_ge(step("wsT_ready"), i + 1)
                pe.wait_ge(step("vn_ready"), i + 1)
                pe.wait_ge(step("y_taken"), i * 4 + 4)
                for n in range(TT):
                    for g in range(4):
                        last = mm(pA[:, n, g * P:(g + 1) * P], vg[:, n, g * P:(g + 1) * P], wsT[:, g, :], start=True, stop=True)
                last.then_inc(step("mixed"), 1)

            def attn_turn(i):
                pe.wait_ge(step("qk_normed"), i + 1)
                pe.wait_ge(step("ya32_ready"), i + 1)
                for j in range(8):
                    for tt in range(TT):
                        o = PS[:, j // 2, (j % 2) * S + tt * P:(j % 2) * S + (tt + 1) * P]
                        last = nc.tensor.transpose(o, qk[:, tt, j * P:(j + 1) * P], ident[:, :])
                last.then_inc(step("qk_turned"), 1)

            def attn_scores(i, qt):
                W = (qt + 1) * P
                pe.wait_ge(step("qkT_ready"), i + 1)
                if qt:
                    pe.wait_ge(step("o_taken"), i * 2 + 1)
                for h in range(H1):
                    for m in range(2):
                        r = slice(m * 64, m * 64 + 64)
                        j = 4 * m + h
                        o = PS[:, j * W // 512, j * W % 512:j * W % 512 + W]
                        last = mm(o, qkT[r, h, qt * P:(qt + 1) * P], qkT[r, 4 + h, 0:W], start=True, stop=True)
                last.then_inc(step("scores"), 1)

            def attn_wturn(i, qt):
                pe.wait_ge(step("w_ready"), i * 2 + qt + 1)
                W = (qt + 1) * P
                pw = prob[:, 0:8 * W].rearrange("p (m h k) -> p m h k", h=H1, m=2)
                for h in range(H1):
                    for kt in range(qt + 1):
                        j = h * (qt + 1) + kt
                        last = nc.tensor.transpose(pB[:, j // 4, (j % 4) * P:(j % 4 + 1) * P], pw[:, 0, h, kt * P:(kt + 1) * P], ident[:, :])
                last.then_inc(step("w_turned"), 1)

            def attn_out(i, qt):
                pe.wait_ge(step("wT_ready"), i * 2 + qt + 1)
                for h in range(H1):
                    for kt in range(qt + 1):
                        last = mm(pA[:, 0, h * P:(h + 1) * P], wT[:, h * (qt + 1) + kt, :], vv[:, kt, h * P:(h + 1) * P],
                                  start=kt == 0, stop=kt == qt)
                last.then_inc(step("o_ready"), 1)

            def attn_oturn(i):
                pe.wait_ge(step("o_normed"), i + 1)
                for h in range(H1):
                    for tt in range(TT):
                        last = nc.tensor.transpose(pA[:, h // 2, (h % 2) * S + tt * P:(h % 2) * S + (tt + 1) * P],
                                                   o32[:, tt, h * P:(h + 1) * P], ident[:, :])
                last.then_inc(step("o_turned"), 1)

            def gated_wait(b, i, g):
                if g["name"] in ("DN0", "DN2"):
                    pe.wait_ge(step("up_free"), layer(b, i) * FP + ((DNK + 1) // 2 if g["name"] == "DN0" else FP))

            def stream(b, i, n, G):
                firsts = {"XBC0": ("h_ready", norm_count(b, i, 0, 0)), "PU0": ("h_ready", norm_count(b, i, 0, 0)),
                          "OUT0": ("mg_ready", layer(b, i) * PAIRS), "UP0": ("h_ready", norm_count(b, i, 1, 0))}
                if G[n]["name"] in firsts:
                    proj_two(b, i, n, G, *firsts[G[n]["name"]])
                elif n == 0 or G[n - 1]["name"] not in firsts:
                    proj(b, i, n, G)

            pe.sem_inc(group_done, 1)
            pe.wait_ge(ident_in, 16)
            pe.wait_ge(x_in, 32)
            for p in range(PAIRS):
                for k in (2 * p, 2 * p + 1):
                    for tt in range(TT):
                        last = nc.tensor.transpose(PS[:, p, (k % 2) * S + tt * P:(k % 2) * S + (tt + 1) * P],
                                                   g01[:, 4 * tt:4 * tt + 4, :].rearrange("p k t -> p (k t)")[:, k * P:(k + 1) * P], ident[:, :])
                last.then_inc(step("x_turned"), 1)
            pe.wait_ge(step("bias_const_in"), 48)
            mm(pC[0:12, :], qkv[0:32, 0:12], qkv[0:32, 512:1024], start=True, stop=True).then_inc(step("bias_product"), 1)
            pe.wait_ge(setup, 3)
            pe.wait_ge(const_in, 64)
            pe.wait_ge(step("bias_row"), 1)
            for p in range(PAIRS - 1):
                mean_pair(1, 0, 0, p)

            with pe.Fori(0, LAYERS) as i:
                mean_pair(1, i, 0, PAIRS - 1)
                after = dict(
                    XBC1=lambda: dt_proj(i),
                    QK0=lambda: scan_open(i, 0), QK1=lambda: scan_rows(i, 0, 0),
                    QK3=lambda: (scan_state(i, 0), scan_out(i, 0, 0), scan_rows(i, 0, 1)),
                    V1=lambda: (scan_state(i, 1), scan_out(i, 0, 1)), Z0=lambda: scan_open(i, 1), Z1=lambda: scan_rows(i, 1, 0),
                    Z3=lambda: (scan_out(i, 1, 0), scan_rows(i, 1, 1)), GV0=lambda: gate_turn(i), GV1=lambda: scan_out(i, 1, 1),
                    GU1=lambda: gate_mix(i), GA0=lambda: mean_square(1, i, sq8, "yb_sq", "yb_ms"),
                    GA2=lambda: attn_turn(i), GA3=lambda: attn_scores(i, 0), GB1=lambda: attn_wturn(i, 0),
                    GB2=lambda: attn_out(i, 0), GB3=lambda: attn_scores(i, 1), GC2=lambda: attn_wturn(i, 1),
                    GC3=lambda: attn_out(i, 1), BA3=lambda: attn_oturn(i))
                before = dict(BA0="ya_ready", BB0="yb_ready", BC0="yc_ready")
                for n, g in enumerate(G1):
                    if g["name"] == "UP0":
                        mean_pair(1, i, 1, PAIRS - 1)
                    if g["name"] in before:
                        pe.wait_ge(step(before[g["name"]]), i + 1)
                    gated_wait(1, i, g)
                    stream(1, i, n, G1)
                    if g["name"] in after:
                        after[g["name"]]()
                    if g["name"] in MEAN_AT:
                        mean_pair(1, i, *MEAN_AT[g["name"]])

            def pool_mix(i):
                pe.wait_ge(step("pu_ready"), i + 1)
                pe.wait_ge(step("par_in2"), i * 48 + 48)
                for k in range(KD):
                    for s in range(TT):
                        last = mm(PS[:, k // 2, (k % 2) * S:(k % 2 + 1) * S], uview[:, s, k * P:(k + 1) * P],
                                  band(s)[:, (k // 2) * S:(k // 2 + 1) * S], start=s == 0, stop=s == TT - 1)
                last.then_inc(step("pooled"), 1)

            uview = ug[:, :, :].rearrange("p k t -> p (k t)").rearrange("p (a c) -> p a c", a=TT)

            def b2_scores(i, u):
                j, qt = u // 2, u % 2
                if u == 0:
                    pe.wait_ge(step("qk2_ready"), i + 1)
                    pe.wait_ge(step("pd_ready"), i + 1)
                else:
                    pe.wait_ge(step("b2_PT_ready"), i * 8 + u)
                px = PS[:, 2 * (u % 2):2 * (u % 2) + 2, :]
                for g in range(3):
                    last = mm(px[:, g // 2, (g % 2) * S:(g % 2 + 1) * S], xbc[:, 4 * g + j, qt * P:(qt + 1) * P],
                              g01[:, 4 * g + j, :], start=True, stop=True)
                last.then_inc(step("b2_scores"), 1)

            def b2_turn(i, u):
                pe.wait_ge(step("b2_P_ready"), i * 8 + u + 1)
                px = PS[:, 2 * (u % 2):2 * (u % 2) + 2, :]
                for k in range(6):
                    last = nc.tensor.transpose(px[:, k // 4, (k % 4) * P:(k % 4 + 1) * P], b2_P[:, k * P:(k + 1) * P], ident[:, :])
                last.then_inc(step("b2_turned"), 1)

            def b2_values(i, j):
                pe.wait_ge(step("b2_PT_ready"), i * 8 + 2 * j + 2)
                if j:
                    pe.wait_ge(step("at_lo"), i * 4 + j)
                else:
                    pe.wait_ge(step("v2_ready"), i + 1)
                v2 = qkv[:, :].rearrange("p (a c) -> p a c", a=TT)
                for g in range(3):
                    for kt in range(TT):
                        last = mm(pC[:, 0:S], v2[:, kt, (4 * g + j) * P:(4 * g + j + 1) * P], b2_PT[:, 2 * g + kt, :],
                                  start=(g, kt) == (0, 0), stop=(g, kt) == (2, 1))
                last.then_inc(step("b2_out"), 1)

            with pe.Fori(0, LAYERS) as i:
                mean_pair(2, i, 0, PAIRS - 1)
                before = dict(WP0="pd_ready", WA0="po_ready", WB0="at_ready")
                for n, g in enumerate(G2):
                    if g["name"] == "UP0":
                        mean_pair(2, i, 1, PAIRS - 1)
                    if g["name"] in before:
                        pe.wait_ge(step(before[g["name"]]), i + 1)
                    gated_wait(2, i, g)
                    stream(2, i, n, G2)
                    if g["name"] in MEAN_AT:
                        mean_pair(2, i, *MEAN_AT[g["name"]])
                    if g["name"] == "Q0":
                        pool_mix(i)
                    if g["name"] in PV_AT:
                        b2_values(i, PV_AT[g["name"]])
                    if g["name"] in SC_AT:
                        b2_scores(i, SC_AT[g["name"]])
                    if g["name"] in TR_AT:
                        b2_turn(i, TR_AT[g["name"]])

            mean_pair(2, LAYERS, 0, PAIRS - 1)
            for p in range(PAIRS):
                pe.wait_ge(step("f_normed"), p + 1)
                for tt in range(TT):
                    for k in (2 * p, 2 * p + 1):
                        last = nc.tensor.transpose(PS[:, 2 * tt + k // 4, (k % 4) * P:(k % 4 + 1) * P], h32[:, k, tt * P:(tt + 1) * P], ident[:, :])
                    if p == PAIRS - 1:
                        last.then_inc(step("out_turned"), 1)

        @block.scalar
        def _(act):
            A = nc.scalar.activation

            def squares(b, i, ready, done, src):
                act.wait_ge(step(ready), layer(b, i) + 1)
                A(sq8, src, ACT.Square).then_inc(step(done), 1)

            def pair_square(b, i, which, p):
                act.wait_ge(step("x_pair"), norm_count(b, i, which, p + 1))
                t = slice(2 * p, 2 * p + 2)
                A(sq8[:, t, :], x[:, t, :], ACT.Square).then_inc(step("sq"), 1)

            def residual_square(b, i, g):
                if g["name"].startswith("OUT") or g["kind"] == "DN" and g["closes"]:
                    which, p = (1, g["n"]) if g["kind"] == "OUT" else (2, g["n"] // 4)
                    pair_square(b, i, which, p)

            def root(ms, value, done):
                act.wait_ge(step(ms), value)
                A(rstd[:, :], pC[:, 0:S], ACT.Sqrt, bias=eps).then_inc(step(done), 1)

            def norm_root(b, i, which):
                root("ms", layer(b, i) * 2 + (which + 1), "root")

            def merged_high(b, i, m, merged):
                t = slice(A_MG + 2 * m, A_MG + 2 * m + 2)
                split_high(i, "mg32_ready", layer(b, i) * PAIRS + (m + 1), t, merged[:, 2 * m:2 * m + 2, :], "mg_hi")

            def small_root(i, sums, tile, n, done):
                act.wait_ge(step(sums), i + 1)
                A(tile, tile, ACT.Sqrt, scale=1.0 / n, bias=eps).then_inc(step(done), 1)

            def split_high(i, ready, value, tiles, src, done):
                act.wait_ge(step(ready), value)
                A(ahi[:, tiles, :], src, ACT.Copy).then_inc(step(done), 1)

            def norm_high(b, i, which, a0):
                for p in range(PAIRS):
                    split_high(i, "h32_ready", norm_count(b, i, which, p + 1), slice(a0 + 2 * p, a0 + 2 * p + 2),
                               h32[:, 2 * p:2 * p + 2, :], "h_hi")

            def bank(g):
                return PJ[:, g["bank"], :]

            def arrived(b, i, n):
                act.wait_ge(group_done, count(b, i, n + 1))

            def conv_open(b, i, g, wkey, bkey, taps, tap, tiles, dst, done):
                for t in range(2):
                    last = A(dst[t], bank(g)[:, t * S:(t + 1) * S], ACT.Identity, bias=col(b, bkey, tiles[t]),
                             scale=col(b, wkey, tiles[t] * taps + tap))
                last.then_inc(step(done), 1)

            act.sem_inc(taken["act"], 1)
            act.dma_start(qkv[0:32, 0:12], C["rel_bias_2"]).then_inc(step("bias_const_in"), 16)
            act.dma_start(qkv[0:32, 512:1024], C["c_onehot"]).then_inc(step("bias_const_in"), 16)
            act.dma_start(qkv[0:12, 1024:1536], C["c_offmask"]).then_inc(step("bias_const_in"), 16)
            act.wait_ge(ident_in, 16)
            A(zero[:, :], ident[:, 0:P // 2], ACT.Copy, scale=0.0).then_inc(setup, 1)
            for p in range(PAIRS):
                pair_square(1, 0, 0, p)
            act.wait_ge(step("bias_row"), 1)
            act.dma_start(C["bias_table"].rearrange("h (c o) -> h c o", o=511),
                          qkv[0:12, 1536:2047].unsqueeze(1).to_broadcast([12, 129, 511])).then_inc(step("bias_stored"), 16)
            with act.Fori(0, LAYERS) as i:
                high_part(act, 1, i, 0, G1)
                norm_root(1, i, 0)
                high_part(act, 1, i, 1, G1)
                norm_high(1, i, 0, A_H)
                high_part(act, 1, i, 2, G1)

                def dt_exp():
                    act.wait_ge(step("dt_abs"), i + 1)
                    A(dte, dta, ACT.Exp, scale=-1.0).then_inc(step("dt_exp"), 1)
                    A(aexp, row("alog"), ACT.Exp).then_inc(step("a_exp"), 1)

                def dt_ln():
                    act.wait_ge(step("dt_one"), i + 1)
                    A(dtl, dtu, ACT.Ln).then_inc(step("dt_ln"), 1)

                def xbc_silu(n):
                    act.wait_ge(step("xbc_conv"), i * 6 + n + 1)
                    v = xbc[:, 2 * n:2 * n + 2, :]
                    A(v, v, ACT.Silu).then_inc(step("xbc_ready"), 1)

                def rows_exp(c, g):
                    act.wait_ge(step("seg_ready"), i * 4 + 2 * c + g + 1)
                    A(dec, dec, ACT.Exp).then_inc(step("dec_exp"), 1)
                    if c == 0:
                        A(dend, dend, ACT.Exp).then_inc(step("dend_exp"), 1)
                    else:
                        if g:
                            act.wait_ge(step("y_ready"), i * 4 + 3)
                        else:
                            act.wait_ge(step("state_ready"), i * 2 + 2)
                        A(cdec, pB.rearrange("p a (h t) -> p (a h) t", t=P), ACT.Exp).then_inc(step("cdec_exp"), 1)

                def gm_square():
                    act.wait_ge(step("vg_ready"), i + 1)
                    for tt in range(TT):
                        A(wsT[:, :, :].rearrange("p g t -> p (g t)"), vg[:, tt, :], ACT.Square, accum_out=gms[:, tt:tt + 1])
                        if tt == 0:
                            act.drain()
                    act.drain()
                    A(gms, gms, ACT.Sqrt, scale=1.0 / 512, bias=eps).then_inc(step("gm_root"), 1)

                def lam_exp():
                    act.wait_ge(step("lam_sums"), i + 1)
                    A(lms, lms, ACT.Exp).then_inc(step("lam_exp"), 1)

                def yb_square():
                    squares(1, i, "yz_ready", "yb_sq", xbc[:, 0:8, :])

                def qk_square():
                    act.wait_ge(step("y_ready"), i * 4 + 4)
                    act.wait_ge(step("qk_in"), i + 1)
                    A(prob, qkv[:, 0:2048], ACT.Square).then_inc(step("qk_sq"), 1)

                def qk_copy():
                    act.wait_ge(step("qk_turned"), i + 1)
                    A(qkT, PS[:, 0:4, :].rearrange("p a (j t) -> p (a j) t", t=S), ACT.Copy).then_inc(step("qkT_ready"), 1)

                def attn_exp(qt):
                    W = (qt + 1) * P
                    act.wait_ge(step("max_ready"), i * 2 + qt + 1)
                    for j in range(8):
                        v = prob[:, j * W:(j + 1) * W]
                        last = A(v, v, ACT.Exp, bias=nb[:, j:j + 1], scale=0.125, accum_out=ps_[:, j:j + 1])
                    last.then_inc(step("attn_exp"), 1)

                def o_square():
                    act.wait_ge(step("o_taken"), i * 2 + 2)
                    A(prob[:, 0:1024], qkv[:, 0:1024], ACT.Square).then_inc(step("o_sq"), 1)

                def yc_high():
                    act.wait_ge(step("o_turned"), i + 1)
                    A(ahi[:, A_YC:A_YC + 4, :], pA.rearrange("p a (j t) -> p (a j) t", t=S), ACT.Copy).then_inc(step("yc_hi"), 1)

                early = dict(GA2=qk_copy)
                after = dict(
                    XBC1=lambda: xbc_silu(0), XBC2=lambda: (xbc_silu(1), dt_exp()), XBC3=lambda: (xbc_silu(2), dt_ln()),
                    XBC4=lambda: xbc_silu(3), XBC5=lambda: (xbc_silu(4), xbc_silu(5)),
                    QK1=lambda: rows_exp(0, 0), QK2=lam_exp, QK3=lambda: rows_exp(0, 1),
                    Z1=lambda: rows_exp(1, 0), Z3=lambda: rows_exp(1, 1), GV1=gm_square, GU0=qk_square,
                    GU1=lambda: (small_root(i, "qk_sums", qs, 64, "qk_root"), yb_square()),
                    GA0=lambda: (split_high(i, "ya32_ready", i + 1, slice(A_YA, A_YA + 4), uu, "ya_hi"), root("yb_ms", i + 1, "yb_root")),
                    GA2=lambda: split_high(i, "yb32_ready", i + 1, slice(A_YB, A_YB + 8), xbc[:, 0:8, :], "yb_hi"),
                    GA3=lambda: attn_exp(0), GB3=lambda: attn_exp(1), GC3=o_square,
                    BA0=lambda: small_root(i, "o_sums", os_, P, "o_root"), BA3=yc_high)

                def take(n, g):
                    kind, m = g["kind"], g["n"]
                    if g["taker"] == "act" or kind in ("XBC", "UP"):
                        arrived(1, i, n)
                    pair = bank(g).rearrange("p (k t) -> p k t", t=S)
                    if kind == "XBC":
                        conv_open(1, i, g, "cw", "cb", 4, 3, (2 * m, 2 * m + 1), (xbc[:, 2 * m, :], xbc[:, 2 * m + 1, :]), "xbc_open")
                    elif kind == "QK":
                        if m == 0:
                            act.wait_ge(step("bias_stored"), 16)
                        last = A(qk[:, :, 256 * m:256 * m + 256], pair, ACT.Copy)
                        last.then_inc(taken["act"], 1)
                        if m == 3:
                            act.drain().then_inc(step("qk_in"), 1)
                    elif kind == "V":
                        A(vv[:, :, 256 * m:256 * m + 256], pair, ACT.Copy).then_inc(taken["act"], 1)
                        if m == 1:
                            act.drain().then_inc(step("v_in"), 1)
                    elif kind == "GV":
                        A(vg[:, :, 256 * m:256 * m + 256], pair, ACT.Gelu_apprx_tanh).then_inc(taken["act"], 1)
                        if m == 1:
                            act.drain().then_inc(step("vg_ready"), 1)
                    elif kind == "GU":
                        A(uu[:, 2 * m:2 * m + 2, :], pair, ACT.Gelu_apprx_tanh).then_inc(taken["act"], 1)
                        if m == 1:
                            act.drain().then_inc(step("u_ready"), 1)
                    elif kind == "Z":
                        A(SZ[:, 2 * m:2 * m + 2, :], pair, ACT.Silu).then_inc(taken["act"], 1)
                        if m == 3:
                            act.drain().then_inc(step("z_ready"), 1)
                    elif kind in ("GA", "GB", "GC"):
                        if kind == "GB" and m == 0:
                            act.wait_ge(step("ya_ready"), i + 1)
                        if kind == "GC" and m == 0:
                            act.wait_ge(step("yb_ready"), i + 1)
                        if kind == "GA" and m == 0:
                            act.wait_ge(step("mixed"), i + 1)
                        reg = dict(GA=G0, GB=ug[:, :, :], GC=SZ)[kind]
                        A(reg[:, 2 * m:2 * m + 2, :], pair, ACT.Sigmoid).then_inc(taken["act"], 1)
                    elif kind == "UP":
                        up_open(1, i, g)

                def up_open(b, i, g):
                    m, val = g["n"] // 2, g["n"] % 2
                    if g["n"] >= 4:
                        act.wait_ge(step("up_free"), layer(b, i) * FP + m - 1)
                    buf = ypair(m % 2, val)
                    t0 = 2 * m + val * FT
                    conv_open(b, i, g, "fw", "fb", 3, 2 if b == 1 else 1, (t0, t0 + 1), (buf[:, 0, :], buf[:, 1, :]), f"up_open{b}")

                def up_act(b, i, m, func):
                    act.wait_ge(step("up_conv"), layer(b, i) * FP + m + 1)
                    v = ypair(m % 2, 0)
                    A(v, v, func).then_inc(step("up_act"), 1)

                def gated_high(b, i, m):
                    split_high(i, "gated32", layer(b, i) * FP + m + 1, slice(A_G + 2 * m, A_G + 2 * m + 2), ypair(m % 2, 0), "gated_hi")

                for n, g in enumerate(G1):
                    if g["name"] == "UP0":
                        norm_root(1, i, 1)
                        norm_high(1, i, 1, A_H2)
                        high_part(act, 1, i, n - 1 + SPL, G1)
                    take(n, g)
                    if g["name"] in early:
                        early[g["name"]]()
                    if g["kind"] == "BC":
                        merged_high(1, i, g["n"], G0)
                    if g["name"] != "OUT3":
                        high_part(act, 1, i, n + SPL, G1)
                    residual_square(1, i, g)
                    if g["name"] in after:
                        after[g["name"]]()
                    if g["kind"] == "UP":
                        if g["n"] % 2 == 1:
                            up_act(1, i, g["n"] // 2, ACT.Silu)
                        elif g["n"] >= 2:
                            gated_high(1, i, g["n"] // 2 - 1)
                        if g["n"] == 2 * FP - 1:
                            gated_high(1, i, FP - 1)

            with act.Fori(0, LAYERS) as i:
                high_part(act, 2, i, 0, G2)
                norm_root(2, i, 0)
                high_part(act, 2, i, 1, G2)
                norm_high(2, i, 0, A_H)
                high_part(act, 2, i, 2, G2)
                uview = ug[:, :, :].rearrange("p k t -> p (k t)").rearrange("p (a c) -> p a c", a=TT)
                v2 = qkv[:, :].rearrange("p (a c) -> p a c", a=TT)

                def b2_exp(u):
                    act.wait_ge(step("b2_max"), i * 8 + u + 1)
                    A(b2_P, b2_P, ACT.Exp, bias=bnm[:, 0:1], accum_out=bsm[:, 0:1]).then_inc(step("b2_exp"), 1)

                def b2_PT_copy(u):
                    act.wait_ge(step("b2_turned"), i * 8 + u + 1)
                    if u >= 2 and u % 2 == 0:
                        act.wait_ge(step("b2_out"), i * 4 + u // 2)
                    px = PS[:, 2 * (u % 2):2 * (u % 2) + 2, :].rearrange("p a c -> p (a c)")[:, 0:768]
                    A(b2_PT[:, :, (u % 2) * P:(u % 2 + 1) * P], px.rearrange("p (k q) -> p k q", q=P), ACT.Copy).then_inc(step("b2_PT_ready"), 1)

                def at_high(j):
                    act.wait_ge(step("b2_out"), i * 4 + j + 1)
                    A(ahi[:, A_AT + j, :], pC[:, 0:S], ACT.Copy).then_inc(step("at_hi"), 1)

                def pd_high():
                    act.wait_ge(step("pooled"), i + 1)
                    A(ahi[:, A_PD:A_PD + 8, :], PS[:, 0:4, :].rearrange("p a (k t) -> p (a k) t", t=S), ACT.Copy).then_inc(step("pd_hi"), 1)

                def take2(n, g):
                    kind, m = g["kind"], g["n"]
                    if g["taker"] == "act" or kind in ("WP", "UP"):
                        arrived(2, i, n)
                    pair = bank(g).rearrange("p (k t) -> p k t", t=S)
                    if kind == "PU":
                        A(uview[:, :, 256 * m:256 * m + 256], pair, ACT.Copy).then_inc(taken["act"], 1)
                        if m == 3:
                            act.drain().then_inc(step("pu_ready"), 1)
                    elif kind == "Q":
                        if m == 0:
                            act.wait_ge(step("pooled"), i + 1)
                        A(xbc[:, 2 * m:2 * m + 2, :], pair, ACT.Copy).then_inc(taken["act"], 1)
                    elif kind == "K":
                        A(g01[:, 2 * m:2 * m + 2, :], pair, ACT.Copy).then_inc(taken["act"], 1)
                        if m == 5:
                            act.drain().then_inc(step("qk2_ready"), 1)
                    elif kind == "V":
                        A(v2[:, :, 256 * m:256 * m + 256], pair, ACT.Copy).then_inc(taken["act"], 1)
                        if m == 5:
                            act.drain().then_inc(step("v2_ready"), 1)
                    elif kind in ("GP", "GT"):
                        if kind == "GT" and m in (0, 3):
                            act.wait_ge(step("b2_scores"), i * 8 + (6 if m else 4))
                        A(gate_t(m) if kind == "GT" else ug[:, 2 * m:2 * m + 2, :], pair, ACT.Sigmoid).then_inc(taken["act"], 1)
                    elif kind == "WP":
                        for t in range(2):
                            last = A(ahi[:, A_PO + 2 * m + t, :], pair[:, t, :], ACT.Copy, scale=col(2, "ps", 2 * m + t))
                        last.then_inc(step("po_hi"), 1)
                    elif kind == "UP" and m % 2 == 0:
                        up_open(2, i, g)

                for n, g in enumerate(G2):
                    if g["name"] == "UP0":
                        norm_root(2, i, 1)
                        norm_high(2, i, 1, A_H2)
                        high_part(act, 2, i, n - 1 + SPL, G2)
                    take2(n, g)
                    if g["name"] in PV_AT:
                        at_high(PV_AT[g["name"]])
                    if g["name"] in TR_AT:
                        b2_PT_copy(TR_AT[g["name"]])
                    if g["kind"] == "WB":
                        merged_high(2, i, g["n"], ug)
                    if g["name"] != "OUT3":
                        high_part(act, 2, i, n + SPL, G2)
                    residual_square(2, i, g)
                    if g["name"] == "Q0":
                        pd_high()
                    if g["name"] in SC_AT:
                        b2_exp(SC_AT[g["name"]])
                    if g["kind"] == "UP":
                        if g["n"] % 2 == 0:
                            up_act(2, i, g["n"] // 2, ACT.Gelu_apprx_tanh)
                        else:
                            gated_high(2, i, g["n"] // 2)
            norm_root(2, LAYERS, 0)
            act.wait_ge(step("out_turned"), 2)
            A(g01[:, 4:8, :].rearrange("p k t -> p (k t)"), pB.rearrange("p a c -> p (a c)"), ACT.Copy).then_inc(step("out_ready_1"), 1)

        @block.vector
        def _(dve):
            V = nc.vector
            TTo = V.tensor_tensor
            STT = V.scalar_tensor_tensor

            def ordered():
                dve.drain()

            def rstd_of(root, value):
                dve.wait_ge(step(root), value)
                V.reciprocal(rstd[:, :], rstd[:, :])
                ordered()

            def norm(b, i, which, gain, a0, between=None):
                rstd_of("root", layer(b, i) * 2 + (which + 1))

                def scaled(p):
                    for k in (2 * p, 2 * p + 1):
                        last = STT(h32[:, k, :], x[:, k, :], col(b, gain, k), rstd[:, :], ALU.mult, ALU.mult)
                    last.then_inc(step("h32_ready"), 1)

                def low(p):
                    t = slice(a0 + 2 * p, a0 + 2 * p + 2)
                    split_low("h_hi", norm_count(b, i, which, p + 1), t, h32[:, 2 * p:2 * p + 2, :], "h_ready")

                scaled(0)
                scaled(1)
                if between:
                    between()
                for p in range(PAIRS):
                    low(p)
                    if p + 2 < PAIRS:
                        scaled(p + 2)

            def split_low(hi, value, tiles, src, done):
                dve.wait_ge(step(hi), value)
                TTo(alo[:, tiles, :], src, ahi[:, tiles, :].bitcast(f32), ALU.subtract).then_inc(step(done), 1)

            def bank(g):
                return PJ[:, g["bank"], :]

            def arrived(b, i, n):
                dve.wait_ge(group_done, count(b, i, n + 1))

            def conv_taps(b, i, g, wkey, taps, shifts, tiles, dst):
                for tap, sh in shifts:
                    for t in range(2):
                        src = bank(g)[:, t * S:(t + 1) * S]
                        o, s = (slice(sh, S), slice(0, S - sh)) if sh > 0 else (slice(0, S + sh), slice(-sh, S))
                        last = STT(dst[t][:, o], src[:, s], col(b, wkey, tiles[t] * taps + tap), dst[t][:, o], ALU.mult, ALU.add)
                    if (tap, sh) != shifts[-1]:
                        ordered()
                return last

            def params_used():
                dve.drain().then_inc(step("layer_done"), 1)

            def merged_low(b, i, m, merged):
                for q in ((m - 1,) if m < PAIRS - 1 else (m - 1, m)):
                    if q >= 0:
                        split_low("mg_hi", layer(b, i) * PAIRS + (q + 1), slice(A_MG + 2 * q, A_MG + 2 * q + 2),
                                  merged[:, 2 * q:2 * q + 2, :], "mg_ready")

            dve.sem_inc(taken["dve"], 1)
            dve.sem_inc(w_lo_dve, 1)
            dve.sem_inc(step("b2_bias_free"), 1)
            dve.sem_inc(step("layer_done"), 1)
            for p in range(PAIRS):
                dve.wait_ge(step("x_turned"), p + 1)
                V.tensor_copy(x[:, 2 * p:2 * p + 2, :], PS[:, p, :].rearrange("p (k t) -> p k t", t=S)).then_inc(step("x_pair"), 1)
            dve.wait_ge(step("bias_product"), 1)
            TTo(qkv[0:12, 1536:2048], pC[0:12, :], qkv[0:12, 1024:1536], ALU.add).then_inc(step("bias_row"), 1)

            with dve.Fori(0, LAYERS) as i:
                low_part(V, 1, i, 0, G1, False)
                dve.wait_ge(step("cols_in1"), i * 16 + 16)
                norm(1, i, 0, "norm1", A_H, lambda: low_part(V, 1, i, 1, G1, False))
                low_part(V, 1, i, 2, G1, False)

                def dt_abs():
                    dve.wait_ge(step("dt_proj"), i + 1)
                    dve.wait_ge(step("par_in1"), i * 64 + 64)
                    TTo(dtx.rearrange("p (c h) -> p c h", c=TT), pC[:, 256:288].rearrange("p (c h) -> p c h", c=TT),
                        bc(row("dtb"), [P, TT, 16], 1), ALU.add)
                    ordered()
                    STT(dta, dtx, -1.0, dtx, ALU.mult, ALU.max).then_inc(step("dt_abs"), 1)

                def dt_one():
                    dve.wait_ge(step("dt_exp"), i + 1)
                    V.tensor_scalar(dtu, dte, 1.0, None, ALU.add).then_inc(step("dt_one"), 1)

                def dt_finish():
                    dve.wait_ge(step("dt_ln"), i + 1)
                    STT(dtv, dtu, -1.0, dte, ALU.add, ALU.subtract)
                    STT(dtx, dtx, 0.0, dtl, ALU.max, ALU.add)
                    V.reciprocal(dta, dtu)
                    ordered()
                    TTo(dtv, dtv, dta, ALU.mult)
                    ordered()
                    TTo(dtv, dtx, dtv, ALU.subtract)
                    ordered()
                    dve.wait_ge(step("a_exp"), i + 1)
                    STT(dtA.rearrange("p (c h) -> p c h", c=TT), dtv.rearrange("p (c h) -> p c h", c=TT), -1.0,
                        bc(aexp, [P, TT, 16], 1), ALU.mult, ALU.mult).then_inc(step("dta_ready"), 1)

                def lam_sums():
                    lv = lam_row.rearrange("p (a b d) -> p a b d", a=2, b=2)
                    TTo(lmp.rearrange("p (a d) -> p a d", a=2), lv[:, :, 0, :], lv[:, :, 1, :], ALU.mult)
                    ordered()
                    V.tensor_reduce(lms, lmp.rearrange("p (a d) -> p a d", a=2), AX.X, ALU.add).then_inc(step("lam_sums"), 1)

                def lam_value():
                    dve.wait_ge(step("lam_exp"), i + 1)
                    TTo(lmv, lms[:, 0:1], lms[:, 1:2], ALU.subtract)
                    ordered()
                    TTo(lmv, lmv, row("li")[:, 0:1], ALU.add)

                def chunk_open(c):
                    dve.wait_ge(step("scan_opened"), i * 2 + c + 1)
                    V.tensor_copy(acum, pC[:, 0:16])
                    for g in range(2):
                        TTo(cbm[:, g, :], pC[:, 128 + 128 * g:256 + 128 * g], tri[:, :], ALU.mult)
                    if c == 0:
                        V.tensor_copy(bT[:, :, :], pB[:, 0, 0:256].rearrange("p (g n) -> p g n", g=2))
                    else:
                        pass
                    TTo(xdt.rearrange("p (h q) -> p h q", q=64), pA.rearrange("p a (h q) -> p (a h) q", q=64),
                        bc(dtv[:, 16 * c:16 * c + 16], [P, 16, 64], 2), ALU.mult).then_inc(step("chunk_ready"), 1)

                def seg(c, g):
                    dve.wait_ge(step("rows_ready"), i * 4 + 2 * c + g + 1)
                    if (c, g) != (0, 0):
                        dve.wait_ge(step("y_ready"), i * 4 + 2 * c + g)
                    rows = pB.rearrange("p a (h t) -> p (a h) t", t=P)
                    TTo(dec, rows, bc(acum[:, 8 * g:8 * g + 8], [P, 8, P], 2), ALU.subtract)
                    if c == 0:
                        TTo(dend, rows[:, :, P - 1], acum[:, 8 * g:8 * g + 8], ALU.subtract)
                    ordered()
                    V.tensor_scalar(dec, dec, 0.0, None, ALU.min).then_inc(step("seg_ready"), 1)

                def dec_mul(c, g):
                    dve.wait_ge(step("dec_exp"), i * 4 + 2 * c + g + 1)
                    last = TTo(dec, dec, bc(cbm[:, g, :], [P, 8, P], 1), ALU.mult)
                    last.then_inc(step("dec_ready"), 1)
                    if c == 0:
                        dve.wait_ge(step("dend_exp"), i * 2 + g + 1)
                        if g:
                            dve.wait_ge(step("state_ready"), i * 2 + 1)
                        TTo(cdec[:, 0:4, :].rearrange("p h t -> p (h t)").rearrange("p (h q) -> p h q", q=64),
                            xdt[:, 512 * g:512 * g + 512].rearrange("p (h q) -> p h q", q=64),
                            bc(dend, [P, 8, 64], 2), ALU.mult).then_inc(step("xdtd_ready"), 1)
                    else:
                        dve.wait_ge(step("cdec_exp"), i * 2 + g + 1)
                        TTo(cdec, cdec, bc(xbc[:, 10 + g, P:2 * P], [P, 8, P], 1), ALU.mult).then_inc(step("cdec_ready"), 1)
                    rows_release()

                def rows_release():
                    ordered()
                    V.tensor_copy(gmr[:, 0:1], acum[:, 0:1]).then_inc(step("rows_taken"), 1)

                def state_copy(g):
                    dve.wait_ge(step("state_ready"), i * 2 + g + 1)
                    V.tensor_copy(prev[:, g, :], pC[:, :]).then_inc(step("prev_ready"), 1)

                def y_take(c, g):
                    dve.wait_ge(step("y_ready"), i * 4 + 2 * c + g + 1)
                    for k in range(4):
                        v = xbc[:, 4 * g + k, c * P:(c + 1) * P]
                        last = STT(v, v, col(1, "sd", 4 * g + k), pA[:, g, k * P:(k + 1) * P], ALU.mult, ALU.add)
                    last.then_inc(step("y_taken"), 1)

                def gm_norm():
                    dve.wait_ge(step("gm_root"), i + 1)
                    V.reciprocal(gmr, gms)
                    ordered()
                    for tt in range(TT):
                        last = STT(vg[:, tt, :], vg[:, tt, :], gmr[:, tt:tt + 1], row("gvg"), ALU.mult, ALU.mult)
                    last.then_inc(step("vn_ready"), 1)
                    dve.wait_ge(step("ws_turned"), i + 1)
                    TTo(wsT[:, :, :], pC.rearrange("p (g t) -> p g t", g=4), bc(tri[:, :], [P, 4, P], 1), ALU.mult).then_inc(step("wsT_ready"), 1)

                def gm_out():
                    dve.wait_ge(step("mixed"), i + 1)
                    dve.wait_ge(step("u_ready"), i + 1)
                    t512 = vg
                    for n in range(TT):
                        TTo(t512[:, n, :], pA[:, n, :], row("gb"), ALU.add)
                    ordered()
                    for n in range(TT):
                        v = uu[:, :, n * P:(n + 1) * P]
                        last = TTo(v, v, t512[:, n, :].rearrange("p (g t) -> p g t", g=4), ALU.mult)
                    last.then_inc(step("ya32_ready"), 1)

                def yz():
                    dve.wait_ge(step("z_ready"), i + 1)
                    TTo(xbc[:, 0:8, :], xbc[:, 0:8, :], SZ, ALU.mult).then_inc(step("yz_ready"), 1)

                def yb_norm():
                    rstd_of("yb_root", i + 1)
                    for k in range(KD):
                        last = STT(xbc[:, k, :], xbc[:, k, :], col(1, "sg", k), rstd[:, :], ALU.mult, ALU.mult)
                    last.then_inc(step("yb32_ready"), 1)

                def qk_sums():
                    dve.wait_ge(step("qk_sq"), i + 1)
                    V.tensor_reduce(qs, prob.rearrange("p (j d) -> p j d", d=64), AX.X, ALU.add).then_inc(step("qk_sums"), 1)

                def qk_norm():
                    v = qk.rearrange("p a (j d) -> p (a j) d", d=64)
                    dve.wait_ge(step("qk_root"), i + 1)
                    V.reciprocal(qr, qs)
                    ordered()
                    TTo(v, v, bc(qr, [P, 32, 64], 2), ALU.mult)
                    ordered()
                    for tt in range(TT):
                        for m, key in ((0, "qg"), (1, "kg")):
                            w = qk[:, tt, 512 * m:512 * m + 512].rearrange("p (j d) -> p j d", d=64)
                            TTo(w, w, bc(row(key), [P, 8, 64], 1), ALU.mult)

                def qk_rope():
                    ordered()
                    v = qk.rearrange("p a (j d) -> p (a j) d", d=64)
                    r4 = [prob[:, 256 * q:256 * q + 256].rearrange("p (j d) -> p j d", d=8) for q in range(4)]
                    for tt in range(TT):
                        w = qk[:, tt, :].rearrange("p (j d) -> p j d", d=64)
                        t1, t2 = w[:, :, 0:8], w[:, :, 8:16]
                        cs, sn = bc(rope[:, tt, 0, :], [P, 16, 8], 1), bc(rope[:, tt, 1, :], [P, 16, 8], 1)
                        z = slice(16 * tt, 16 * tt + 16)
                        TTo(r4[0][:, z, :], t1, cs, ALU.mult)
                        TTo(r4[1][:, z, :], t2, sn, ALU.mult)
                        TTo(r4[2][:, z, :], t2, cs, ALU.mult)
                        TTo(r4[3][:, z, :], t1, sn, ALU.mult)
                    ordered()
                    TTo(v[:, :, 0:8], r4[0], r4[1], ALU.subtract)
                    TTo(v[:, :, 8:16], r4[2], r4[3], ALU.add).then_inc(step("qk_normed"), 1)

                def attn_max(qt):
                    W = (qt + 1) * P
                    dve.wait_ge(step("scores"), i * 2 + qt + 1)
                    if qt:
                        dve.wait_ge(step("w_turned"), i * 2 + 1)
                    pv = prob[:, 0:8 * W].rearrange("p (j k) -> p j k", j=8)
                    nb_banks = 8 * W // 512
                    TTo(pv, PS[:, 0:nb_banks, :].rearrange("p a (j k) -> p (a j) k", k=W), bc(amask[:, S - W:S], [P, 8, W], 1), ALU.add)
                    ordered()
                    V.tensor_reduce(mx, pv, AX.X, ALU.max)
                    ordered()
                    V.tensor_scalar(nb, mx, -0.125, None, ALU.mult).then_inc(step("max_ready"), 1)

                def attn_weights(qt):
                    W = (qt + 1) * P
                    dve.wait_ge(step("attn_exp"), i * 2 + qt + 1)
                    V.reciprocal(pr, ps_)
                    ordered()
                    odd = pr[:, 4:8]
                    V.tensor_scalar(odd, odd, lmv, None, ALU.mult)
                    ordered()
                    pv = prob[:, 0:8 * W].rearrange("p (j k) -> p j k", j=8)
                    TTo(pv, pv, bc(pr, [P, 8, W], 2), ALU.mult)
                    ordered()
                    pw = prob[:, 0:8 * W].rearrange("p (m h k) -> p m h k", h=H1, m=2)
                    TTo(pw[:, 0, :, :], pw[:, 0, :, :], pw[:, 1, :, :], ALU.subtract).then_inc(step("w_ready"), 1)

                def wT_copy(qt):
                    dve.wait_ge(step("w_turned"), i * 2 + qt + 1)
                    J = 4 * (qt + 1)
                    V.tensor_copy(wT[:, 0:J, :], pB.rearrange("p a (j t) -> p (a j) t", t=P)[:, 0:J, :]).then_inc(step("wT_ready"), 1)

                def o_take(qt):
                    dve.wait_ge(step("o_ready"), i * 2 + qt + 1)
                    V.tensor_copy(o32[:, qt, :], pA[:, 0, :]).then_inc(step("o_taken"), 1)

                def o_sums():
                    dve.wait_ge(step("o_sq"), i + 1)
                    V.tensor_reduce(os_, prob[:, 0:1024].rearrange("p (j d) -> p j d", d=P), AX.X, ALU.add).then_inc(step("o_sums"), 1)

                def o_norm():
                    dve.wait_ge(step("o_root"), i + 1)
                    V.reciprocal(orr, os_)
                    ordered()
                    V.tensor_scalar(orr, orr, row("li")[:, 1:2], None, ALU.mult)
                    ordered()
                    v = o32.rearrange("p a (h d) -> p (a h) d", d=P)
                    TTo(v, v, bc(orr, [P, 8, P], 2), ALU.mult)
                    ordered()
                    TTo(v, v, bc(row("sub"), [P, 8, P], 1), ALU.mult).then_inc(step("o_normed"), 1)

                def yc_low():
                    split_low("yc_hi", i + 1, slice(A_YC, A_YC + 4), pA.rearrange("p a (j t) -> p (a j) t", t=S), "yc_ready")

                early = dict(
                    QK0=lambda: chunk_open(0), QK1=lambda: seg(0, 0), QK3=lambda: (state_copy(0), y_take(0, 0), seg(0, 1)),
                    V1=lambda: (state_copy(1), y_take(0, 1)), Z0=lambda: chunk_open(1), Z1=lambda: seg(1, 0),
                    Z3=lambda: (y_take(1, 0), seg(1, 1)), GV1=lambda: y_take(1, 1), GU0=gm_norm, GU1=gm_out,
                    GA0=qk_norm, GA1=qk_rope, GA3=lambda: attn_max(0), GB1=lambda: wT_copy(0), GB2=lambda: o_take(0),
                    GB3=lambda: attn_max(1), GC0=lambda: attn_weights(1), GC2=lambda: wT_copy(1), GC3=lambda: o_take(1))
                after = dict(
                    XBC2=lambda: (dt_abs(), dt_one()), XBC3=dt_finish, XBC4=lam_sums,
                    QK1=lambda: dec_mul(0, 0), QK2=lam_value, QK3=lambda: dec_mul(0, 1), Z1=lambda: dec_mul(1, 0),
                    Z3=lambda: dec_mul(1, 1), GV1=yz, GU0=qk_sums,
                    GA0=lambda: split_low("ya_hi", i + 1, slice(A_YA, A_YA + 4), uu, "ya_ready"), GA1=yb_norm,
                    GA2=lambda: split_low("yb_hi", i + 1, slice(A_YB, A_YB + 8), xbc[:, 0:8, :], "yb_ready"),
                    GA3=lambda: attn_weights(0), GC3=o_sums, BA1=o_norm, BB0=yc_low)

                def take(n, g):
                    kind, m = g["kind"], g["n"]
                    if g["taker"] != "dve" or not g["closes"]:
                        return
                    pair = bank(g).rearrange("p (k t) -> p k t", t=S)
                    if kind == "XBC":
                        dve.wait_ge(step("xbc_open"), i * 6 + m + 1)
                        conv_taps(1, i, g, "cw", 4, ((2, 1), (1, 2), (0, 3)), (2 * m, 2 * m + 1),
                                  (xbc[:, 2 * m, :], xbc[:, 2 * m + 1, :])).then_inc(step("xbc_conv"), 1)
                        ordered()
                        dve.drain().then_inc(taken["dve"], 1)
                    elif kind == "BA":
                        arrived(1, i, n)
                        v = G0[:, 2 * m:2 * m + 2, :]
                        TTo(v, pair, v, ALU.mult).then_inc(taken["dve"], 1)
                    elif kind in ("BB", "BC"):
                        arrived(1, i, n)
                        v = (ug[:, 2 * m:2 * m + 2, :] if kind == "BB" else SZ[:, 2 * m:2 * m + 2, :])
                        TTo(v, pair, v, ALU.mult).then_inc(taken["dve"], 1)
                        ordered()
                        o = G0[:, 2 * m:2 * m + 2, :]
                        last = TTo(o, o, v, ALU.add)
                        if kind == "BC":
                            last.then_inc(step("mg32_ready"), 1)
                            merged_low(1, i, m, G0)
                    elif kind in ("OUT", "DN"):
                        residual(1, i, n, g)
                    elif kind == "UP":
                        up_take(1, i, n, g)

                def residual(b, i, n, g):
                    arrived(b, i, n)
                    m = g["n"] if g["kind"] == "OUT" else g["n"] // 4
                    pair = bank(g).rearrange("p (k t) -> p k t", t=S)
                    v = x[:, 2 * m:2 * m + 2, :]
                    TTo(v, pair, v, ALU.add).then_inc(taken["dve"], 1)
                    dve.drain().then_inc(step("x_pair"), 1)

                def up_take(b, i, n, g):
                    m, val = g["n"] // 2, g["n"] % 2
                    buf = ypair(m % 2, val)
                    t0 = 2 * m + val * FT
                    if b == 1:
                        dve.wait_ge(step("up_open1"), i * (2 * FP) + g["n"] + 1)
                        last = conv_taps(1, i, g, "fw", 3, ((1, 1), (0, 2)), (t0, t0 + 1), (buf[:, 0, :], buf[:, 1, :]))
                        last.then_inc(taken["dve"], 1)
                        if not val:
                            dve.drain().then_inc(step("up_conv"), 1)
                    elif not val:
                        dve.wait_ge(step("up_open2"), i * FP + m + 1)
                        last = conv_taps(2, i, g, "fw", 3, ((0, 1), (2, -1)), (t0, t0 + 1), (buf[:, 0, :], buf[:, 1, :]))
                        last.then_inc(taken["dve"], 1)
                        dve.drain().then_inc(step("up_conv"), 1)

                def gate_up(b, i, n, g):
                    m = g["n"] // 2
                    v = ypair(m % 2, 0)
                    if b == 1:
                        ordered()
                    dve.wait_ge(step("up_act"), layer(b, i) * FP + m + 1)
                    if b == 1:
                        TTo(v, v, ypair(m % 2, 1), ALU.mult).then_inc(step("gated32"), 1)
                    else:
                        arrived(2, i, n)
                        TTo(v, bank(g).rearrange("p (k t) -> p k t", t=S), v, ALU.mult).then_inc(taken["dve"], 1)
                        dve.drain().then_inc(step("gated32"), 1)

                def gated_low(b, i, m):
                    dve.wait_ge(step("gated_hi"), layer(b, i) * FP + m + 1)
                    t = slice(A_G + 2 * m, A_G + 2 * m + 2)
                    TTo(alo[:, t, :], ypair(m % 2, 0), ahi[:, t, :].bitcast(f32), ALU.subtract).then_inc(step("up_free"), 1)
                    if m == FP - 1:
                        params_used()

                def up_stream(b, i, n, g, G):
                    if g["n"] % 2 == 1:
                        gate_up(b, i, n, g)
                    elif g["n"] >= 2:
                        gated_low(b, i, g["n"] // 2 - 1)
                    if g["n"] == 2 * FP - 1:
                        gated_low(b, i, FP - 1)

                for n, g in enumerate(G1):
                    if g["name"] == "UP0":
                        norm(1, i, 1, "norm2", A_H2)
                        low_part(V, 1, i, n - 1 + SPL, G1, False)
                    take(n, g)
                    if g["name"] in early:
                        ordered()
                        early[g["name"]]()
                    if g["name"] != "OUT3":
                        low_part(V, 1, i, n + SPL, G1, False)
                    if g["name"] in after:
                        ordered()
                        after[g["name"]]()
                    if g["kind"] == "UP":
                        up_stream(1, i, n, g, G1)

            with dve.Fori(0, LAYERS) as i:
                dve.wait_ge(step("par_in2"), i * 48 + 48)
                low_part(V, 2, i, 0, G2, False)
                norm(2, i, 0, "norm1", A_H, lambda: low_part(V, 2, i, 1, G2, False))
                low_part(V, 2, i, 2, G2, False)

                def b2_max(u):
                    dve.wait_ge(step("b2_scores"), i * 8 + u + 1)
                    dve.wait_ge(step("b2_bias_in"), i * 384 + 48 * (u + 1))
                    px = PS[:, 2 * (u % 2):2 * (u % 2) + 2, :].rearrange("p a c -> p (a c)")[:, 0:768]
                    if u:
                        dve.wait_ge(step("b2_turned"), i * 8 + u)
                    STT(b2_P, px, float(P) ** -0.5, b2_bias.rearrange("p g k -> p (g k)"), ALU.mult, ALU.add).then_inc(step("b2_bias_free"), 1)
                    ordered()
                    V.tensor_reduce(bmx[:, 0:1], b2_P, AX.X, ALU.max)
                    ordered()
                    V.tensor_scalar(bnm[:, 0:1], bmx[:, 0:1], -1.0, None, ALU.mult).then_inc(step("b2_max"), 1)

                def b2_norm(u):
                    dve.wait_ge(step("b2_exp"), i * 8 + u + 1)
                    V.reciprocal(brr[:, 0:1], bsm[:, 0:1])
                    ordered()
                    V.tensor_scalar(b2_P, b2_P, brr[:, 0:1], None, ALU.mult).then_inc(step("b2_P_ready"), 1)

                def at_low(j):
                    dve.wait_ge(step("at_hi"), i * 4 + j + 1)
                    last = TTo(alo[:, A_AT + j, :], pC[:, 0:S], ahi[:, A_AT + j, :].bitcast(f32), ALU.subtract)
                    last.then_inc(step("at_lo"), 1)
                    if j == 3:
                        dve.drain().then_inc(step("at_ready"), 1)

                def take2(n, g):
                    kind, m = g["kind"], g["n"]
                    if g["taker"] != "dve" or not g["closes"]:
                        return
                    pair = bank(g).rearrange("p (k t) -> p k t", t=S)
                    if kind == "WP":
                        dve.wait_ge(step("po_hi"), i * 4 + m + 1)
                        for t in range(2):
                            k = A_PO + 2 * m + t
                            last = STT(alo[:, k, :], pair[:, t, :], col(2, "ps", 2 * m + t), ahi[:, k, :].bitcast(f32), ALU.mult, ALU.subtract)
                        last.then_inc(taken["dve"], 1)
                        if m == 3:
                            dve.drain().then_inc(step("po_ready"), 1)
                    elif kind == "WA":
                        arrived(2, i, n)
                        v = ug[:, 2 * m:2 * m + 2, :]
                        TTo(v, pair, v, ALU.mult).then_inc(taken["dve"], 1)
                    elif kind == "WB":
                        arrived(2, i, n)
                        v, o = gate_t(m), ug[:, 2 * m:2 * m + 2, :]
                        TTo(v, pair, v, ALU.mult).then_inc(taken["dve"], 1)
                        ordered()
                        TTo(o, o, v, ALU.add).then_inc(step("mg32_ready"), 1)
                        merged_low(2, i, m, ug)
                    elif kind in ("OUT", "DN"):
                        residual(2, i, n, g)
                    elif kind == "UP":
                        up_take(2, i, n, g)

                for n, g in enumerate(G2):
                    if g["name"] == "UP0":
                        norm(2, i, 1, "norm2", A_H2)
                        low_part(V, 2, i, n - 1 + SPL, G2, False)
                    take2(n, g)
                    if g["name"] in PV_AT:
                        at_low(PV_AT[g["name"]])
                    if g["name"] in SC_AT:
                        b2_max(SC_AT[g["name"]])
                    if g["name"] != "OUT3":
                        low_part(V, 2, i, n + SPL, G2, False)
                    if g["name"] in SC_AT:
                        b2_norm(SC_AT[g["name"]])
                    if g["name"] == "Q0":
                        split_low("pd_hi", i + 1, slice(A_PD, A_PD + 8), PS[:, 0:4, :].rearrange("p a (k t) -> p (a k) t", t=S), "pd_ready")
                    if g["kind"] == "UP":
                        up_stream(2, i, n, g, G2)

            rstd_of("root", 4 * LAYERS + 1)
            for k in range(KD):
                last = STT(h32[:, k, :], x[:, k, :], colsf[:, k:k + 1], rstd[:, :], ALU.mult, ALU.mult)
                if k % 2:
                    last.then_inc(step("f_normed"), 1)
            dve.wait_ge(step("out_turned"), 1)
            V.tensor_copy(g01[:, 0:4, :].rearrange("p k t -> p (k t)"), pA.rearrange("p a c -> p (a c)")).then_inc(step("out_ready_0"), 1)


def kernel(**inputs):
    import numpy as np
    import concourse.bacc as bacc
    from concourse import mybir
    from concourse.bass_utils import run_bass_kernel_spmd as run

    f32 = mybir.dt.float32
    a = {k: np.ascontiguousarray(v) for k, v in inputs.items()}
    L, S, P = 2, 256, 128

    def by_feature(v):
        v = v.reshape(L, -1, P, *v.shape[2:])
        return np.moveaxis(v, 2, 1).reshape(L, P, -1)

    cols_1 = np.concatenate([by_feature(a["attn_norm_g"]), by_feature(a["ssm_conv_w"]), by_feature(a["ssm_conv_b"]),
                             by_feature(a["ssm_norm_g"]), by_feature(np.repeat(a["ssm_d"], 64, axis=1)),
                             by_feature(a["ffn_norm_g"]), by_feature(a["ffn_conv_w"]), by_feature(a["ffn_conv_b"])], axis=2)
    cols_2 = np.concatenate([by_feature(a["norm1_2"]), by_feature(a["pool_scale_2"]), by_feature(a["norm2_2"]),
                             by_feature(np.moveaxis(a["conv_w_2"], 1, 2)), by_feature(a["conv_b_2"])], axis=2)
    cols_f = np.ascontiguousarray(a["norm_f_2"].reshape(8, P).T)
    li = np.array([[0.8 - 0.6 * np.exp(-0.3 * n)] for n in range(L)])
    li = np.concatenate([li, 1.0 - li], axis=1).astype(np.float32)
    rows_1 = np.concatenate([a["gm_v_norm_g"], a["gm_b_s"].reshape(L, -1), a["da_q_norm_g"], a["da_k_norm_g"], a["da_subln_g"],
                             a["ssm_dt_bias"], a["ssm_a_log"], li], axis=1)
    p = np.arange(P)
    ident = np.eye(P, dtype=np.float32)
    tri = (p[:, None] <= p[None, :]).astype(np.float32)
    amask = np.concatenate([np.zeros((P, P)), np.where(p[None, :] <= p[:, None], 0.0, -1e30)], axis=1).astype(np.float32)
    inv = (1.0 / (np.float32(500000.0) ** (np.arange(0, 16, 2, dtype=np.float32) / np.float32(16)))).astype(np.float32)
    ang = (np.arange(S, dtype=np.float32)[:, None] * inv[None, :]).astype(np.float32).astype(np.float64)
    rope = np.stack([np.cos(ang), np.sin(ang)], axis=1).astype(np.float32).reshape(2, P, 2, 8)
    rope = np.ascontiguousarray(np.moveaxis(rope, 0, 1)).reshape(P, 32)
    off = np.arange(511) - 255
    n = -off
    mag = np.abs(n)
    large = np.minimum(8 + (np.log(np.maximum(mag, 1) / 8) / np.log(1024 / 8) * 8).astype(np.int32), 15)
    bucket = (n < 0) * 16 + np.where(mag < 8, mag, large)
    onehot = np.zeros((32, 512), np.float32)
    onehot[bucket, np.arange(511)] = 1.0
    offmask = np.full((12, 512), -1e30, np.float32)
    for g, (window, dilation) in enumerate(((128, 1), (512, 4), (2048, 16))):
        ok = (off % dilation == 0) & (mag <= window // (2 * dilation) * dilation)
        offmask[4 * g:4 * g + 4, :511] = np.where(ok, 0.0, -1e30)
    band = np.zeros((S, 4, S), np.float64)
    for g, w in enumerate((2, 4, 8, 16)):
        for t in range(S):
            lo, hi = max(t - w // 2, 0), min(t - w // 2 + w, S)
            band[lo:hi, g, t] = 1.0 / (hi - lo)
            band[t, g, t] -= 1.0
    band = band.astype(np.float32).reshape(2, P, 4 * S)

    feeds = {k: a[k] for k in ("x", "w_in", "gm_w_s", "w_branch_a", "w_branch_b", "w_branch_c", "w_out", "ffn_w_up", "ffn_w_down",
                               "w_in_2", "w_pool_2", "w_a_2", "w_b_2", "w_o_2", "w_up_2", "w_down_2", "rel_bias_2")}
    feeds.update(cols_1=cols_1, cols_2=cols_2, cols_f=cols_f, rows_1=rows_1, lam_1=a["da_lambda"].reshape(L, -1), c_ident=ident, c_tri=tri, c_amask=amask, c_rope=rope,
                 c_onehot=onehot, c_offmask=offmask, c_band=band)
    nc = bacc.Bacc("TRN2", target_bir_lowering=False, num_devices=1)
    arrays, t_in = {}, {}
    for name, v in feeds.items():
        arrays[f"in_{name}"] = np.ascontiguousarray(v)
        t_in[name] = nc.dram_tensor(f"in_{name}", v.shape, f32, kind="ExternalInput").ap()
    t_in["bias_table"] = nc.dram_tensor("bias_table", (12, 129 * 511), f32, kind="Internal").ap()
    out = nc.dram_tensor("out", (1, S, 1024), f32, kind="ExternalOutput").ap()
    build_program(nc, t_in, out)
    r = run(nc, [arrays], core_ids=[0])
    return r.results[0]["out"]
```

```python
def plan_block(names, first_bank=0):
    groups = []
    bank = first_bank
    for name, count, kt, cols, tile, form, taker in names:
        for n in (range(count) if isinstance(count, int) else count):
            per_bank = 4 if name == "DN" else 1
            sub = n % per_bank
            groups.append(dict(name=f"{name}{n}", kind=name, n=n, kt=kt, cols=cols, form=form, taker=taker,
                               tile=tile(n), bank=bank % 3, opens=sub == 0, closes=sub == per_bank - 1, sub=sub))
            if sub == per_bank - 1:
                bank += 1
    return groups


def down_part(n):
    first, second = n % 2, n % 4 // 2
    return (n // 4 * 2 + first, second) if n < 4 else (n // 4 * 2 + second, first)


def ring(count, slots, skips):
    at, place, last = 0, [], []
    user = {s: s - slots for s in range(slots)}
    for n in range(count + 2):
        assert n != count or at % slots == 0
        at += n in skips
        place.append(at % slots)
        last.append(user[at % slots])
        user[at % slots] = n
        at += 1
    return place, last


def build_program(nc, t_in, out):
    import concourse.bass as bass
    from concourse import mybir
    from contextlib import ExitStack

    f32, f32r = mybir.dt.float32, mybir.dt.float32r
    ACT = mybir.ActivationFunctionType
    ALU = mybir.AluOpType
    AX = mybir.AxisListType

    P = 128
    S = 256
    TT = S // P
    D = 1024
    KD = D // P
    PAIRS = KD // 2
    LAYERS = 2
    EPS = 1e-6
    LOW, HIGH = 5, 3
    AHEAD = 2
    SLOT = 2048
    BANKS = 3
    FF = 2816
    FP = FF // 256
    FT = FF // P
    DNK = FT // 2
    MAX_WINDOW = 16
    H1 = 4
    NEG = -1e30

    A_H, A_YA, A_YB, A_YC, A_MG, A_H2, A_G = 0, 8, 12, 20, 0, 22, 0
    A_PD, A_PO, A_AT = 8, 16, 24
    A_XG = (22, 8)
    A_NORM = (A_H, A_H2)

    const = lambda v: (lambda n: v)
    pool_tile = lambda n: A_PD + 2 * n
    G1 = plan_block([
        ("XBC", 6, 8, 256, const(A_H), "A", "dve"),
        ("QK", 4, 8, 256, const(A_H), "B", "act"),
        ("V", 2, 8, 256, const(A_H), "B", "act"),
        ("Z", 4, 8, 256, const(A_H), "A", "act"),
        ("GV", 2, 8, 256, const(A_H), "B", "act"),
        ("GU", 2, 8, 256, const(A_H), "A", "act"),
        ("GA", 4, 8, 256, const(A_H), "A", "act"),
        ("GB", 4, 8, 256, const(A_H), "A", "act"),
        ("GC", 4, 8, 256, const(A_H), "A", "act"),
        ("BA", 4, 4, 256, const(A_YA), "A", "dve"),
        *[(kind, [m], kt, 256, const(tile), "A", "dve") for kind, m, kt, tile in (
            ("BB", 0, 8, A_YB), ("BB", 1, 8, A_YB), ("BC", 0, 4, A_YC), ("BC", 1, 4, A_YC), ("BB", 2, 8, A_YB),
            ("BC", 2, 4, A_YC), ("BC", 3, 4, A_YC), ("BB", 3, 8, A_YB))],
        ("OUT", 4, 8, 256, const(A_MG), "A", "dve"),
        ("UP", 2 * FP, 8, 256, const(A_H2), "A", "dve"),
        ("DN", 16, DNK, 128, lambda n: A_G + DNK * down_part(n)[1], "A", "dve"),
    ])
    G2 = plan_block([
        ("PU", 4, 8, 256, const(A_H), "B", "act"),
        ("Q", 6, 8, 256, const(A_H), "A", "act"),
        ("K", 6, 8, 256, const(A_H), "A", "act"),
        *[(kind, ms, {"WP": 2, "WB": 4}.get(kind, 8), 256, tile, form, taker) for kind, ms, tile, form, taker in (
            ("WP", [0], pool_tile, "A", "dve"), ("V", [0], const(A_H), "B", "act"),
            ("WP", [1], pool_tile, "A", "dve"), ("V", range(1, 6), const(A_H), "B", "act"),
            ("WP", [2], pool_tile, "A", "dve"), ("GP", [0], const(A_H), "A", "act"),
            ("WP", [3], pool_tile, "A", "dve"), ("GP", range(1, 4), const(A_H), "A", "act"),
            ("WA", range(3), const(A_PO), "A", "dve"), ("GT", range(4), const(A_H), "A", "act"),
            ("WB", range(4), const(A_AT), "A", "dve"), ("WA", [3], const(A_PO), "A", "dve"))],
        ("OUT", 4, 8, 256, const(A_MG), "A", "dve"),
        ("UP", 2 * FP, 8, 256, const(A_H2), "A", "dve"),
        ("DN", 16, DNK, 128, lambda n: A_G + DNK * down_part(n)[1], "A", "dve"),
    ])
    for b, G in ((1, G1), (2, G2)):
        for g in G:
            g["block"] = b
    assert all(G1[n][key] == G2[n][key] for n in range(2) for key in ("kt", "cols"))
    FIRST = ("XBC0", "PU0", "UP0")
    MERGED = ("BC0", "BC1", "BC2", "BB3", "WB0", "WB1", "WB2", "WA3")

    C = t_in
    COLS1 = dict(norm1=(0, 8), cw=(8, 48), cb=(56, 12), sg=(68, 8), sd=(76, 8), norm2=(84, 8), fw=(92, 132), fb=(224, 44))
    COLS2 = dict(norm1=(0, 8), ps=(8, 8), norm2=(16, 8), fw=(24, 66), fb=(90, 22))
    ROWS1 = dict(gvg=(0, 512), gb=(512, 512), qg=(1024, 64), kg=(1088, 64), sub=(1152, 128), dtb=(1280, 16),
                 alog=(1296, 16), li=(1312, 2))
    NC1, NC2, NR1 = 268, 112, 1314

    ctx = ExitStack()
    with ctx:
        def sb(name, shape, dt=f32):
            return ctx.enter_context(nc.sbuf_tensor(name, shape, dt))

        def sem(name):
            return ctx.enter_context(nc.semaphore(name))

        raw = nc.alloc_sbuf_tensor_at("w_raw", [P, LOW, SLOT], f32, offset=-(-nc.sbuf_base // 32) * 32)
        wlo = sb("w_low", [P, LOW, SLOT], f32r)
        whi = sb("w_hi", [P, HIGH, SLOT], f32r)
        ahi = sb("act_hi", [P, 30, S], f32r)
        alo = sb("act_lo", [P, 30, S], f32r)
        x = sb("x", [P, KD, S])
        g01 = sb("gates_01", [P, 2 * KD, S])
        ug = sb("spatial_uv", [P, KD, S])
        xbc = sb("xbc", [P, 12, S])
        qkv = sb("qkv", [P, 12 * S])
        tmp = sb("tmp", [P, 16 * S])
        cols1 = sb("cols1", [P, NC1])
        cols2 = cols1[:, 0:NC2]
        rows1 = sb("rows1", [P, NR1])
        ident, tri = sb("ident", [P, P]), sb("tri", [P, P])
        amask = sb("amask", [P, S])
        ones = sb("ones", [P, P])
        rope = sb("rope", [P, TT, 2, 8])
        zero = sb("zero", [P, P // 2], f32r)
        rstd = sb("rstd", [P, TT])
        rstd_all = sb("rstd_all", [P, S])
        yrstd = sb("y_rstd", [P, TT])
        sm = sb("small", [P, 400])
        eps = sm[:, 399:400]

        PS = ctx.enter_context(nc.psum_tensor("chain_ps", [P, 5, 512], f32))
        PJ = ctx.enter_context(nc.psum_tensor("proj_ps", [P, BANKS, 512], f32))
        pA, pB, pC = PS[:, 0:2, :], PS[:, 2:4, :], PS[:, 4, :]

        quarter = lambda q, n=1: tmp[:, q * 1024:(q + n) * 1024]
        sq8 = quarter(0, 2).rearrange("p (k t) -> p k t", t=S)
        h32 = quarter(2, 2).rearrange("p (k t) -> p k t", t=S)
        xdt = quarter(0)
        dec = quarter(1).rearrange("p (h t) -> p h t", t=P)
        cdec = quarter(2).rearrange("p (h t) -> p h t", t=P)
        prev = quarter(3).rearrange("p (g q) -> p g q", g=2)
        qkT = quarter(0, 2).rearrange("p (j t) -> p j t", t=S)
        prob = quarter(2, 2)
        qk = qkv[:, 0:2048].rearrange("p (a c) -> p a c", a=TT)
        vv = qkv[:, 2048:3072].rearrange("p (a c) -> p a c", a=TT)
        o32 = qkv[:, 0:1024].rearrange("p (a c) -> p a c", a=TT)
        wT = qkv[:, 1024:2048].rearrange("p (j t) -> p j t", t=P)
        vg = ug[:, 0:4, :].rearrange("p k t -> p (k t)").rearrange("p (a c) -> p a c", a=TT)
        uu = ug[:, 4:8, :]
        G0, SZ = g01[:, 0:8, :], g01[:, 8:16, :]

        at = [0]

        def small(n):
            at[0] += n
            return sm[:, at[0] - n:at[0]]
        dtx, dta, dte, dtu, dtl, dtv, dtA = [small(32) for _ in range(7)]
        aexp, acum = small(16), small(16)
        dend = small(8)
        gms, gmr = small(2), small(2)
        qs, qr = small(32), small(32)
        mx, nb, ps_, pr = small(8), small(8), small(8), small(8)
        os_, orr = small(8), small(8)
        lms, lmv, root_scratch = small(2), small(1), small(1)
        bmx, bnm, bsm, brr = [small(2) for _ in range(4)]
        early = g01[:, 0:8, :].rearrange("p k t -> p (k t)")
        cbm = early[:, 0:256].rearrange("p (g t) -> p g t", g=2)
        bT = early[:, 256:512].rearrange("p (g n) -> p g n", g=2)
        wsT = early[:, 512:1024].rearrange("p (g t) -> p g t", g=4)
        wsn = early[:, 1024:1536].rearrange("p (g s) -> p g s", g=4)
        lmp = early[:, 1536:1664]
        dtw = early[:, 1664:1792].rearrange("p (k h) -> p k h", k=KD)
        lam_row = early[:, 1792:2048]

        w_loaded = [sem(f"w_loaded{n}") for n in range(LOW)]
        w_hi, w_lo_dve, w_lo_pool, group_done = sem("w_hi"), sem("w_lo_dve"), sem("w_lo_pool"), sem("group_done")
        taken = dict(act=sem("taken_act"), dve=sem("taken_dve"))
        loads_cleared = sem("loads_cleared")
        const_in, ident_in, x_in, setup = sem("const_in"), sem("ident_in"), sem("x_in"), sem("setup")
        out_in = sem("out_stored")
        STEPS = {}

        def step(name):
            if name not in STEPS:
                STEPS[name] = sem(name)
            return STEPS[name]

        def layer(b, i):
            return i + LAYERS if b == 2 else i

        def norm_count(b, i, which, pair):
            return layer(b, i) * (2 * PAIRS) + (PAIRS * which + pair)

        NG = {1: len(G1), 2: len(G2)}
        BASE = {1: 0, 2: LAYERS * len(G1)}
        NTAKE = {b: {e: sum(1 for g in G if g["taker"] == e and g["closes"]) for e in ("act", "dve")}
                 for b, G in ((1, G1), (2, G2))}
        at_name = {b: {g["name"]: n for n, g in enumerate(G)} for b, G in ((1, G1), (2, G2))}
        skips = lambda b, *names: [at_name[b][name] for name in names]
        LOW_AT, LOW_LAST, HIGH_AT, HIGH_LAST = {}, {}, {}, {}
        LOW_AT[1], LOW_LAST[1] = ring(NG[1], LOW, skips(1, "UP3", "UP8", "UP13", "UP18"))
        LOW_AT[2], LOW_LAST[2] = ring(NG[2], LOW, skips(2, "UP8"))
        HIGH_AT[1], HIGH_LAST[1] = ring(NG[1], HIGH, skips(1, "UP11"))
        HIGH_AT[2], HIGH_LAST[2] = ring(NG[2], HIGH, [])
        NLOAD = {b: [LOW_AT[b][:NG[b]].count(s) for s in range(LOW)] for b in (1, 2)}
        SPLITS = {}
        for b in (1, 2):
            SPLITS[b], at_group = {}, -1
            for n in range(AHEAD, NG[b] + AHEAD):
                at_group = max(at_group, HIGH_LAST[b][n])
                SPLITS[b].setdefault(at_group, []).append(n)

        def scaled_count(b, i, g):
            if b == 1:
                return i * 4 + (2 * (g["kind"] == "UP") + g["n"] + 1)
            return i * 2 + (4 * LAYERS + g["n"] + 1)

        def count(b, i, k):
            return i * NG[b] + (BASE[b] + k + LOW)

        def plain_count(b, i, k):
            return i * NG[b] + (BASE[b] + k)

        def taken_count(b, e, i, g):
            G = G1 if b == 1 else G2
            k = sum(1 for q in G[:g] if q["taker"] == e and q["closes"])
            base = LAYERS * NTAKE[1][e] if b == 2 else 0
            return i * NTAKE[b][e] + (base + k + 1)

        block = ctx.enter_context(nc.Block())

        def group_view(t, slot, g):
            return t[:, slot, 0:g["kt"] * g["cols"]].rearrange("p (k n) -> p k n", k=g["kt"])

        def weight_source(b, i, g):
            kind, n, c = g["kind"], g["n"], g["cols"]
            lay = bass.ds(i, 1)

            def of(name, k0, k1, c0):
                return C[name][lay, k0:k1, c0:c0 + c].rearrange("a (k p) n -> p (a k) n", p=P)
            if kind == "UP":
                return of("ffn_w_up" if b == 1 else "w_up_2", 0, D, (n % 2) * FF + (n // 2) * 256)
            if kind == "DN":
                return of("ffn_w_down" if b == 1 else "w_down_2", down_part(n)[1] * DNK * P, (down_part(n)[1] + 1) * DNK * P, down_part(n)[0] * P)
            if b == 1:
                first = dict(GU=0, GV=512, Z=1024, XBC=2048, QK=3600, V=4624, GA=5136, GB=6160, GC=7184)
                if kind in first:
                    return of("w_in", 0, D, first[kind] + 256 * n)
                name = dict(BA="w_branch_a", BB="w_branch_b", BC="w_branch_c", OUT="w_out")[kind]
                return of(name, 0, g["kt"] * P, 256 * n)
            first = dict(PU=0, Q=1024, K=2560, V=4096, GP=5632, GT=6656)
            if kind in first:
                return of("w_in_2", 0, D, first[kind] + 256 * n)
            if kind == "WP":
                return C["w_pool_2"][lay, n, :, :].rearrange("a (k p) n -> p (a k) n", p=P)
            name = dict(WA="w_a_2", WB="w_b_2", OUT="w_o_2")[kind]
            return of(name, 0, g["kt"] * P, 256 * n)

        def bias_loads(sp, i, u):
            sp.wait_ge(step("b2_bias_free"), i * 8 + (u + 1))
            sp.sem_inc(loads_cleared, 1)
            j, qt = u // 2, u % 2
            for g in range(3):
                row = C["bias_table"][4 * g + j, 255 - qt * P:255 - qt * P + P * 510]
                sp.dma_start(b2_bias[:, g, :], row.rearrange("(q f) -> q f", f=510)[:, 0:S]).then_inc(step("b2_bias_in"), 16)

        def gate_t(m):
            return xbc[:, 4 * m:4 * m + 2, :] if m < 3 else xbc[:, 2:7:4, :]

        b2_bias = tmp[:, 0:768].rearrange("p (g k) -> p g k", g=3)
        b2_P = tmp[:, 768:1536]
        b2_PT = tmp[:, 1536:3072].rearrange("p (k q) -> p k q", q=S)

        POOL_K = {8: 4, 4: 2, 2: 1, DNK: 6}

        def low_part(eng, b, i, n, G, on_pool):
            g = G[n % len(G)]
            slot = LOW_AT[b][n]
            cut = g["kt"] - POOL_K[g["kt"]]
            ks = slice(cut, g["kt"]) if on_pool else slice(0, cut)
            eng.wait_ge(w_hi, plain_count(b, i, n + 1))
            eng.tensor_tensor(group_view(wlo, slot, g)[:, ks, :], group_view(raw, slot, g)[:, ks, :],
                              group_view(whi, HIGH_AT[b][n], g)[:, ks, :].bitcast(f32), ALU.subtract
                              ).then_inc(w_lo_pool if on_pool else w_lo_dve, 1)

        def high_part(act, b, i, n, G):
            g = G[n % len(G)]
            slot = LOW_AT[b][n]
            before = LOW_AT[b][:n].count(slot) + (LAYERS * NLOAD[1][slot] if b == 2 else 0)
            act.wait_ge(w_loaded[slot], i * (16 * NLOAD[b][slot]) + 16 * (before + 1))
            act.wait_ge(group_done, count(b, i, HIGH_LAST[b][n] + 1))
            act.activation(group_view(whi, HIGH_AT[b][n], g), group_view(raw, slot, g), ACT.Copy).then_inc(w_hi, 1)

        def col(b, key, k):
            t, o = (cols1, COLS1) if b == 1 else (cols2, COLS2)
            return t[:, o[key][0] + k:o[key][0] + k + 1]

        def row(key):
            return rows1[:, ROWS1[key][0]:ROWS1[key][0] + ROWS1[key][1]]

        def bc(ap, dims, axis):
            return ap.unsqueeze(axis).to_broadcast(dims)

        def band(s):
            return xbc[:, 4 * s:4 * s + 4, :].rearrange("p k t -> p (k t)")

        def ypair(buf, val):
            q = 2 * buf + val
            return tmp[:, q * 512:(q + 1) * 512].rearrange("p (k t) -> p k t", t=S)

        BIAS_AT = {}
        SC_AT, TR_AT, PV_AT = {}, {}, {}
        hooks2 = ([f"V{n}" for n in range(5)] + ["WP2"] + [f"GP{n}" for n in range(4)] + [f"WA{n}" for n in range(3)]
                  + [f"GT{n}" for n in range(4)])
        for u in range(8):
            SC_AT[hooks2[2 * u]] = u
            TR_AT[hooks2[2 * u + 1]] = u
            at2 = [g["name"] for g in G2]
            BIAS_AT["K0" if u == 0 else at2[at2.index(hooks2[2 * u - 2]) + LOW]] = u
            if u % 2:
                PV_AT[hooks2[min(2 * u + 3, len(hooks2) - 1)]] = u // 2

        @block.sync
        def _(sp):
            def load(b, i, n, source):
                sp.wait_ge(group_done, count(b, i, LOW_LAST[b][n] + 1))
                sp.sem_inc(loads_cleared, 1)
                slot = LOW_AT[b][n]
                g = (G1 if b == 1 else G2)[n % NG[b]]
                sp.dma_start(group_view(raw, slot, g), source).then_inc(w_loaded[slot], 16)

            sp.dma_start(ident[:, :], C["c_ident"]).then_inc(ident_in, 16)
            for tt in range(TT):
                sp.dma_start(g01[:, 4 * tt:4 * tt + 4, :].rearrange("p k t -> p (k t)"), C["x"][0, tt * P:(tt + 1) * P, :]).then_inc(x_in, 16)
            sp.dma_start(cols1[:, :], C["cols"][0, :, :]).then_inc(step("cols_in"), 16)
            for dst, name in ((tri, "c_tri"), (amask, "c_amask")):
                sp.dma_start(dst[:, :], C[name]).then_inc(const_in, 16)
            sp.dma_start(rope[:, :, :, :].rearrange("p a b c -> p (a b c)"), C["c_rope"]).then_inc(const_in, 16)
            for b, G in ((1, G1), (2, G2)):
                if b == 2:
                    sp.wait_ge(step("bias_stored"), 16)
                    sp.sem_inc(loads_cleared, 1)
                with sp.Fori(0, LAYERS) as i:
                    sp.wait_ge(step("layer_done"), layer(b, i) + 1)
                    sp.sem_inc(loads_cleared, 1)
                    lay = bass.ds(i, 1)
                    if b == 2:
                        for s in range(TT):
                            sp.dma_start(band(s), C["c_band"][s, :, :]).then_inc(step("par_in2"), 16)
                    for n, g in enumerate(G):
                        load(b, i, n, weight_source(b, i, g))
                        if b == 1 and n == 1:
                            sp.wait_ge(step("x_turned"), PAIRS)
                            sp.sem_inc(loads_cleared, 1)
                            sp.dma_start(rows1[:, :], C["rows_1"][lay, :].to_broadcast([P, NR1])).then_inc(step("par_in1"), 16)
                            sp.dma_start(lam_row, C["lam_1"][lay, :].to_broadcast([P, 256])).then_inc(step("par_in1"), 16)
                            sp.dma_start(dtw[:, :, :], C["w_in"][lay, :, 3584:3600].rearrange("a (k p) n -> p (a k) n", p=P)).then_inc(step("par_in1"), 16)
                            sp.dma_start(wsn[:, :, :], C["gm_w_s"][lay, :, :, :].rearrange("a g t s -> t (a g) s")).then_inc(step("par_in1"), 16)
                        if g["name"] == "DN5":
                            sp.wait_ge(step("layer_done"), layer(b, i) + 2)
                            sp.sem_inc(loads_cleared, 1)
                            sp.dma_start(cols1[:, :], C["cols"][bass.ds(layer(b, i) + 1, 1), :, :].rearrange("a p c -> p (a c)")).then_inc(step("cols_in"), 16)
                        if b == 2 and g["name"] in BIAS_AT:
                            bias_loads(sp, i, BIAS_AT[g["name"]])
            for n in range(AHEAD):
                load(2, LAYERS - 1, NG[2] + n, weight_source(2, 0, G2[n]))
            for tt in range(TT):
                sp.wait_ge(step(f"out_ready_{tt}"), 1)
                sp.dma_start(out[0, tt * P:(tt + 1) * P, :], g01[:, 4 * tt:4 * tt + 4, :].rearrange("p k t -> p (k t)")).then_inc(out_in, 16)
            sp.wait_ge(out_in, 16 * TT)
            sp.wait_ge(step("bias_stored"), 16)

        @block.gpsimd
        def _(pool):
            nc.gpsimd.memset(ones[:, :], 1.0 / D).then_inc(setup, 1)
            nc.gpsimd.memset(eps, EPS).then_inc(setup, 1)
            def square_sum(b, i, which, p):
                pool.wait_ge(step("sq"), norm_count(b, i, which, p + 1))
                nc.gpsimd.tensor_tensor(sq8[:, 2 * p, :], sq8[:, 2 * p, :], sq8[:, 2 * p + 1, :], ALU.add).then_inc(step("sq_sum"), 1)

            for p in range(PAIRS):
                square_sum(1, 0, 0, p)
                if p >= PAIRS - AHEAD:
                    low_part(nc.gpsimd, 1, 0, p - (PAIRS - AHEAD), G1, True)
            for b, G in ((1, G1), (2, G2)):
                with pool.Fori(0, LAYERS) as i:
                    for q in SPLITS[b].get(-1, ()):
                        low_part(nc.gpsimd, b, i, q, G, True)
                    for n, g in enumerate(G):
                        residual = g["kind"] == "OUT" or g["kind"] == "DN" and g["closes"]
                        which, p = (1, g["n"]) if g["kind"] == "OUT" else (2, g["n"] // 4)
                        if g["name"] == "OUT3":
                            square_sum(b, i, which, p)
                        for q in SPLITS[b].get(n, ()):
                            low_part(nc.gpsimd, b, i, q, G, True)
                        if residual and g["name"] != "OUT3":
                            square_sum(b, i, which, p)

        @block.tensor
        def _(pe):
            mm = nc.tensor.matmul

            def proj_waits(b, i, n, G):
                g = G[n]
                pe.wait_ge(w_lo_dve, plain_count(b, i, n + 1))
                pe.wait_ge(w_lo_pool, plain_count(b, i, n + 1))
                if g["opens"]:
                    old = max((q for q in range(n) if G[q]["closes"] and G[q]["bank"] == g["bank"]), default=None)
                    e = "dve" if old is None else G[old]["taker"]
                    pe.wait_ge(taken[e], taken_count(b, e, i, 0 if old is None else old + 1))

            def open_bank(g):
                mm(PJ[:, g["bank"], :], zero[:, 0:1].to_broadcast([P, P]),
                   zero[:, :].unsqueeze(1).to_broadcast([P, 8, P // 2]), start=True, stop=False)

            def products(g, n, t, ks, start, stop, a0):
                hi, lo = group_view(whi, HIGH_AT[g["block"]][n], g), group_view(wlo, LOW_AT[g["block"]][n], g)
                half = down_part(g["n"])[0] % 2 if g["kind"] == "DN" else t
                o = PJ[:, g["bank"], half * 256:(half + 1) * 256]
                for k in ks:
                    if g["form"] == "A":
                        wh, wl = hi[:, k, t * P:(t + 1) * P], lo[:, k, t * P:(t + 1) * P]
                        xh, xl = ahi[:, a0 + k, :], alo[:, a0 + k, :]
                        three = ((wh, xh), (wh, xl), (wl, xh))
                    else:
                        xh, xl = ahi[:, a0 + k, t * P:(t + 1) * P], alo[:, a0 + k, t * P:(t + 1) * P]
                        three = ((xh, hi[:, k, :]), (xh, lo[:, k, :]), (xl, hi[:, k, :]))
                    for q, (held, moved) in enumerate(three):
                        last = mm(o, held, moved, start=start and k == ks[0] and q == 0, stop=stop and k == ks[-1] and q == 2)
                return last

            def proj(b, i, n, G, normed=None):
                g = G[n]
                proj_waits(b, i, n, G)
                if g["kind"] == "DN":
                    in_turns, second = g["n"] < 4, down_part(g["n"])[1] == 1
                    if in_turns and g["opens"]:
                        open_bank(g)
                    last = products(g, n, 0, range(g["kt"]), not in_turns and not second,
                                    g["closes"] if in_turns else second, g["tile"])
                else:
                    for t in range(2):
                        if normed is not None and t == 0:
                            for p in range(PAIRS):
                                pe.wait_ge(step("h_ready"), normed + (p + 1))
                                products(g, n, t, range(2 * p, 2 * p + 2), p == 0, p == PAIRS - 1, g["tile"])
                        else:
                            last = products(g, n, t, range(g["kt"]), True, True, g["tile"])
                last.then_inc(group_done, 1)

            def proj_two(b, i, n, G, ready, before, a0, behind):
                for p in range(PAIRS):
                    pe.wait_ge(step(ready), before + (p + 1))
                    for q in (n, n + 1):
                        if p == 0:
                            proj_waits(b, i, q, G)
                            open_bank(G[q])
                        for t in range(2):
                            last = products(G[q], q, t, range(2 * p, 2 * p + 2), False, p == PAIRS - 1 and t == 1, a0)
                        if p == PAIRS - 1:
                            last.then_inc(group_done, 1)
                    if p in behind:
                        behind[p]()

            def mean_pair(b, i, which, *pairs):
                for p in pairs:
                    mean_of_pair(b, i, which, p)

            def mean_of_pair(b, i, which, p):
                pe.wait_ge(step("sq_sum"), norm_count(b, i, which, p + 1))
                for tt in range(TT):
                    last = mm(PS[:, tt, 0:1], sq8[:, 2 * p, tt * P:(tt + 1) * P], ones[:, 0:1], start=p == 0, stop=p == PAIRS - 1)
                if p == PAIRS - 1:
                    last.then_inc(step("ms"), 1)

            MEAN_AT = dict(OUT2=(1, 0), OUT3=(1, 1, 2), DN5=(2, 0), DN9=(2, 1), DN13=(2, 2))

            def scan_mean(i):
                pe.wait_ge(step("yb_sq"), i + 1)
                for tt in range(TT):
                    for k in range(KD):
                        last = mm(pC[:, S + tt:S + tt + 1], sq8[:, k, tt * P:(tt + 1) * P], ones[:, 0:1], start=k == 0, stop=k == KD - 1)
                last.then_inc(step("yb_ms"), 1)

            def spread(ready, value, tile, done):
                pe.wait_ge(step(ready), value)
                for tt in range(TT):
                    last = mm(pC[:, tt * P:(tt + 1) * P], tile[:, tt:tt + 1].to_broadcast([P, P]), ident[:, :], start=True, stop=True)
                last.then_inc(step(done), 1)

            def norm_spread(b, i, which):
                spread("rstd_ready", layer(b, i) * 2 + (which + 1), rstd, "rstd_spread")

            def dt_proj(i):
                pe.wait_ge(step("par_in1"), i * 64 + 64)
                for c in range(TT):
                    for k in range(KD):
                        last = mm(pC[:, 256 + 16 * c:272 + 16 * c], h32[:, k, c * P:(c + 1) * P], dtw[:, k, :],
                                  start=k == 0, stop=k == KD - 1)
                last.then_inc(step("dt_proj"), 1)

            def scan_open(i, c):
                pe.wait_ge(step("dta_ready"), i + 1)
                pe.wait_ge(step("xbc_ready"), i * 6 + 6)
                if c:
                    pe.wait_ge(step("y_taken"), i * 4 + 2)
                    pe.wait_ge(step("prev_ready"), i * 2 + 2)
                t = slice(c * P, (c + 1) * P)
                mm(pC[:, 0:16], tri[:, :], dtA[:, 16 * c:16 * c + 16], start=True, stop=True)
                for g in range(2):
                    mm(pC[:, 128 + 128 * g:256 + 128 * g], xbc[:, 8 + g, t], xbc[:, 10 + g, t], start=True, stop=True)
                    if c == 0:
                        nc.tensor.transpose(pB[:, 0, g * P:(g + 1) * P], xbc[:, 8 + g, t], ident[:, :])
                for k in range(8):
                    last = nc.tensor.transpose(pA[:, k // 4, (k % 4) * P:(k % 4 + 1) * P], xbc[:, k, t], ident[:, :])
                last.then_inc(step("scan_opened"), 1)

            def scan_rows(i, c, g):
                if (c, g) == (0, 0):
                    pe.wait_ge(step("chunk_ready"), i * 2 + 1)
                else:
                    pe.wait_ge(step("rows_taken"), i * 4 + 2 * c + g)
                for h in range(8):
                    last = mm(pB[:, h // 4, (h % 4) * P:(h % 4 + 1) * P],
                              dtA[:, 16 * c + 8 * g + h:16 * c + 8 * g + h + 1].to_broadcast([P, P]), tri[:, :], start=True, stop=True)
                last.then_inc(step("rows_ready"), 1)

            def scan_state(i, g):
                pe.wait_ge(step("xdtd_ready"), i * 2 + g + 1)
                pe.wait_ge(step("chunk_ready"), i * 2 + 1)
                if g:
                    pe.wait_ge(step("prev_ready"), i * 2 + 1)
                mm(pC[:, :], bT[:, g, :], cdec[:, 0:4, :].rearrange("p h t -> p (h t)"), start=True, stop=True).then_inc(step("state_ready"), 1)

            def scan_out(i, c, g):
                pe.wait_ge(step("dec_ready"), i * 4 + 2 * c + g + 1)
                if c:
                    pe.wait_ge(step("cdec_ready"), i * 2 + g + 1)
                for h in range(8):
                    r = slice((h % 2) * 64, (h % 2) * 64 + 64)
                    o = pA[r, g, (h // 2) * P:(h // 2 + 1) * P]
                    last = mm(o, xdt[:, (8 * g + h) * 64:(8 * g + h + 1) * 64], dec[:, h, :], start=True, stop=c == 0)
                    if c:
                        last = mm(o, prev[:, g, h * 64:(h + 1) * 64], cdec[:, h, :], start=False, stop=True)
                last.then_inc(step("y_ready"), 1)

            def gate_turn(i):
                pe.wait_ge(step("chunk_ready"), i * 2 + 2)
                for g in range(4):
                    last = nc.tensor.transpose(pC[:, g * P:(g + 1) * P], wsn[:, g, :], ident[:, :])
                last.then_inc(step("ws_turned"), 1)

            def gate_mix(i):
                pe.wait_ge(step("wsT_ready"), i + 1)
                pe.wait_ge(step("vn_ready"), i + 1)
                pe.wait_ge(step("y_taken"), i * 4 + 4)
                for n in range(TT):
                    for g in range(4):
                        last = mm(pA[:, n, g * P:(g + 1) * P], vg[:, n, g * P:(g + 1) * P], wsT[:, g, :], start=True, stop=True)
                last.then_inc(step("mixed"), 1)

            def attn_turn(i):
                pe.wait_ge(step("qk_normed"), i + 1)
                pe.wait_ge(step("ya32_ready"), i + 1)
                for j in range(8):
                    for tt in range(TT):
                        o = PS[:, j // 2, (j % 2) * S + tt * P:(j % 2) * S + (tt + 1) * P]
                        last = nc.tensor.transpose(o, qk[:, tt, j * P:(j + 1) * P], ident[:, :])
                last.then_inc(step("qk_turned"), 1)

            def attn_scores(i, qt):
                W = (qt + 1) * P
                pe.wait_ge(step("qkT_ready"), i + 1)
                if qt:
                    pe.wait_ge(step("o_taken"), i * 2 + 1)
                for h in range(H1):
                    for m in range(2):
                        r = slice(m * 64, m * 64 + 64)
                        j = 4 * m + h
                        o = PS[:, j * W // 512, j * W % 512:j * W % 512 + W]
                        last = mm(o, qkT[r, h, qt * P:(qt + 1) * P], qkT[r, 4 + h, 0:W], start=True, stop=True)
                last.then_inc(step("scores"), 1)

            def attn_wturn(i, qt):
                pe.wait_ge(step("w_ready"), i * 2 + qt + 1)
                W = (qt + 1) * P
                pw = prob[:, 0:8 * W].rearrange("p (m h k) -> p m h k", h=H1, m=2)
                for h in range(H1):
                    for kt in range(qt + 1):
                        j = h * (qt + 1) + kt
                        last = nc.tensor.transpose(pB[:, j // 4, (j % 4) * P:(j % 4 + 1) * P], pw[:, 0, h, kt * P:(kt + 1) * P], ident[:, :])
                last.then_inc(step("w_turned"), 1)

            def attn_out(i, qt):
                pe.wait_ge(step("wT_ready"), i * 2 + qt + 1)
                for h in range(H1):
                    for kt in range(qt + 1):
                        last = mm(pA[:, 0, h * P:(h + 1) * P], wT[:, h * (qt + 1) + kt, :], vv[:, kt, h * P:(h + 1) * P],
                                  start=kt == 0, stop=kt == qt)
                last.then_inc(step("o_ready"), 1)

            def attn_oturn(i):
                pe.wait_ge(step("o_normed"), i + 1)
                for h in range(H1):
                    for tt in range(TT):
                        last = nc.tensor.transpose(pA[:, h // 2, (h % 2) * S + tt * P:(h % 2) * S + (tt + 1) * P],
                                                   o32[:, tt, h * P:(h + 1) * P], ident[:, :])
                last.then_inc(step("o_turned"), 1)

            def gated_wait(b, i, g):
                if g["name"] in ("DN0", "DN2"):
                    pe.wait_ge(step("up_free"), layer(b, i) * FP + ((DNK + 1) // 2 if g["name"] == "DN0" else FP))

            def stream(b, i, n, G):
                def first(which):
                    behind = {0: lambda: mean_pair(b, i, which, PAIRS - 1), 1: lambda: norm_spread(b, i, which)}
                    return "xg_ready", norm_count(b, i, which, 0), A_XG[which], behind

                firsts = {"XBC0": first(0), "PU0": first(0), "UP0": first(1),
                          "OUT0": ("mg_ready", layer(b, i) * PAIRS, A_MG, {})}
                if G[n]["name"] in firsts:
                    proj_two(b, i, n, G, *firsts[G[n]["name"]])
                elif n == 0 or G[n - 1]["name"] not in firsts:
                    third = G[n]["name"] in ("XBC2", "PU2", "UP2")
                    proj(b, i, n, G, norm_count(b, i, G[n]["kind"] == "UP", 0) if third else None)

            pe.sem_inc(group_done, LOW)
            pe.wait_ge(ident_in, 16)
            pe.wait_ge(x_in, 32)
            for p in range(PAIRS):
                for k in (2 * p, 2 * p + 1):
                    for tt in range(TT):
                        last = nc.tensor.transpose(PS[:, p, (k % 2) * S + tt * P:(k % 2) * S + (tt + 1) * P],
                                                   g01[:, 4 * tt:4 * tt + 4, :].rearrange("p k t -> p (k t)")[:, k * P:(k + 1) * P], ident[:, :])
                last.then_inc(step("x_turned"), 1)
            pe.wait_ge(step("bias_const_in"), 48)
            mm(pC[0:12, :], qkv[0:32, 0:12], qkv[0:32, 512:1024], start=True, stop=True).then_inc(step("bias_product"), 1)
            pe.wait_ge(setup, 3)
            pe.wait_ge(const_in, 48)
            pe.wait_ge(step("bias_row"), 1)
            for p in range(PAIRS - 1):
                mean_pair(1, 0, 0, p)

            with pe.Fori(0, LAYERS) as i:
                after = dict(
                    XBC2=lambda: dt_proj(i),
                    QK0=lambda: scan_open(i, 0), QK1=lambda: scan_rows(i, 0, 0),
                    QK3=lambda: (scan_state(i, 0), scan_out(i, 0, 0), scan_rows(i, 0, 1)),
                    V1=lambda: (scan_state(i, 1), scan_out(i, 0, 1)), Z0=lambda: scan_open(i, 1), Z1=lambda: scan_rows(i, 1, 0),
                    Z3=lambda: (scan_out(i, 1, 0), scan_rows(i, 1, 1)), GV0=lambda: gate_turn(i), GV1=lambda: scan_out(i, 1, 1),
                    GU1=lambda: gate_mix(i), GA0=lambda: scan_mean(i), GA1=lambda: spread("yb_rstd", i + 1, yrstd, "yb_spread"),
                    GA2=lambda: attn_turn(i), GA3=lambda: attn_scores(i, 0), GB1=lambda: attn_wturn(i, 0),
                    GB2=lambda: attn_out(i, 0), GB3=lambda: attn_scores(i, 1), GC2=lambda: attn_wturn(i, 1),
                    GC3=lambda: attn_out(i, 1), BA3=lambda: attn_oturn(i))
                before = dict(BA0="ya_ready", BB0="yb_ready", BC0="yc_ready")
                for n, g in enumerate(G1):
                    if g["name"] in before:
                        pe.wait_ge(step(before[g["name"]]), i + 1)
                    gated_wait(1, i, g)
                    stream(1, i, n, G1)
                    if g["name"] in after:
                        after[g["name"]]()
                    if g["name"] in MEAN_AT:
                        mean_pair(1, i, *MEAN_AT[g["name"]])

            def pool_mix(i):
                pe.wait_ge(step("pu_ready"), i + 1)
                pe.wait_ge(step("par_in2"), i * 32 + 32)
                for k in range(KD):
                    for s in range(TT):
                        t0 = max(s * P - MAX_WINDOW // 2, 0)
                        last = mm(PS[:, k // 2, (k % 2) * S + t0:(k % 2 + 1) * S], uview[:, s, k * P:(k + 1) * P],
                                  band(s)[:, (k // 2) * S + t0:(k // 2 + 1) * S], start=s == 0, stop=s == TT - 1)
                last.then_inc(step("pooled"), 1)

            uview = ug[:, :, :].rearrange("p k t -> p (k t)").rearrange("p (a c) -> p a c", a=TT)

            def b2_scores(i, u):
                j, qt = u // 2, u % 2
                if u == 0:
                    pe.wait_ge(step("qk2_ready"), i + 1)
                    pe.wait_ge(step("pd_ready"), i + 1)
                else:
                    pe.wait_ge(step("b2_PT_ready"), i * 8 + u)
                px = PS[:, 2 * (u % 2):2 * (u % 2) + 2, :]
                for g in range(3):
                    last = mm(px[:, g // 2, (g % 2) * S:(g % 2 + 1) * S], xbc[:, 4 * g + j, qt * P:(qt + 1) * P],
                              g01[:, 4 * g + j, :], start=True, stop=True)
                last.then_inc(step("b2_scores"), 1)

            def b2_turn(i, u):
                pe.wait_ge(step("b2_P_ready"), i * 8 + u + 1)
                px = PS[:, 2 * (u % 2):2 * (u % 2) + 2, :]
                for k in range(6):
                    last = nc.tensor.transpose(px[:, k // 4, (k % 4) * P:(k % 4 + 1) * P], b2_P[:, k * P:(k + 1) * P], ident[:, :])
                last.then_inc(step("b2_turned"), 1)

            def b2_values(i, j):
                pe.wait_ge(step("b2_PT_ready"), i * 8 + 2 * j + 2)
                if j:
                    pe.wait_ge(step("at_lo"), i * 4 + j)
                else:
                    pe.wait_ge(step("v2_ready"), i + 1)
                v2 = qkv[:, :].rearrange("p (a c) -> p a c", a=TT)
                for g in range(3):
                    for kt in range(TT):
                        last = mm(pC[:, 0:S], v2[:, kt, (4 * g + j) * P:(4 * g + j + 1) * P], b2_PT[:, 2 * g + kt, :],
                                  start=(g, kt) == (0, 0), stop=(g, kt) == (2, 1))
                last.then_inc(step("b2_out"), 1)

            with pe.Fori(0, LAYERS) as i:
                before = dict(WP0="pd_ready", WA0="po_ready", WB0="at_ready")
                for n, g in enumerate(G2):
                    if g["name"] in before:
                        pe.wait_ge(step(before[g["name"]]), i + 1)
                    gated_wait(2, i, g)
                    stream(2, i, n, G2)
                    if g["name"] in MEAN_AT:
                        mean_pair(2, i, *MEAN_AT[g["name"]])
                    if g["name"] == "Q0":
                        pool_mix(i)
                    if g["name"] in PV_AT:
                        b2_values(i, PV_AT[g["name"]])
                    if g["name"] in SC_AT:
                        b2_scores(i, SC_AT[g["name"]])
                    if g["name"] in TR_AT:
                        b2_turn(i, TR_AT[g["name"]])

            mean_pair(2, LAYERS, 0, PAIRS - 1)
            norm_spread(2, LAYERS, 0)
            for p in range(PAIRS):
                pe.wait_ge(step("f_normed"), p + 1)
                for tt in range(TT):
                    for k in (2 * p, 2 * p + 1):
                        last = nc.tensor.transpose(PS[:, 2 * tt + k // 4, (k % 4) * P:(k % 4 + 1) * P], h32[:, k, tt * P:(tt + 1) * P], ident[:, :])
                    if p == PAIRS - 1:
                        last.then_inc(step("out_turned"), 1)

        @block.scalar
        def _(act):
            A = nc.scalar.activation

            def split_behind(b, i, n, G):
                for q in SPLITS[b].get(n, ()):
                    high_part(act, b, i, q, G)

            def squares(b, i, ready, done, src):
                act.wait_ge(step(ready), layer(b, i) + 1)
                A(sq8, src, ACT.Square).then_inc(step(done), 1)

            def pair_square(b, i, which, p):
                act.wait_ge(step("x_pair"), norm_count(b, i, which, p + 1))
                t = slice(2 * p, 2 * p + 2)
                A(sq8[:, t, :], x[:, t, :], ACT.Square).then_inc(step("sq"), 1)

            def xg_high(b, i, which, p):
                t = slice(2 * p, 2 * p + 2)
                a0 = A_XG[which % 2]
                split_high(i, "xg32", norm_count(b, i, which, p + 1), slice(a0 + 2 * p, a0 + 2 * p + 2), h32[:, t, :], "xg_hi")

            def residual(b, i, g):
                if g["kind"] == "OUT" or g["kind"] == "DN" and g["closes"]:
                    which, p = (1, g["n"]) if g["kind"] == "OUT" else (2, g["n"] // 4)
                    pair_square(b, i, which, p)
                    xg_high(b, i, which, p)

            def root(ms, value, src, tile, done):
                act.wait_ge(step(ms), value)
                A(tile[:, :], src, ACT.Sqrt, bias=eps).then_inc(step(done), 1)

            def norm_root(b, i, which):
                root("ms", layer(b, i) * 2 + (which + 1), PS[:, 0:2, 0:1].rearrange("p a c -> p (a c)"), rstd, "root")

            def root_table():
                A(root_scratch, eps, ACT.Sqrt)

            def merged_high(b, i, m, merged):
                t = slice(A_MG + 2 * m, A_MG + 2 * m + 2)
                split_high(i, "mg32_ready", layer(b, i) * PAIRS + (m + 1), t, merged[:, 2 * m:2 * m + 2, :], "mg_hi")

            def small_root(i, sums, tile, n, done):
                act.wait_ge(step(sums), i + 1)
                A(tile, tile, ACT.Sqrt, scale=1.0 / n, bias=eps).then_inc(step(done), 1)

            def split_high(i, ready, value, tiles, src, done):
                act.wait_ge(step(ready), value)
                A(ahi[:, tiles, :], src, ACT.Copy).then_inc(step(done), 1)

            def norm_high(b, i, which, a0):
                for p in range(PAIRS):
                    split_high(i, "h32_ready", norm_count(b, i, which, p + 1), slice(a0 + 2 * p, a0 + 2 * p + 2),
                               h32[:, 2 * p:2 * p + 2, :], "h_hi")

            def bank(g):
                return PJ[:, g["bank"], :]

            def arrived(b, i, n):
                g = (G1 if b == 1 else G2)[n]
                if g["kind"] in ("XBC", "UP") and g["n"] < 2:
                    act.wait_ge(step("banks_scaled"), scaled_count(b, i, g))
                else:
                    act.wait_ge(group_done, count(b, i, n + 1))

            def conv_open(b, i, g, wkey, bkey, taps, tap, tiles, dst, done):
                for t in range(2):
                    last = A(dst[t], bank(g)[:, t * S:(t + 1) * S], ACT.Identity, bias=col(b, bkey, tiles[t]),
                             scale=col(b, wkey, tiles[t] * taps + tap))
                last.then_inc(step(done), 1)

            act.sem_inc(taken["act"], 1)
            act.dma_start(qkv[0:32, 0:12], C["rel_bias_2"]).then_inc(step("bias_const_in"), 16)
            act.dma_start(qkv[0:32, 512:1024], C["c_onehot"]).then_inc(step("bias_const_in"), 16)
            act.dma_start(qkv[0:12, 1024:1536], C["c_offmask"]).then_inc(step("bias_const_in"), 16)
            act.wait_ge(ident_in, 16)
            A(zero[:, :], ident[:, 0:P // 2], ACT.Copy, scale=0.0).then_inc(setup, 1)
            for p in range(PAIRS):
                pair_square(1, 0, 0, p)
                xg_high(1, 0, 0, p)
                if p >= PAIRS - AHEAD:
                    high_part(act, 1, 0, p - (PAIRS - AHEAD), G1)
            act.wait_ge(step("bias_row"), 1)
            act.dma_start(C["bias_table"].rearrange("h (c o) -> h c o", o=511),
                          qkv[0:12, 1536:2047].unsqueeze(1).to_broadcast([12, 129, 511])).then_inc(step("bias_stored"), 16)
            with act.Fori(0, LAYERS) as i:
                split_behind(1, i, -1, G1)
                norm_root(1, i, 0)
                norm_high(1, i, 0, A_H)

                def dt_exp():
                    act.wait_ge(step("dt_abs"), i + 1)
                    A(dte, dta, ACT.Exp, scale=-1.0).then_inc(step("dt_exp"), 1)
                    A(aexp, row("alog"), ACT.Exp).then_inc(step("a_exp"), 1)

                def dt_ln():
                    act.wait_ge(step("dt_one"), i + 1)
                    A(dtl, dtu, ACT.Ln).then_inc(step("dt_ln"), 1)

                def xbc_silu(n):
                    act.wait_ge(step("xbc_conv"), i * 6 + n + 1)
                    v = xbc[:, 2 * n:2 * n + 2, :]
                    A(v, v, ACT.Silu).then_inc(step("xbc_ready"), 1)

                def rows_exp(c, g):
                    act.wait_ge(step("seg_ready"), i * 4 + 2 * c + g + 1)
                    A(dec, dec, ACT.Exp).then_inc(step("dec_exp"), 1)
                    if c == 0:
                        A(dend, dend, ACT.Exp).then_inc(step("dend_exp"), 1)
                    else:
                        if g:
                            act.wait_ge(step("y_ready"), i * 4 + 3)
                        else:
                            act.wait_ge(step("state_ready"), i * 2 + 2)
                        A(cdec, pB.rearrange("p a (h t) -> p (a h) t", t=P), ACT.Exp).then_inc(step("cdec_exp"), 1)

                def gm_square():
                    act.wait_ge(step("vg_ready"), i + 1)
                    for tt in range(TT):
                        A(wsT[:, :, :].rearrange("p g t -> p (g t)"), vg[:, tt, :], ACT.Square, accum_out=gms[:, tt:tt + 1])
                        if tt == 0:
                            act.drain()
                    act.drain()
                    A(gms, gms, ACT.Sqrt, scale=1.0 / 512, bias=eps).then_inc(step("gm_root"), 1)

                def lam_exp():
                    act.wait_ge(step("lam_sums"), i + 1)
                    A(lms, lms, ACT.Exp).then_inc(step("lam_exp"), 1)

                def yb_square():
                    squares(1, i, "yz_ready", "yb_sq", xbc[:, 0:8, :])

                def qk_square():
                    act.wait_ge(step("y_ready"), i * 4 + 4)
                    act.wait_ge(step("qk_in"), i + 1)
                    A(prob, qkv[:, 0:2048], ACT.Square).then_inc(step("qk_sq"), 1)

                def qk_copy():
                    act.wait_ge(step("qk_turned"), i + 1)
                    A(qkT, PS[:, 0:4, :].rearrange("p a (j t) -> p (a j) t", t=S), ACT.Copy).then_inc(step("qkT_ready"), 1)

                def attn_exp(qt):
                    W = (qt + 1) * P
                    act.wait_ge(step("max_ready"), i * 2 + qt + 1)
                    for j in range(8):
                        v = prob[:, j * W:(j + 1) * W]
                        last = A(v, v, ACT.Exp, bias=nb[:, j:j + 1], scale=0.125, accum_out=ps_[:, j:j + 1])
                    last.then_inc(step("attn_exp"), 1)

                def o_square():
                    act.wait_ge(step("o_taken"), i * 2 + 2)
                    A(prob[:, 0:1024], qkv[:, 0:1024], ACT.Square).then_inc(step("o_sq"), 1)

                def yc_high():
                    act.wait_ge(step("o_turned"), i + 1)
                    A(ahi[:, A_YC:A_YC + 4, :], pA.rearrange("p a (j t) -> p (a j) t", t=S), ACT.Copy).then_inc(step("yc_hi"), 1)

                early = dict(GA2=qk_copy, BA3=yc_high)
                after = dict(
                    XBC1=lambda: xbc_silu(0), XBC2=lambda: (xbc_silu(1), dt_exp()), XBC3=lambda: (xbc_silu(2), dt_ln()),
                    XBC4=lambda: xbc_silu(3), XBC5=lambda: (xbc_silu(4), xbc_silu(5)),
                    QK1=lambda: rows_exp(0, 0), QK2=lam_exp, QK3=lambda: rows_exp(0, 1),
                    Z1=lambda: rows_exp(1, 0), Z3=lambda: rows_exp(1, 1), GV1=gm_square, GU0=qk_square,
                    GU1=lambda: (small_root(i, "qk_sums", qs, 64, "qk_root"), yb_square()),
                    GA0=lambda: (split_high(i, "ya32_ready", i + 1, slice(A_YA, A_YA + 4), uu, "ya_hi"), root("yb_ms", i + 1, pC[:, S:S + TT], yrstd, "yb_root")),
                    GA2=lambda: split_high(i, "yb32_ready", i + 1, slice(A_YB, A_YB + 8), xbc[:, 0:8, :], "yb_hi"),
                    GA3=lambda: attn_exp(0), GB3=lambda: attn_exp(1), GC3=o_square,
                    BA0=lambda: small_root(i, "o_sums", os_, P, "o_root"))

                def take(n, g):
                    kind, m = g["kind"], g["n"]
                    if g["taker"] == "act" or kind in ("XBC", "UP"):
                        arrived(1, i, n)
                    pair = bank(g).rearrange("p (k t) -> p k t", t=S)
                    if kind == "XBC":
                        conv_open(1, i, g, "cw", "cb", 4, 3, (2 * m, 2 * m + 1), (xbc[:, 2 * m, :], xbc[:, 2 * m + 1, :]), "xbc_open")
                    elif kind == "QK":
                        if m == 0:
                            act.wait_ge(step("bias_stored"), 16)
                        last = A(qk[:, :, 256 * m:256 * m + 256], pair, ACT.Copy)
                        last.then_inc(taken["act"], 1)
                        if m == 3:
                            act.drain().then_inc(step("qk_in"), 1)
                    elif kind == "V":
                        A(vv[:, :, 256 * m:256 * m + 256], pair, ACT.Copy).then_inc(taken["act"], 1)
                        if m == 1:
                            act.drain().then_inc(step("v_in"), 1)
                    elif kind == "GV":
                        A(vg[:, :, 256 * m:256 * m + 256], pair, ACT.Gelu_apprx_tanh).then_inc(taken["act"], 1)
                        if m == 1:
                            act.drain().then_inc(step("vg_ready"), 1)
                    elif kind == "GU":
                        A(uu[:, 2 * m:2 * m + 2, :], pair, ACT.Gelu_apprx_tanh).then_inc(taken["act"], 1)
                        if m == 1:
                            act.drain().then_inc(step("u_ready"), 1)
                    elif kind == "Z":
                        A(SZ[:, 2 * m:2 * m + 2, :], pair, ACT.Silu).then_inc(taken["act"], 1)
                        if m == 3:
                            act.drain().then_inc(step("z_ready"), 1)
                    elif kind in ("GA", "GB", "GC"):
                        if kind == "GB" and m == 0:
                            act.wait_ge(step("ya_ready"), i + 1)
                        if kind == "GC" and m == 0:
                            act.wait_ge(step("yb_ready"), i + 1)
                        if kind == "GA" and m == 0:
                            act.wait_ge(step("mixed"), i + 1)
                        reg = dict(GA=G0, GB=ug[:, :, :], GC=SZ)[kind]
                        A(reg[:, 2 * m:2 * m + 2, :], pair, ACT.Sigmoid).then_inc(taken["act"], 1)
                    elif kind == "UP":
                        up_open(1, i, g)

                def up_open(b, i, g):
                    m, val = g["n"] // 2, g["n"] % 2
                    if g["n"] >= 4:
                        act.wait_ge(step("up_free"), layer(b, i) * FP + m - 1)
                    buf = ypair(m % 2, val)
                    t0 = 2 * m + val * FT
                    conv_open(b, i, g, "fw", "fb", 3, 2 if b == 1 else 1, (t0, t0 + 1), (buf[:, 0, :], buf[:, 1, :]), f"up_open{b}")

                def up_act(b, i, m, func):
                    act.wait_ge(step("up_conv"), layer(b, i) * FP + m + 1)
                    v = ypair(m % 2, 0)
                    A(v, v, func).then_inc(step("up_act"), 1)

                def gated_high(b, i, m):
                    split_high(i, "gated32", layer(b, i) * FP + m + 1, slice(A_G + 2 * m, A_G + 2 * m + 2), ypair(m % 2, 0), "gated_hi")

                for n, g in enumerate(G1):
                    if g["name"] == "UP0":
                        norm_root(1, i, 1)
                        norm_high(1, i, 1, A_H2)
                    if g["name"] in FIRST:
                        split_behind(1, i, n, G1)
                    take(n, g)
                    if g["name"] in early:
                        early[g["name"]]()
                    if g["name"] == "BB3":
                        merged_high(1, i, g["n"], G0)
                    if g["name"] == "OUT3":
                        residual(1, i, g)
                    if g["name"] not in FIRST:
                        split_behind(1, i, n, G1)
                    if g["name"] != "OUT3":
                        residual(1, i, g)
                    if g["name"] in MERGED and g["name"] != "BB3":
                        merged_high(1, i, g["n"], G0)
                    if g["name"] == "DN0":
                        root_table()
                    if g["name"] in after:
                        after[g["name"]]()
                    if g["kind"] == "UP":
                        if g["n"] % 2 == 1:
                            up_act(1, i, g["n"] // 2, ACT.Silu)
                        elif g["n"] >= 2:
                            gated_high(1, i, g["n"] // 2 - 1)
                        if g["n"] == 2 * FP - 1:
                            gated_high(1, i, FP - 1)

            with act.Fori(0, LAYERS) as i:
                split_behind(2, i, -1, G2)
                norm_root(2, i, 0)
                norm_high(2, i, 0, A_H)
                uview = ug[:, :, :].rearrange("p k t -> p (k t)").rearrange("p (a c) -> p a c", a=TT)
                v2 = qkv[:, :].rearrange("p (a c) -> p a c", a=TT)

                def b2_exp(u):
                    act.wait_ge(step("b2_max"), i * 8 + u + 1)
                    A(b2_P, b2_P, ACT.Exp, bias=bnm[:, 0:1], accum_out=bsm[:, 0:1]).then_inc(step("b2_exp"), 1)

                def b2_PT_copy(u):
                    act.wait_ge(step("b2_turned"), i * 8 + u + 1)
                    if u >= 2 and u % 2 == 0:
                        act.wait_ge(step("b2_out"), i * 4 + u // 2)
                    px = PS[:, 2 * (u % 2):2 * (u % 2) + 2, :].rearrange("p a c -> p (a c)")[:, 0:768]
                    A(b2_PT[:, :, (u % 2) * P:(u % 2 + 1) * P], px.rearrange("p (k q) -> p k q", q=P), ACT.Copy).then_inc(step("b2_PT_ready"), 1)

                def at_high(j):
                    act.wait_ge(step("b2_out"), i * 4 + j + 1)
                    A(ahi[:, A_AT + j, :], pC[:, 0:S], ACT.Copy).then_inc(step("at_hi"), 1)

                def pd_high():
                    act.wait_ge(step("pooled"), i + 1)
                    A(ahi[:, A_PD:A_PD + 8, :], PS[:, 0:4, :].rearrange("p a (k t) -> p (a k) t", t=S), ACT.Copy).then_inc(step("pd_hi"), 1)

                def take2(n, g):
                    kind, m = g["kind"], g["n"]
                    if g["taker"] == "act" or kind in ("WP", "UP"):
                        arrived(2, i, n)
                    pair = bank(g).rearrange("p (k t) -> p k t", t=S)
                    if kind == "PU" and m < 2:
                        act.wait_ge(step("rstd_ready"), layer(2, i) * 2 + 1)
                        for tt in range(TT):
                            last = A(uview[:, tt, 256 * m:256 * m + 256], pair[:, tt, :], ACT.Copy, scale=rstd[:, tt:tt + 1])
                        last.then_inc(taken["act"], 1)
                    elif kind == "PU":
                        A(uview[:, :, 256 * m:256 * m + 256], pair, ACT.Copy).then_inc(taken["act"], 1)
                        if m == 3:
                            act.drain().then_inc(step("pu_ready"), 1)
                    elif kind == "Q":
                        if m == 0:
                            act.wait_ge(step("pooled"), i + 1)
                        A(xbc[:, 2 * m:2 * m + 2, :], pair, ACT.Copy).then_inc(taken["act"], 1)
                    elif kind == "K":
                        A(g01[:, 2 * m:2 * m + 2, :], pair, ACT.Copy).then_inc(taken["act"], 1)
                        if m == 5:
                            act.drain().then_inc(step("qk2_ready"), 1)
                    elif kind == "V":
                        A(v2[:, :, 256 * m:256 * m + 256], pair, ACT.Copy).then_inc(taken["act"], 1)
                        if m == 5:
                            act.drain().then_inc(step("v2_ready"), 1)
                    elif kind in ("GP", "GT"):
                        if kind == "GT" and m in (0, 3):
                            act.wait_ge(step("b2_scores"), i * 8 + (6 if m else 4))
                        A(gate_t(m) if kind == "GT" else ug[:, 2 * m:2 * m + 2, :], pair, ACT.Sigmoid).then_inc(taken["act"], 1)
                    elif kind == "WP":
                        for t in range(2):
                            last = A(ahi[:, A_PO + 2 * m + t, :], pair[:, t, :], ACT.Copy, scale=col(2, "ps", 2 * m + t))
                        last.then_inc(step("po_hi"), 1)
                    elif kind == "UP" and m % 2 == 0:
                        up_open(2, i, g)

                for n, g in enumerate(G2):
                    if g["name"] == "UP0":
                        norm_root(2, i, 1)
                        norm_high(2, i, 1, A_H2)
                    if g["name"] in FIRST:
                        split_behind(2, i, n, G2)
                    take2(n, g)
                    if g["name"] in PV_AT:
                        at_high(PV_AT[g["name"]])
                    if g["name"] in TR_AT:
                        b2_PT_copy(TR_AT[g["name"]])
                    if g["name"] == "WA3":
                        merged_high(2, i, g["n"], ug)
                    if g["name"] == "OUT3":
                        residual(2, i, g)
                    if g["name"] not in FIRST:
                        split_behind(2, i, n, G2)
                    if g["name"] != "OUT3":
                        residual(2, i, g)
                    if g["name"] in MERGED and g["name"] != "WA3":
                        merged_high(2, i, g["n"], ug)
                    if g["name"] in ("WB0", "DN0"):
                        root_table()
                    if g["name"] == "Q0":
                        pd_high()
                    if g["name"] in SC_AT:
                        b2_exp(SC_AT[g["name"]])
                    if g["kind"] == "UP":
                        if g["n"] % 2 == 0:
                            up_act(2, i, g["n"] // 2, ACT.Gelu_apprx_tanh)
                        else:
                            gated_high(2, i, g["n"] // 2)
            norm_root(2, LAYERS, 0)
            act.wait_ge(step("out_turned"), 2)
            A(g01[:, 4:8, :].rearrange("p k t -> p (k t)"), pB.rearrange("p a c -> p (a c)"), ACT.Copy).then_inc(step("out_ready_1"), 1)

        @block.vector
        def _(dve):
            V = nc.vector
            TTo = V.tensor_tensor
            STT = V.scalar_tensor_tensor

            def ordered():
                dve.drain()

            def rstd_of(root, value, tile, done):
                dve.wait_ge(step(root), value)
                V.reciprocal(tile[:, :], tile[:, :]).then_inc(step(done), 1)

            spread_rstd = pC[:, 0:S]

            def norm_rstd(count):
                rstd_of("root", count, rstd, "rstd_ready")
                dve.wait_ge(step("rstd_spread"), count)
                V.tensor_copy(rstd_all[:, :], spread_rstd)
                ordered()

            def xg_scaled(b, i, which, p):
                for k in (2 * p, 2 * p + 1):
                    last = V.tensor_scalar(h32[:, k, :], x[:, k, :], col(b, "norm2" if which == 1 else "norm1", k), None, ALU.mult)
                last.then_inc(step("xg32"), 1)

            def xg_low(b, i, which, p):
                t = slice(A_XG[which % 2] + 2 * p, A_XG[which % 2] + 2 * p + 2)
                split_low("xg_hi", norm_count(b, i, which, p + 1), t, h32[:, 2 * p:2 * p + 2, :], "xg_ready")

            def normed(p, done):
                v = h32[:, 2 * p:2 * p + 2, :]
                TTo(v, v, bc(rstd_all[:, :], [P, 2, S], 1), ALU.mult).then_inc(step(done), 1)

            def norm(b, i, which, a0):
                norm_rstd(layer(b, i) * 2 + (which + 1))
                normed(0, "h32_ready")
                normed(1, "h32_ready")
                for p in range(PAIRS):
                    t = slice(a0 + 2 * p, a0 + 2 * p + 2)
                    split_low("h_hi", norm_count(b, i, which, p + 1), t, h32[:, 2 * p:2 * p + 2, :], "h_ready")
                    if p + 2 < PAIRS:
                        normed(p + 2, "h32_ready")

            def split_behind(b, i, n, G):
                for q in SPLITS[b].get(n, ()):
                    low_part(V, b, i, q, G, False)

            def scale_bank(b, i, n, g):
                arrived(b, i, n)
                v = bank(g).rearrange("p (k t) -> p k t", t=S)
                TTo(v, v, bc(rstd_all[:, :], [P, 2, S], 1), ALU.mult).then_inc(step("banks_scaled"), 1)
                ordered()

            def split_low(hi, value, tiles, src, done):
                dve.wait_ge(step(hi), value)
                TTo(alo[:, tiles, :], src, ahi[:, tiles, :].bitcast(f32), ALU.subtract).then_inc(step(done), 1)

            def bank(g):
                return PJ[:, g["bank"], :]

            def arrived(b, i, n):
                dve.wait_ge(group_done, count(b, i, n + 1))

            def conv_taps(b, i, g, wkey, taps, shifts, tiles, dst):
                for tap, sh in shifts:
                    for t in range(2):
                        src = bank(g)[:, t * S:(t + 1) * S]
                        o, s = (slice(sh, S), slice(0, S - sh)) if sh > 0 else (slice(0, S + sh), slice(-sh, S))
                        last = STT(dst[t][:, o], src[:, s], col(b, wkey, tiles[t] * taps + tap), dst[t][:, o], ALU.mult, ALU.add)
                    if (tap, sh) != shifts[-1]:
                        ordered()
                return last

            def params_used():
                dve.drain().then_inc(step("layer_done"), 1)

            def merged_low(b, i, m, merged):
                for q in ((m - 1,) if m < PAIRS - 1 else (m - 1, m)):
                    if q >= 0:
                        split_low("mg_hi", layer(b, i) * PAIRS + (q + 1), slice(A_MG + 2 * q, A_MG + 2 * q + 2),
                                  merged[:, 2 * q:2 * q + 2, :], "mg_ready")

            dve.sem_inc(taken["dve"], 1)
            dve.sem_inc(step("b2_bias_free"), 1)
            dve.sem_inc(step("layer_done"), 1)
            for p in range(PAIRS):
                dve.wait_ge(step("x_turned"), p + 1)
                V.tensor_copy(x[:, 2 * p:2 * p + 2, :], PS[:, p, :].rearrange("p (k t) -> p k t", t=S)).then_inc(step("x_pair"), 1)
                ordered()
                if p == 0:
                    dve.wait_ge(step("cols_in"), 16)
                xg_scaled(1, 0, 0, p)
            dve.wait_ge(step("bias_product"), 1)
            TTo(qkv[0:12, 1536:2048], pC[0:12, :], qkv[0:12, 1024:1536], ALU.add).then_inc(step("bias_row"), 1)

            for p in range(PAIRS):
                xg_low(1, 0, 0, p)
                if p >= PAIRS - AHEAD:
                    low_part(V, 1, 0, p - (PAIRS - AHEAD), G1, False)

            with dve.Fori(0, LAYERS) as i:
                split_behind(1, i, -1, G1)
                norm(1, i, 0, A_H)

                def dt_abs():
                    dve.wait_ge(step("dt_proj"), i + 1)
                    dve.wait_ge(step("par_in1"), i * 64 + 64)
                    TTo(dtx.rearrange("p (c h) -> p c h", c=TT), pC[:, 256:288].rearrange("p (c h) -> p c h", c=TT),
                        bc(row("dtb"), [P, TT, 16], 1), ALU.add)
                    ordered()
                    STT(dta, dtx, -1.0, dtx, ALU.mult, ALU.max).then_inc(step("dt_abs"), 1)

                def dt_one():
                    dve.wait_ge(step("dt_exp"), i + 1)
                    V.tensor_scalar(dtu, dte, 1.0, None, ALU.add).then_inc(step("dt_one"), 1)

                def dt_finish():
                    dve.wait_ge(step("dt_ln"), i + 1)
                    STT(dtv, dtu, -1.0, dte, ALU.add, ALU.subtract)
                    STT(dtx, dtx, 0.0, dtl, ALU.max, ALU.add)
                    V.reciprocal(dta, dtu)
                    ordered()
                    TTo(dtv, dtv, dta, ALU.mult)
                    ordered()
                    TTo(dtv, dtx, dtv, ALU.subtract)
                    ordered()
                    dve.wait_ge(step("a_exp"), i + 1)
                    STT(dtA.rearrange("p (c h) -> p c h", c=TT), dtv.rearrange("p (c h) -> p c h", c=TT), -1.0,
                        bc(aexp, [P, TT, 16], 1), ALU.mult, ALU.mult).then_inc(step("dta_ready"), 1)

                def lam_sums():
                    lv = lam_row.rearrange("p (a b d) -> p a b d", a=2, b=2)
                    TTo(lmp.rearrange("p (a d) -> p a d", a=2), lv[:, :, 0, :], lv[:, :, 1, :], ALU.mult)
                    ordered()
                    V.tensor_reduce(lms, lmp.rearrange("p (a d) -> p a d", a=2), AX.X, ALU.add).then_inc(step("lam_sums"), 1)

                def lam_value():
                    dve.wait_ge(step("lam_exp"), i + 1)
                    TTo(lmv, lms[:, 0:1], lms[:, 1:2], ALU.subtract)
                    ordered()
                    TTo(lmv, lmv, row("li")[:, 0:1], ALU.add)

                def chunk_open(c):
                    dve.wait_ge(step("scan_opened"), i * 2 + c + 1)
                    V.tensor_copy(acum, pC[:, 0:16])
                    for g in range(2):
                        TTo(cbm[:, g, :], pC[:, 128 + 128 * g:256 + 128 * g], tri[:, :], ALU.mult)
                    if c == 0:
                        V.tensor_copy(bT[:, :, :], pB[:, 0, 0:256].rearrange("p (g n) -> p g n", g=2))
                    else:
                        pass
                    TTo(xdt.rearrange("p (h q) -> p h q", q=64), pA.rearrange("p a (h q) -> p (a h) q", q=64),
                        bc(dtv[:, 16 * c:16 * c + 16], [P, 16, 64], 2), ALU.mult).then_inc(step("chunk_ready"), 1)

                def seg(c, g):
                    dve.wait_ge(step("rows_ready"), i * 4 + 2 * c + g + 1)
                    if (c, g) != (0, 0):
                        dve.wait_ge(step("y_ready"), i * 4 + 2 * c + g)
                    rows = pB.rearrange("p a (h t) -> p (a h) t", t=P)
                    TTo(dec, rows, bc(acum[:, 8 * g:8 * g + 8], [P, 8, P], 2), ALU.subtract)
                    if c == 0:
                        TTo(dend, rows[:, :, P - 1], acum[:, 8 * g:8 * g + 8], ALU.subtract)
                    ordered()
                    V.tensor_scalar(dec, dec, 0.0, None, ALU.min).then_inc(step("seg_ready"), 1)

                def dec_mul(c, g):
                    dve.wait_ge(step("dec_exp"), i * 4 + 2 * c + g + 1)
                    last = TTo(dec, dec, bc(cbm[:, g, :], [P, 8, P], 1), ALU.mult)
                    last.then_inc(step("dec_ready"), 1)
                    if c == 0:
                        dve.wait_ge(step("dend_exp"), i * 2 + g + 1)
                        if g:
                            dve.wait_ge(step("state_ready"), i * 2 + 1)
                        TTo(cdec[:, 0:4, :].rearrange("p h t -> p (h t)").rearrange("p (h q) -> p h q", q=64),
                            xdt[:, 512 * g:512 * g + 512].rearrange("p (h q) -> p h q", q=64),
                            bc(dend, [P, 8, 64], 2), ALU.mult).then_inc(step("xdtd_ready"), 1)
                    else:
                        dve.wait_ge(step("cdec_exp"), i * 2 + g + 1)
                        TTo(cdec, cdec, bc(xbc[:, 10 + g, P:2 * P], [P, 8, P], 1), ALU.mult).then_inc(step("cdec_ready"), 1)
                    rows_release()

                def rows_release():
                    ordered()
                    V.tensor_copy(gmr[:, 0:1], acum[:, 0:1]).then_inc(step("rows_taken"), 1)

                def state_copy(g):
                    dve.wait_ge(step("state_ready"), i * 2 + g + 1)
                    V.tensor_copy(prev[:, g, :], pC[:, :]).then_inc(step("prev_ready"), 1)

                def y_take(c, g):
                    dve.wait_ge(step("y_ready"), i * 4 + 2 * c + g + 1)
                    for k in range(4):
                        v = xbc[:, 4 * g + k, c * P:(c + 1) * P]
                        last = STT(v, v, col(1, "sd", 4 * g + k), pA[:, g, k * P:(k + 1) * P], ALU.mult, ALU.add)
                    last.then_inc(step("y_taken"), 1)

                def gm_norm():
                    dve.wait_ge(step("gm_root"), i + 1)
                    V.reciprocal(gmr, gms)
                    ordered()
                    for tt in range(TT):
                        last = STT(vg[:, tt, :], vg[:, tt, :], gmr[:, tt:tt + 1], row("gvg"), ALU.mult, ALU.mult)
                    last.then_inc(step("vn_ready"), 1)
                    dve.wait_ge(step("ws_turned"), i + 1)
                    TTo(wsT[:, :, :], pC.rearrange("p (g t) -> p g t", g=4), bc(tri[:, :], [P, 4, P], 1), ALU.mult).then_inc(step("wsT_ready"), 1)

                def gm_out():
                    dve.wait_ge(step("mixed"), i + 1)
                    dve.wait_ge(step("u_ready"), i + 1)
                    t512 = vg
                    for n in range(TT):
                        TTo(t512[:, n, :], pA[:, n, :], row("gb"), ALU.add)
                    ordered()
                    for n in range(TT):
                        v = uu[:, :, n * P:(n + 1) * P]
                        last = TTo(v, v, t512[:, n, :].rearrange("p (g t) -> p g t", g=4), ALU.mult)
                    last.then_inc(step("ya32_ready"), 1)

                def yz():
                    dve.wait_ge(step("z_ready"), i + 1)
                    TTo(xbc[:, 0:8, :], xbc[:, 0:8, :], SZ, ALU.mult).then_inc(step("yz_ready"), 1)

                def yb_norm():
                    dve.wait_ge(step("yb_spread"), i + 1)
                    for k in range(KD):
                        last = STT(xbc[:, k, :], xbc[:, k, :], col(1, "sg", k), spread_rstd, ALU.mult, ALU.mult)
                    last.then_inc(step("yb32_ready"), 1)

                def qk_sums():
                    dve.wait_ge(step("qk_sq"), i + 1)
                    V.tensor_reduce(qs, prob.rearrange("p (j d) -> p j d", d=64), AX.X, ALU.add).then_inc(step("qk_sums"), 1)

                def qk_norm():
                    v = qk.rearrange("p a (j d) -> p (a j) d", d=64)
                    dve.wait_ge(step("qk_root"), i + 1)
                    V.reciprocal(qr, qs)
                    ordered()
                    TTo(v, v, bc(qr, [P, 32, 64], 2), ALU.mult)
                    ordered()
                    for tt in range(TT):
                        for m, key in ((0, "qg"), (1, "kg")):
                            w = qk[:, tt, 512 * m:512 * m + 512].rearrange("p (j d) -> p j d", d=64)
                            TTo(w, w, bc(row(key), [P, 8, 64], 1), ALU.mult)

                def qk_rope():
                    ordered()
                    v = qk.rearrange("p a (j d) -> p (a j) d", d=64)
                    r4 = [prob[:, 256 * q:256 * q + 256].rearrange("p (j d) -> p j d", d=8) for q in range(4)]
                    for tt in range(TT):
                        w = qk[:, tt, :].rearrange("p (j d) -> p j d", d=64)
                        t1, t2 = w[:, :, 0:8], w[:, :, 8:16]
                        cs, sn = bc(rope[:, tt, 0, :], [P, 16, 8], 1), bc(rope[:, tt, 1, :], [P, 16, 8], 1)
                        z = slice(16 * tt, 16 * tt + 16)
                        TTo(r4[0][:, z, :], t1, cs, ALU.mult)
                        TTo(r4[1][:, z, :], t2, sn, ALU.mult)
                        TTo(r4[2][:, z, :], t2, cs, ALU.mult)
                        TTo(r4[3][:, z, :], t1, sn, ALU.mult)
                    ordered()
                    TTo(v[:, :, 0:8], r4[0], r4[1], ALU.subtract)
                    TTo(v[:, :, 8:16], r4[2], r4[3], ALU.add).then_inc(step("qk_normed"), 1)

                def attn_max(qt):
                    W = (qt + 1) * P
                    dve.wait_ge(step("scores"), i * 2 + qt + 1)
                    if qt:
                        dve.wait_ge(step("w_turned"), i * 2 + 1)
                    pv = prob[:, 0:8 * W].rearrange("p (j k) -> p j k", j=8)
                    nb_banks = 8 * W // 512
                    TTo(pv, PS[:, 0:nb_banks, :].rearrange("p a (j k) -> p (a j) k", k=W), bc(amask[:, S - W:S], [P, 8, W], 1), ALU.add)
                    ordered()
                    V.tensor_reduce(mx, pv, AX.X, ALU.max)
                    ordered()
                    V.tensor_scalar(nb, mx, -0.125, None, ALU.mult).then_inc(step("max_ready"), 1)

                def attn_weights(qt):
                    W = (qt + 1) * P
                    dve.wait_ge(step("attn_exp"), i * 2 + qt + 1)
                    V.reciprocal(pr, ps_)
                    ordered()
                    odd = pr[:, 4:8]
                    V.tensor_scalar(odd, odd, lmv, None, ALU.mult)
                    ordered()
                    pv = prob[:, 0:8 * W].rearrange("p (j k) -> p j k", j=8)
                    TTo(pv, pv, bc(pr, [P, 8, W], 2), ALU.mult)
                    ordered()
                    pw = prob[:, 0:8 * W].rearrange("p (m h k) -> p m h k", h=H1, m=2)
                    TTo(pw[:, 0, :, :], pw[:, 0, :, :], pw[:, 1, :, :], ALU.subtract).then_inc(step("w_ready"), 1)

                def wT_copy(qt):
                    dve.wait_ge(step("w_turned"), i * 2 + qt + 1)
                    J = 4 * (qt + 1)
                    V.tensor_copy(wT[:, 0:J, :], pB.rearrange("p a (j t) -> p (a j) t", t=P)[:, 0:J, :]).then_inc(step("wT_ready"), 1)

                def o_take(qt):
                    dve.wait_ge(step("o_ready"), i * 2 + qt + 1)
                    V.tensor_copy(o32[:, qt, :], pA[:, 0, :]).then_inc(step("o_taken"), 1)

                def o_sums():
                    dve.wait_ge(step("o_sq"), i + 1)
                    V.tensor_reduce(os_, prob[:, 0:1024].rearrange("p (j d) -> p j d", d=P), AX.X, ALU.add).then_inc(step("o_sums"), 1)

                def o_norm():
                    dve.wait_ge(step("o_root"), i + 1)
                    V.reciprocal(orr, os_)
                    ordered()
                    V.tensor_scalar(orr, orr, row("li")[:, 1:2], None, ALU.mult)
                    ordered()
                    v = o32.rearrange("p a (h d) -> p (a h) d", d=P)
                    TTo(v, v, bc(orr, [P, 8, P], 2), ALU.mult)
                    ordered()
                    TTo(v, v, bc(row("sub"), [P, 8, P], 1), ALU.mult).then_inc(step("o_normed"), 1)

                def yc_low():
                    split_low("yc_hi", i + 1, slice(A_YC, A_YC + 4), pA.rearrange("p a (j t) -> p (a j) t", t=S), "yc_ready")

                early = dict(
                    QK0=lambda: chunk_open(0), QK1=lambda: seg(0, 0), QK3=lambda: (state_copy(0), y_take(0, 0), seg(0, 1)),
                    V1=lambda: (state_copy(1), y_take(0, 1)), Z0=lambda: chunk_open(1), Z1=lambda: seg(1, 0),
                    Z3=lambda: (y_take(1, 0), seg(1, 1)), GV1=lambda: y_take(1, 1), GU0=gm_norm, GU1=gm_out,
                    GA0=qk_norm, GA1=qk_rope, GA3=lambda: attn_max(0), GB1=lambda: wT_copy(0), GB2=lambda: o_take(0),
                    GB3=lambda: attn_max(1), GC0=lambda: attn_weights(1), GC2=lambda: wT_copy(1), GC3=lambda: o_take(1), BB0=yc_low)
                after = dict(
                    XBC2=lambda: (dt_abs(), dt_one()), XBC3=dt_finish, QK0=lam_sums,
                    QK1=lambda: dec_mul(0, 0), QK2=lam_value, QK3=lambda: dec_mul(0, 1), Z1=lambda: dec_mul(1, 0),
                    Z3=lambda: dec_mul(1, 1), GV1=yz, GU0=qk_sums,
                    GA0=lambda: (split_low("ya_hi", i + 1, slice(A_YA, A_YA + 4), uu, "ya_ready"), rstd_of("yb_root", i + 1, yrstd, "yb_rstd")),
                    GA1=yb_norm,
                    GA2=lambda: split_low("yb_hi", i + 1, slice(A_YB, A_YB + 8), xbc[:, 0:8, :], "yb_ready"),
                    GA3=lambda: attn_weights(0), GC3=o_sums, BA0=o_norm)

                def take(n, g):
                    kind, m = g["kind"], g["n"]
                    if g["taker"] != "dve" or not g["closes"]:
                        return
                    pair = bank(g).rearrange("p (k t) -> p k t", t=S)
                    if kind == "XBC":
                        dve.wait_ge(step("xbc_open"), i * 6 + m + 1)
                        conv_taps(1, i, g, "cw", 4, ((2, 1), (1, 2), (0, 3)), (2 * m, 2 * m + 1),
                                  (xbc[:, 2 * m, :], xbc[:, 2 * m + 1, :])).then_inc(step("xbc_conv"), 1)
                        ordered()
                        dve.drain().then_inc(taken["dve"], 1)
                    elif kind == "BA":
                        arrived(1, i, n)
                        v = G0[:, 2 * m:2 * m + 2, :]
                        TTo(v, pair, v, ALU.mult).then_inc(taken["dve"], 1)
                    elif kind in ("BB", "BC"):
                        arrived(1, i, n)
                        v = (ug[:, 2 * m:2 * m + 2, :] if kind == "BB" else SZ[:, 2 * m:2 * m + 2, :])
                        TTo(v, pair, v, ALU.mult).then_inc(taken["dve"], 1)
                        ordered()
                        o = G0[:, 2 * m:2 * m + 2, :]
                        last = TTo(o, o, v, ALU.add)
                        if g["name"] in MERGED:
                            last.then_inc(step("mg32_ready"), 1)
                            merged_low(1, i, m, G0)
                    elif kind in ("OUT", "DN"):
                        residual(1, i, n, g)
                    elif kind == "UP":
                        up_take(1, i, n, g)

                def residual(b, i, n, g):
                    arrived(b, i, n)
                    m = g["n"] if g["kind"] == "OUT" else g["n"] // 4
                    pair = bank(g).rearrange("p (k t) -> p k t", t=S)
                    v = x[:, 2 * m:2 * m + 2, :]
                    TTo(v, pair, v, ALU.add).then_inc(taken["dve"], 1)
                    dve.drain().then_inc(step("x_pair"), 1)
                    if g["name"] == "DN3":
                        dve.wait_ge(step("cols_in"), layer(b, i) * 16 + 32)
                    xg_scaled(b, i, 1 if g["kind"] == "OUT" else 2, m)
                    if m == PAIRS - 1:
                        xg_low(b, i, 1 if g["kind"] == "OUT" else 2, m)

                def residual_low(b, i, g):
                    if g["name"] in ("OUT0", "OUT1", "OUT2"):
                        xg_low(b, i, 1, g["n"])
                    elif g["name"] in ("DN3", "DN7", "DN11"):
                        xg_low(b, i, 2, g["n"] // 4)

                def up_take(b, i, n, g):
                    m, val = g["n"] // 2, g["n"] % 2
                    buf = ypair(m % 2, val)
                    t0 = 2 * m + val * FT
                    if b == 1:
                        dve.wait_ge(step("up_open1"), i * (2 * FP) + g["n"] + 1)
                        last = conv_taps(1, i, g, "fw", 3, ((1, 1), (0, 2)), (t0, t0 + 1), (buf[:, 0, :], buf[:, 1, :]))
                        last.then_inc(taken["dve"], 1)
                        if not val:
                            dve.drain().then_inc(step("up_conv"), 1)
                    elif not val:
                        dve.wait_ge(step("up_open2"), i * FP + m + 1)
                        last = conv_taps(2, i, g, "fw", 3, ((0, 1), (2, -1)), (t0, t0 + 1), (buf[:, 0, :], buf[:, 1, :]))
                        last.then_inc(taken["dve"], 1)
                        dve.drain().then_inc(step("up_conv"), 1)

                def gate_up(b, i, n, g):
                    m = g["n"] // 2
                    v = ypair(m % 2, 0)
                    if b == 1:
                        ordered()
                    dve.wait_ge(step("up_act"), layer(b, i) * FP + m + 1)
                    if b == 1:
                        TTo(v, v, ypair(m % 2, 1), ALU.mult).then_inc(step("gated32"), 1)
                    else:
                        arrived(2, i, n)
                        TTo(v, bank(g).rearrange("p (k t) -> p k t", t=S), v, ALU.mult).then_inc(taken["dve"], 1)
                        dve.drain().then_inc(step("gated32"), 1)

                def gated_low(b, i, m):
                    dve.wait_ge(step("gated_hi"), layer(b, i) * FP + m + 1)
                    t = slice(A_G + 2 * m, A_G + 2 * m + 2)
                    TTo(alo[:, t, :], ypair(m % 2, 0), ahi[:, t, :].bitcast(f32), ALU.subtract).then_inc(step("up_free"), 1)
                    if m == FP - 1:
                        params_used()

                def up_stream(b, i, n, g, G):
                    if g["n"] % 2 == 1:
                        gate_up(b, i, n, g)
                    elif g["n"] >= 2:
                        gated_low(b, i, g["n"] // 2 - 1)
                    if g["n"] == 2 * FP - 1:
                        gated_low(b, i, FP - 1)

                for n, g in enumerate(G1):
                    if g["name"] == "UP0":
                        norm(1, i, 1, A_H2)
                    if g["name"] in FIRST:
                        if g["kind"] != "PU":
                            scale_bank(1, i, n, g)
                            scale_bank(1, i, n + 1, G1[n + 1])
                        split_behind(1, i, n, G1)
                    take(n, g)
                    if g["name"] in early:
                        ordered()
                        early[g["name"]]()
                    if g["name"] not in FIRST:
                        split_behind(1, i, n, G1)
                    residual_low(1, i, g)
                    if g["name"] in after:
                        ordered()
                        after[g["name"]]()
                    if g["kind"] == "UP":
                        up_stream(1, i, n, g, G1)

            with dve.Fori(0, LAYERS) as i:
                dve.wait_ge(step("par_in2"), i * 32 + 32)
                split_behind(2, i, -1, G2)
                norm(2, i, 0, A_H)

                def b2_max(u):
                    dve.wait_ge(step("b2_scores"), i * 8 + u + 1)
                    dve.wait_ge(step("b2_bias_in"), i * 384 + 48 * (u + 1))
                    px = PS[:, 2 * (u % 2):2 * (u % 2) + 2, :].rearrange("p a c -> p (a c)")[:, 0:768]
                    if u:
                        dve.wait_ge(step("b2_turned"), i * 8 + u)
                    STT(b2_P, px, float(P) ** -0.5, b2_bias.rearrange("p g k -> p (g k)"), ALU.mult, ALU.add).then_inc(step("b2_bias_free"), 1)
                    ordered()
                    V.tensor_reduce(bmx[:, 0:1], b2_P, AX.X, ALU.max)
                    ordered()
                    V.tensor_scalar(bnm[:, 0:1], bmx[:, 0:1], -1.0, None, ALU.mult).then_inc(step("b2_max"), 1)

                def b2_norm(u):
                    dve.wait_ge(step("b2_exp"), i * 8 + u + 1)
                    V.reciprocal(brr[:, 0:1], bsm[:, 0:1])
                    ordered()
                    V.tensor_scalar(b2_P, b2_P, brr[:, 0:1], None, ALU.mult).then_inc(step("b2_P_ready"), 1)

                def at_low(j):
                    dve.wait_ge(step("at_hi"), i * 4 + j + 1)
                    last = TTo(alo[:, A_AT + j, :], pC[:, 0:S], ahi[:, A_AT + j, :].bitcast(f32), ALU.subtract)
                    last.then_inc(step("at_lo"), 1)
                    if j == 3:
                        dve.drain().then_inc(step("at_ready"), 1)

                def take2(n, g):
                    kind, m = g["kind"], g["n"]
                    if g["taker"] != "dve" or not g["closes"]:
                        return
                    pair = bank(g).rearrange("p (k t) -> p k t", t=S)
                    if kind == "WP":
                        dve.wait_ge(step("po_hi"), i * 4 + m + 1)
                        for t in range(2):
                            k = A_PO + 2 * m + t
                            last = STT(alo[:, k, :], pair[:, t, :], col(2, "ps", 2 * m + t), ahi[:, k, :].bitcast(f32), ALU.mult, ALU.subtract)
                        last.then_inc(taken["dve"], 1)
                        if m == 3:
                            dve.drain().then_inc(step("po_ready"), 1)
                    elif kind in ("WA", "WB"):
                        arrived(2, i, n)
                        o, gate = ug[:, 2 * m:2 * m + 2, :], gate_t(m)
                        v = o if kind == "WA" else gate
                        TTo(v, pair, v, ALU.mult).then_inc(taken["dve"], 1)
                        if g["name"] in MERGED:
                            ordered()
                            TTo(o, o, gate, ALU.add).then_inc(step("mg32_ready"), 1)
                            merged_low(2, i, m, ug)
                    elif kind in ("OUT", "DN"):
                        residual(2, i, n, g)
                    elif kind == "UP":
                        up_take(2, i, n, g)

                for n, g in enumerate(G2):
                    if g["name"] == "UP0":
                        norm(2, i, 1, A_H2)
                    if g["name"] in FIRST:
                        if g["kind"] != "PU":
                            scale_bank(2, i, n, g)
                            scale_bank(2, i, n + 1, G2[n + 1])
                        split_behind(2, i, n, G2)
                    take2(n, g)
                    if g["name"] in PV_AT:
                        at_low(PV_AT[g["name"]])
                    if g["name"] in SC_AT:
                        b2_max(SC_AT[g["name"]])
                    if g["name"] not in FIRST:
                        split_behind(2, i, n, G2)
                    residual_low(2, i, g)
                    if g["name"] in SC_AT:
                        b2_norm(SC_AT[g["name"]])
                    if g["name"] == "Q0":
                        split_low("pd_hi", i + 1, slice(A_PD, A_PD + 8), PS[:, 0:4, :].rearrange("p a (k t) -> p (a k) t", t=S), "pd_ready")
                    if g["kind"] == "UP":
                        up_stream(2, i, n, g, G2)

            norm_rstd(4 * LAYERS + 1)
            for p in range(PAIRS):
                normed(p, "f_normed")
            dve.wait_ge(step("out_turned"), 1)
            V.tensor_copy(g01[:, 0:4, :].rearrange("p k t -> p (k t)"), pA.rearrange("p a c -> p (a c)")).then_inc(step("out_ready_0"), 1)


def kernel(**inputs):
    import numpy as np
    import concourse.bacc as bacc
    from concourse import mybir
    from concourse.bass_utils import run_bass_kernel_spmd as run

    f32 = mybir.dt.float32
    a = {k: np.ascontiguousarray(v) for k, v in inputs.items()}
    L, S, P = 2, 256, 128

    def by_feature(v):
        v = v.reshape(L, -1, P, *v.shape[2:])
        return np.moveaxis(v, 2, 1).reshape(L, P, -1)

    cols_1 = np.concatenate([by_feature(a["attn_norm_g"]), by_feature(a["ssm_conv_w"]), by_feature(a["ssm_conv_b"]),
                             by_feature(a["ssm_norm_g"]), by_feature(np.repeat(a["ssm_d"], 64, axis=1)),
                             by_feature(a["ffn_norm_g"]), by_feature(a["ffn_conv_w"]), by_feature(a["ffn_conv_b"])], axis=2)
    cols_2 = np.concatenate([by_feature(a["norm1_2"]), by_feature(a["pool_scale_2"]), by_feature(a["norm2_2"]),
                             by_feature(np.moveaxis(a["conv_w_2"], 1, 2)), by_feature(a["conv_b_2"])], axis=2)
    cols = np.zeros((2 * L + 1, P, cols_1.shape[2]), np.float32)
    cols[:L] = cols_1
    cols[L:2 * L, :, :cols_2.shape[2]] = cols_2
    cols[2 * L, :, :8] = a["norm_f_2"].reshape(8, P).T
    li = np.array([[0.8 - 0.6 * np.exp(-0.3 * n)] for n in range(L)])
    li = np.concatenate([li, 1.0 - li], axis=1).astype(np.float32)
    rows_1 = np.concatenate([a["gm_v_norm_g"], a["gm_b_s"].reshape(L, -1), a["da_q_norm_g"], a["da_k_norm_g"], a["da_subln_g"],
                             a["ssm_dt_bias"], a["ssm_a_log"], li], axis=1)
    p = np.arange(P)
    ident = np.eye(P, dtype=np.float32)
    tri = (p[:, None] <= p[None, :]).astype(np.float32)
    amask = np.concatenate([np.zeros((P, P)), np.where(p[None, :] <= p[:, None], 0.0, -1e30)], axis=1).astype(np.float32)
    inv = (1.0 / (np.float32(500000.0) ** (np.arange(0, 16, 2, dtype=np.float32) / np.float32(16)))).astype(np.float32)
    ang = (np.arange(S, dtype=np.float32)[:, None] * inv[None, :]).astype(np.float32).astype(np.float64)
    rope = np.stack([np.cos(ang), np.sin(ang)], axis=1).astype(np.float32).reshape(2, P, 2, 8)
    rope = np.ascontiguousarray(np.moveaxis(rope, 0, 1)).reshape(P, 32)
    off = np.arange(511) - 255
    n = -off
    mag = np.abs(n)
    large = np.minimum(8 + (np.log(np.maximum(mag, 1) / 8) / np.log(1024 / 8) * 8).astype(np.int32), 15)
    bucket = (n < 0) * 16 + np.where(mag < 8, mag, large)
    onehot = np.zeros((32, 512), np.float32)
    onehot[bucket, np.arange(511)] = 1.0
    offmask = np.full((12, 512), -1e30, np.float32)
    for g, (window, dilation) in enumerate(((128, 1), (512, 4), (2048, 16))):
        ok = (off % dilation == 0) & (mag <= window // (2 * dilation) * dilation)
        offmask[4 * g:4 * g + 4, :511] = np.where(ok, 0.0, -1e30)
    band = np.zeros((S, 4, S), np.float64)
    for g, w in enumerate((2, 4, 8, 16)):
        for t in range(S):
            lo, hi = max(t - w // 2, 0), min(t - w // 2 + w, S)
            band[lo:hi, g, t] = 1.0 / (hi - lo)
            band[t, g, t] -= 1.0
    band = band.astype(np.float32).reshape(2, P, 4 * S)

    feeds = {k: a[k] for k in ("x", "w_in", "gm_w_s", "w_branch_a", "w_branch_b", "w_branch_c", "w_out", "ffn_w_up", "ffn_w_down",
                               "w_in_2", "w_pool_2", "w_a_2", "w_b_2", "w_o_2", "w_up_2", "w_down_2", "rel_bias_2")}
    feeds.update(cols=cols, rows_1=rows_1, lam_1=a["da_lambda"].reshape(L, -1), c_ident=ident, c_tri=tri, c_amask=amask, c_rope=rope,
                 c_onehot=onehot, c_offmask=offmask, c_band=band)
    nc = bacc.Bacc("TRN2", target_bir_lowering=False, num_devices=1)
    arrays, t_in = {}, {}
    for name, v in feeds.items():
        arrays[f"in_{name}"] = np.ascontiguousarray(v)
        t_in[name] = nc.dram_tensor(f"in_{name}", v.shape, f32, kind="ExternalInput").ap()
    t_in["bias_table"] = nc.dram_tensor("bias_table", (12, 129 * 511), f32, kind="Internal").ap()
    out = nc.dram_tensor("out", (1, S, 1024), f32, kind="ExternalOutput").ap()
    build_program(nc, t_in, out)
    r = run(nc, [arrays], core_ids=[0])
    return r.results[0]["out"]
```
